# Optimizing a Trainium2 kernel written in Bass

```python
import jax, jax.numpy as jnp
from jax import lax
import numpy as np

D_MODEL = 1024
BATCH = 1
SEQ = 512
DEPTH = 2

CHUNK = 64
REC_CHUNK = 16
Q_BLOCK = 128
N_MEM = 256
EPS = 1e-6
MASK_VALUE = -1e30
LB_FLOOR = 1e-30

MLA_HEADS = 4
MLA_Q_LORA = 256
MLA_KV_LORA = 256
MLA_NOPE = 128
MLA_ROPE = 64
MLA_V = 128
MLA_QK = MLA_NOPE + MLA_ROPE
ROPE_THETA = 10000.0

GLA_HEADS = 4
GLA_DK = 32
GLA_DV = 64
GLA_GATE_RANK = 16
GLA_TAU = 16.0

HGRN_HEADS = 4
HGRN_DK = 64
HGRN_DV = 64

D_MIX = MLA_HEADS * MLA_V + GLA_HEADS * GLA_DV + HGRN_HEADS * HGRN_DV

IN_SIZES = (
    MLA_Q_LORA, MLA_KV_LORA, MLA_ROPE,
    GLA_HEADS * GLA_DK, GLA_HEADS * GLA_DK, GLA_HEADS * GLA_DV,
    GLA_GATE_RANK, GLA_HEADS * GLA_DV,
    HGRN_HEADS * HGRN_DK, HGRN_HEADS * HGRN_DK,
    HGRN_HEADS * HGRN_DV, HGRN_HEADS * HGRN_DV,
)
P_IN = sum(IN_SIZES)

CA_HEADS = 4
CA_HEAD_DIM = 128

D_FF = 2816
CONV_WIDTH = 3

kernel_name = 'hybrid_mla_gla_hgrn2_memory_convglu'

def rms_norm(x, gain):
    xf = x.astype(jnp.float32)
    y = xf * lax.rsqrt(jnp.mean(xf * xf, axis=-1, keepdims=True) + EPS)
    return y.astype(x.dtype) * gain

def rotary(x, cos, sin):
    x1, x2 = jnp.split(x, 2, axis=-1)
    return jnp.concatenate([x1 * cos - x2 * sin, x2 * cos + x1 * sin], axis=-1)

def chunked_gated_recurrence(q, k, v, log_decay):
    B, S, H, DK = q.shape
    DV = v.shape[-1]
    n = S // REC_CHUNK

    def to_chunks(t):
        return t.astype(jnp.float32).reshape(B, n, REC_CHUNK, H, t.shape[-1]).transpose(0, 3, 1, 2, 4)

    qc, kc, vc, gc = to_chunks(q), to_chunks(k), to_chunks(v), to_chunks(log_decay)
    b = jnp.cumsum(gc, axis=3)
    b_last = b[:, :, :, -1:, :]
    causal = jnp.tril(jnp.ones((REC_CHUNK, REC_CHUNK), dtype=jnp.float32))
    rel = b[:, :, :, :, None, :] - b[:, :, :, None, :, :]
    pair_decay = jnp.exp(jnp.minimum(rel, 0.0)) * causal[:, :, None]
    scores = jnp.einsum('bhnid,bhnjd,bhnijd->bhnij', qc, kc, pair_decay)
    o_intra = jnp.einsum('bhnij,bhnjv->bhniv', scores, vc)

    updates = jnp.einsum('bhnjd,bhnjv->bhndv', kc * jnp.exp(b_last - b), vc)
    decays = jnp.exp(b_last[:, :, :, 0, :])

    def step(state, inp):
        decay, upd = inp
        return decay[..., None] * state + upd, state

    init = jnp.zeros((B, H, DK, DV), jnp.float32)
    _, starts = lax.scan(step, init, (jnp.moveaxis(decays, 2, 0), jnp.moveaxis(updates, 2, 0)))
    starts = jnp.moveaxis(starts, 0, 2)
    o_inter = jnp.einsum('bhnid,bhndv->bhniv', qc * jnp.exp(b), starts)
    o = (o_intra + o_inter).transpose(0, 2, 3, 1, 4).reshape(B, S, H, DV)
    return o.astype(v.dtype)

def mla_mixer(q_lat, kv_lat, k_rope, cos, sin, q_lat_norm, w_q_up, kv_lat_norm, w_kv_up, q_norm, k_norm):
    B, S, _ = q_lat.shape
    H = MLA_HEADS
    q = (rms_norm(q_lat, q_lat_norm) @ w_q_up).reshape(B, S, H, MLA_QK)
    kv = (rms_norm(kv_lat, kv_lat_norm) @ w_kv_up).reshape(B, S, H, MLA_NOPE + MLA_V)
    k_nope, v = kv[..., :MLA_NOPE], kv[..., MLA_NOPE:]
    k = jnp.concatenate([k_nope, jnp.broadcast_to(k_rope[:, :, None, :], (B, S, H, MLA_ROPE))], axis=-1)
    q = rms_norm(q, q_norm)
    k = rms_norm(k, k_norm)
    q = jnp.concatenate([q[..., :MLA_NOPE], rotary(q[..., MLA_NOPE:], cos, sin)], axis=-1)
    k = jnp.concatenate([k[..., :MLA_NOPE], rotary(k[..., MLA_NOPE:], cos, sin)], axis=-1)

    n_blocks = S // Q_BLOCK
    q_blocks = jnp.moveaxis(q.reshape(B, n_blocks, Q_BLOCK, H, MLA_QK), 1, 0)
    key_chunk = jnp.arange(S) // CHUNK
    scale = MLA_QK ** -0.5

    def attend(args):
        qb, blk = args
        s = jnp.einsum('bqhd,bkhd->bhqk', qb, k).astype(jnp.float32) * scale
        q_chunk = (blk * Q_BLOCK + jnp.arange(Q_BLOCK)) // CHUNK
        s = jnp.where(key_chunk[None, :] <= q_chunk[:, None], s, MASK_VALUE)
        p = jax.nn.softmax(s, axis=-1).astype(v.dtype)
        return jnp.einsum('bhqk,bkhd->bqhd', p, v)

    out = lax.map(attend, (q_blocks, jnp.arange(n_blocks)))
    return jnp.moveaxis(out, 0, 1).reshape(B, S, H * MLA_V)

def gla_mixer(q, k, v, gate_lr, r, w_gate, b_gate, out_norm):
    B, S, _ = q.shape
    H = GLA_HEADS
    log_alpha = jax.nn.log_sigmoid((gate_lr @ w_gate + b_gate).astype(jnp.float32)) / GLA_TAU
    o = chunked_gated_recurrence(
        q.reshape(B, S, H, GLA_DK) * (GLA_DK ** -0.5),
        k.reshape(B, S, H, GLA_DK),
        v.reshape(B, S, H, GLA_DV),
        log_alpha.reshape(B, S, H, GLA_DK))
    o = rms_norm(o, out_norm) * jax.nn.silu(r.reshape(B, S, H, GLA_DV))
    return o.reshape(B, S, H * GLA_DV)

def hgrn2_mixer(q, f_logit, i, g, lower_bound, out_norm):
    B, S, _ = q.shape
    H = HGRN_HEADS
    z = f_logit.astype(jnp.float32)
    log_f = jnp.logaddexp(jnp.log(jnp.maximum(lower_bound, LB_FLOOR)),
                          jnp.log1p(-lower_bound) + jax.nn.log_sigmoid(z))
    log_f = jnp.minimum(log_f, 0.0)
    one_minus_f = (1.0 - lower_bound) * jax.nn.sigmoid(-z)
    o = chunked_gated_recurrence(
        jax.nn.silu(q).reshape(B, S, H, HGRN_DK) * (HGRN_DK ** -0.5),
        one_minus_f.reshape(B, S, H, HGRN_DK),
        i.reshape(B, S, H, HGRN_DV),
        log_f.reshape(B, S, H, HGRN_DK))
    o = rms_norm(o, out_norm) * jax.nn.silu(g.reshape(B, S, H, HGRN_DV))
    return o.reshape(B, S, H * HGRN_DV)

def memory_cross_attention(h_norm, mem_norm, w_q, w_kv, q_norm, k_norm, w_out):
    B, S, _ = h_norm.shape
    M = mem_norm.shape[1]
    q = (h_norm @ w_q).reshape(B, S, CA_HEADS, CA_HEAD_DIM)
    kv = (mem_norm @ w_kv).reshape(B, M, CA_HEADS, 2 * CA_HEAD_DIM)
    k, v = kv[..., :CA_HEAD_DIM], kv[..., CA_HEAD_DIM:]
    q = rms_norm(q, q_norm)
    k = rms_norm(k, k_norm)
    s = jnp.einsum('bshd,bmhd->bhsm', q, k).astype(jnp.float32) * (CA_HEAD_DIM ** -0.5)
    p = jax.nn.softmax(s, axis=-1).astype(v.dtype)
    o = jnp.einsum('bhsm,bmhd->bshd', p, v).reshape(B, S, CA_HEADS * CA_HEAD_DIM)
    return o @ w_out

def conv_glu_ffn(h_norm, w_in, conv_w, conv_b, w_out):
    gate, up = jnp.split(h_norm @ w_in, 2, axis=-1)
    S = gate.shape[1]
    padded = jnp.pad(gate, ((0, 0), (CONV_WIDTH - 1, 0), (0, 0)))
    conv = conv_b
    for t in range(CONV_WIDTH):
        conv = conv + padded[:, t:t + S, :] * conv_w[t]
    return (jax.nn.silu(conv) * up) @ w_out

def setup_inputs(seed: int = 0) -> dict:
    key = jax.random.key(seed)
    ks = iter(jax.random.split(key, 40))
    f32 = jnp.float32
    out_scale = (2 * DEPTH) ** -0.5

    def dense(shape, fan_in, scale=1.0):
        return jax.random.normal(next(ks), shape, f32) * (scale * fan_in ** -0.5)

    def gain(shape):
        return 1.0 + 0.02 * jax.random.normal(next(ks), shape, f32)

    def small(shape):
        return 0.01 * jax.random.normal(next(ks), shape, f32)

    L = DEPTH
    x = jax.random.normal(next(ks), (BATCH, SEQ, D_MODEL), f32)
    mem = jax.random.normal(next(ks), (BATCH, N_MEM, D_MODEL), f32)
    start = jax.random.randint(next(ks), (BATCH, 1), 0, 4096, dtype=jnp.int32)
    positions = (start + jnp.arange(SEQ, dtype=jnp.int32)[None, :]).astype(jnp.int32)
    return {
        'x': x,
        'mem': mem,
        'positions': positions,
        'norm_mix': gain((L, D_MODEL)),
        'w_in': dense((L, D_MODEL, P_IN), D_MODEL),
        'mla_q_lat_norm': gain((L, MLA_Q_LORA)),
        'w_q_up': dense((L, MLA_Q_LORA, MLA_HEADS * MLA_QK), MLA_Q_LORA),
        'mla_kv_lat_norm': gain((L, MLA_KV_LORA)),
        'w_kv_up': dense((L, MLA_KV_LORA, MLA_HEADS * (MLA_NOPE + MLA_V)), MLA_KV_LORA),
        'mla_q_norm': gain((L, MLA_QK)),
        'mla_k_norm': gain((L, MLA_QK)),
        'gla_w_gate': dense((L, GLA_GATE_RANK, GLA_HEADS * GLA_DK), GLA_GATE_RANK),
        'gla_b_gate': small((L, GLA_HEADS * GLA_DK)),
        'gla_out_norm': gain((L, GLA_DV)),
        'hgrn_lb_logits': 0.1 * jax.random.normal(next(ks), (L, HGRN_HEADS * HGRN_DK), f32),
        'hgrn_out_norm': gain((L, HGRN_DV)),
        'w_mix_out': dense((L, D_MIX, D_MODEL), D_MIX, out_scale),
        'norm_ca': gain((L, D_MODEL)),
        'norm_mem': gain((L, D_MODEL)),
        'w_ca_q': dense((L, D_MODEL, CA_HEADS * CA_HEAD_DIM), D_MODEL),
        'w_ca_kv': dense((L, D_MODEL, 2 * CA_HEADS * CA_HEAD_DIM), D_MODEL),
        'ca_q_norm': gain((L, CA_HEAD_DIM)),
        'ca_k_norm': gain((L, CA_HEAD_DIM)),
        'w_ca_out': dense((L, CA_HEADS * CA_HEAD_DIM, D_MODEL), CA_HEADS * CA_HEAD_DIM, out_scale),
        'norm_ffn': gain((L, D_MODEL)),
        'w_ffn_in': dense((L, D_MODEL, 2 * D_FF), D_MODEL),
        'ffn_conv_w': dense((L, CONV_WIDTH, D_FF), CONV_WIDTH),
        'ffn_conv_b': small((L, D_FF)),
        'w_ffn_out': dense((L, D_FF, D_MODEL), D_FF, out_scale),
    }

def reference(x, mem, positions, norm_mix, w_in, mla_q_lat_norm, w_q_up, mla_kv_lat_norm, w_kv_up,
              mla_q_norm, mla_k_norm, gla_w_gate, gla_b_gate, gla_out_norm, hgrn_lb_logits, hgrn_out_norm,
              w_mix_out, norm_ca, norm_mem, w_ca_q, w_ca_kv, ca_q_norm, ca_k_norm, w_ca_out,
              norm_ffn, w_ffn_in, ffn_conv_w, ffn_conv_b, w_ffn_out):
    gamma = jax.nn.softmax(hgrn_lb_logits.astype(jnp.float32), axis=0)
    lower_bounds = jnp.cumsum(gamma, axis=0) - gamma[0]

    inv_freq = ROPE_THETA ** (-jnp.arange(0, MLA_ROPE, 2, dtype=jnp.float32) / MLA_ROPE)
    ang = positions.astype(jnp.float32)[..., None] * inv_freq
    cos = jnp.cos(ang)[:, :, None, :].astype(x.dtype)
    sin = jnp.sin(ang)[:, :, None, :].astype(x.dtype)

    split_points = np.cumsum(IN_SIZES)[:-1].tolist()
    h = x
    for l in range(DEPTH):
        n = rms_norm(h, norm_mix[l])
        (a_q_lat, a_kv_lat, a_k_rope, b_q, b_k, b_v, b_gate_lr, b_r,
         c_q, c_f, c_i, c_g) = jnp.split(n @ w_in[l], split_points, axis=-1)
        y_a = mla_mixer(a_q_lat, a_kv_lat, a_k_rope, cos, sin, mla_q_lat_norm[l], w_q_up[l],
                        mla_kv_lat_norm[l], w_kv_up[l], mla_q_norm[l], mla_k_norm[l])
        y_b = gla_mixer(b_q, b_k, b_v, b_gate_lr, b_r, gla_w_gate[l], gla_b_gate[l], gla_out_norm[l])
        y_c = hgrn2_mixer(c_q, c_f, c_i, c_g, lower_bounds[l], hgrn_out_norm[l])
        h = h + jnp.concatenate([y_a, y_b, y_c], axis=-1) @ w_mix_out[l]
        h = h + memory_cross_attention(rms_norm(h, norm_ca[l]), rms_norm(mem, norm_mem[l]),
                                       w_ca_q[l], w_ca_kv[l], ca_q_norm[l], ca_k_norm[l], w_ca_out[l])
        h = h + conv_glu_ffn(rms_norm(h, norm_ffn[l]), w_ffn_in[l], ffn_conv_w[l], ffn_conv_b[l], w_ffn_out[l])
    return h


_drawn_inputs = setup_inputs


def setup_inputs(seed=0):
    import zlib

    import numpy as np

    out = dict(_drawn_inputs(seed))
    spreads = {}
    factors = {'norm_mix': 5.178,
     'mla_q_lat_norm': 8.0,
     'mla_kv_lat_norm': 8.0,
     'mla_q_norm': 8.0,
     'mla_k_norm': 8.0,
     'gla_b_gate': 8.0,
     'gla_out_norm': 8.0,
     'hgrn_lb_logits': 8.0,
     'hgrn_out_norm': 8.0,
     'norm_ca': 8.0,
     'norm_mem': 8.0,
     'ca_q_norm': 8.0,
     'ca_k_norm': 8.0,
     'norm_ffn': 4.8,
     'ffn_conv_b': 8.0}
    for name, (base, spread) in spreads.items():
        noise = np.random.default_rng([zlib.crc32(name.encode()), seed]).standard_normal(out[name].shape)
        drawn = base * np.exp(spread * noise) if base else spread * noise
        out[name] = __import__('jax').numpy.asarray(drawn.astype(out[name].dtype))
    for name, factor in factors.items():
        out[name] = (out[name] * factor).astype(out[name].dtype)
    return out
```

```python
def build_trunk(nc, A, out):
    import concourse.bass as bass
    from concourse import mybir
    from contextlib import ExitStack
    import math
    import numpy as np

    f32, f32r, bf16 = mybir.dt.float32, mybir.dt.float32r, mybir.dt.bfloat16
    i32, u8 = mybir.dt.int32, mybir.dt.uint8
    ACT, ALU, AX = mybir.ActivationFunctionType, mybir.AluOpType, mybir.AxisListType

    P = 128
    DEPTH, D, P_IN = A["w_in"].shape
    SEQ = A["x"].shape[1]
    NM = A["mem"].shape[1]
    NT, KD, MT = SEQ // P, D // P, NM // P
    QL, KVL = A["w_q_up"].shape[1], A["w_kv_up"].shape[1]
    NH = 4
    NOPE = VD = P
    QK = A["w_q_up"].shape[2] // NH
    ROPE = QK - NOPE
    GDK, GDV = A["gla_w_gate"].shape[2] // NH, A["gla_out_norm"].shape[1]
    RANK = A["gla_w_gate"].shape[1]
    HDK, HDV = A["hgrn_lb_logits"].shape[1] // NH, A["hgrn_out_norm"].shape[1]
    DFF = A["w_ffn_out"].shape[1]
    CONV = A["ffn_conv_w"].shape[1]
    FC = DFF // P
    FG = 2
    FCG = FC // FG
    EPS, MASKED, TAU, THETA, LB_FLOOR, BLOCK = 1e-6, -1e30, 16.0, 10000.0, 1e-30, 64
    C_QL, C_KVL = 0, QL
    C_ROPE = C_KVL + KVL
    C_BQ = C_ROPE + ROPE
    C_BK = C_BQ + NH * GDK
    C_BV = C_BK + NH * GDK
    C_LR = C_BV + NH * GDV
    C_BR = C_LR + RANK
    C_CQ = C_BR + NH * GDV
    C_CF = C_CQ + NH * HDK
    C_CI = C_CF + NH * HDK
    C_CG = C_CI + NH * HDV
    HALF = D // 2
    VG = NH * GDV + RANK

    rows_of, at = {}, 0
    for name, n in (("norm_mix", KD), ("mla_q_lat_norm", QL // P), ("mla_kv_lat_norm", KVL // P),
                    ("gla_b_gate", 1), ("norm_ca", KD), ("norm_mem", KD), ("norm_ffn", KD),
                    ("ffn_conv_w", CONV * FC), ("ffn_conv_b", FC)):
        rows_of[name] = (at, n)
        at += n
    ROWS = at
    spread_of, at = {}, 0
    for name, n in (("mla_q_norm", QK), ("mla_k_norm", QK), ("gla_out_norm", GDV), ("hgrn_out_norm", HDV),
                    ("ca_q_norm", P), ("ca_k_norm", P)):
        spread_of[name] = (at, n)
        at += n
    SPREAD = at

    slabs, slab_at = [], {}

    def slab(name, nk, cols, src):
        slab_at[name] = len(slabs)
        slabs.append((nk, cols, src))

    def cut(w, k0, nk, c0, cols):
        def parts(l, dst):
            yield (dst[:, 0:nk * cols].rearrange("p (k c) -> p k c", k=nk),
                   w[l, k0 * P:(k0 + nk) * P, c0:c0 + cols].rearrange("(k p) c -> p k c", p=P))
        return parts

    for n in range(4):
        slab(("lat", n), KD, P, cut(A["w_in"], 0, KD, n * P, P))
    slab("rope", KD, ROPE, cut(A["w_in"], 0, KD, C_ROPE, ROPE))
    PAIR = 2 * QK

    def q_up_parts(n):
        def parts(l, dst):
            for k in range(2):
                src = A["w_q_up"][l, k * P:(k + 1) * P, n * PAIR:(n + 1) * PAIR].rearrange("p (h x) -> p h x", h=2)
                for x0, x1 in ((0, NOPE), (NOPE, QK)):
                    d = dst[:, k * PAIR + 2 * x0:k * PAIR + 2 * x1].rearrange("p (h x) -> p h x", h=2)
                    yield d, src[:, :, x0:x1]
        return parts

    def kv_up_parts(n):
        def parts(l, dst):
            for k in range(2):
                src = A["w_kv_up"][l, k * P:(k + 1) * P].rearrange("p (h x) -> p h x", h=NH)
                yield (dst[:, k * NH * P:(k + 1) * NH * P].rearrange("p (h x) -> p h x", h=NH),
                       src[:, :, n * P:(n + 1) * P])
        return parts

    for n in range(2):
        slab(("q_up", n), 2, PAIR, q_up_parts(n))
    for n in range(2):
        slab(("kv_up", n), 2, NH * P, kv_up_parts(n))
    FEATS = [C_CF, C_CF + P, C_CQ, C_CQ + P, C_BQ, C_BK]
    for n, c in enumerate(FEATS):
        slab(("feat", n), KD, P, cut(A["w_in"], 0, KD, c, P))
    TOKS = {"vg": (C_BV, VG, (3, 3, 2)), "br": (C_BR, NH * GDV, (4, 4)),
            "cig": (C_CI, NH * HDV * 2, (2, 2, 2, 2))}
    for name, (c, cols, ks) in TOKS.items():
        for n, nk in enumerate(ks):
            slab((name, n), nk, cols, cut(A["w_in"], sum(ks[:n]), nk, c, cols))

    def halves(name, w, nk_all, k0=0, out_cols=HALF):
        for half in range(2):
            for n in range((nk_all + 1) // 2):
                nk = min(2, nk_all - 2 * n)
                slab((name, half, n), nk, out_cols, cut(w, k0 + 2 * n, nk, half * out_cols, out_cols))

    halves("mix", A["w_mix_out"], KD)
    halves("ckv", A["w_ca_kv"], KD)
    for n in range(KD // 2):
        slab(("caq", n), 2, NH * P, cut(A["w_ca_q"], 2 * n, 2, 0, NH * P))
    halves("cao", A["w_ca_out"], NH)
    for g in range(FG):
        for c in range(FCG):
            slab(("gate", g, c), KD, P, cut(A["w_ffn_in"], 0, KD, (g * FCG + c) * P, P))
            slab(("up", g, c), KD, P, cut(A["w_ffn_in"], 0, KD, DFF + (g * FCG + c) * P, P))
        halves(("ffo", g), A["w_ffn_out"], FCG, k0=g * FCG)
    NS = len(slabs)
    RAW, SPLIT, SLAB = 3, 3, 1024

    with ExitStack() as ctx:
        def sb(name, shape, dt=f32):
            return ctx.enter_context(nc.sbuf_tensor(name, shape, dt))

        h = sb("h", [P, NT, D])
        raw = [sb(f"raw{i}", [P, SLAB]) for i in range(RAW)]
        w_hi = [sb(f"w_hi{i}", [P, SLAB], f32r) for i in range(SPLIT)]
        w_lo = [sb(f"w_lo{i}", [P, SLAB], f32r) for i in range(SPLIT)]
        ident = sb("ident", [P, P])
        ones = sb("ones", [P, P])
        pair_mask = {m: sb(f"pair_mask{m}", [P, P], u8) for m in (1, 2, 4, 8)}
        cos, sin = sb("cos", [P, NT, ROPE // 2]), sb("sin", [P, NT, ROPE // 2])
        eps_c = sb("eps_c", [P, 1])
        lb_all = sb("lb_all", [P, 2, DEPTH])
        lb_floor, lb_rest = sb("lb_floor", [P, 2]), sb("lb_rest", [P, 2])
        gains = sb("gains", [P, P])
        spread = sb("spread", [P, SPREAD])
        w_gate = sb("w_gate", [RANK, NH * GDK])
        r_bc = sb("r_bc", [P, SEQ])
        r_diag = sb("r_diag", [P, NT, P])
        kr_tok = sb("kr_tok", [P, NT, ROPE])
        small = sb("small", [P, 520])

        KB = 1024
        ARENA = 141 * KB + 256
        arena = sb("arena", [P, ARENA // 4])
        base = nc.sbuf_base - ARENA

        def place(name, kb, shape, dt=f32):
            size = 4 * int(np.prod(shape[1:]))
            assert int(kb * KB) + size <= ARENA, name
            return nc.alloc_sbuf_tensor_at(name, shape, dt, offset=base + int(kb * KB))

        x_hi = place("x_hi", 0, [P, KD, SEQ], f32r)
        x_lo = place("x_lo", 16, [P, KD, SEQ], f32r)
        y_hi, y_lo = x_hi, x_lo
        scores_g = place("scores_g", 8, [P, NH, NT, P])
        scores_h = place("scores_h", 24, [P, NH, NT, P])
        R0, R1, R2, R3, R4, R5, R6 = 32, 48, 72, 80, 104, 125, 141.25
        lat_hi = place("lat_hi", R0, [P, 4, SEQ], f32r)
        lat_lo = place("lat_lo", R0 + 8, [P, 4, SEQ], f32r)
        probsT = place("probsT", R0, [P, NT, SEQ])
        probs = [place(f"probs{i}", R0 + 8 + 2 * i, [P, SEQ]) for i in range(2)]
        lrT = place("lrT", R0 + 12, [RANK, SEQ])
        gate_tmp = place("gate_tmp", R0 + 14, [P, SEQ])
        lat = place("lat", R1, [P, 4, SEQ])
        lat_sq = place("lat_sq", R1 + 8, [P, 4, SEQ])
        qT_n, qT_r = place("qT_n", R1, [P, NH, SEQ]), place("qT_r", R1 + 8, [P, 2, SEQ])
        kT_n, kT_r = place("kT_n", R1 + 12, [P, NH, SEQ]), place("kT_r", R1 + 20, [P, 2, SEQ])
        v_tok = place("v_tok", R2, [P, NT, NH * VD])
        q_tok, k_tok = place("q_tok", R3, [P, NT, NH * QK]), place("k_tok", R3 + 12, [P, NT, NH * QK])
        o_tok = place("o_tok", R3, [P, NT, 512])
        k_hat = place("k_hat", R3 + 8, [P, 3, NT, P])
        state = place("state", R3 + 14, [P, NT - 1, 512])
        o_sq = place("o_sq", R3 + 20, [P, 512])
        Q, K = place("Q", R4, [P, 3, SEQ]), place("K", R4 + 6, [P, 3, SEQ])
        decay = place("decay", R4 + 12, [P, 3, SEQ])
        decay_m = place("decay_m", R4 + 18, [P, 3, SEQ // 2])
        vg_tok = place("vg_tok", R5, [P, NT, VG])
        ci_tok = place("ci_tok", R5 + 4.25, [P, NT, NH * HDV])
        sg_tok = place("sg_tok", R5 + 8.25, [P, NT, 512])
        mem_tok = place("mem_tok", R0, [P, MT, D])
        m_hi, m_lo = place("m_hi", R1, [P, KD, NM], f32r), place("m_lo", R1 + 8, [P, KD, NM], f32r)
        ckv_tok = place("ckv_tok", R2, [P, MT, D])
        ckv_sq = place("ckv_sq", R3, [P, MT, NH, P])
        ckT = place("ckT", R3 + 4, [P, NH, NM])
        cq_tok = place("cq_tok", R3 + 8, [P, NT, NH * P])
        cqT = place("cqT", R3 + 16, [P, NH, SEQ])
        cq_sq = place("cq_sq", R4, [P, NT, NH * P])
        cprobsT = place("cprobsT", R4 + 8, [P, MT, SEQ])
        cprobs = [place(f"cprobs{i}", R4 + 12 + i, [P, NM]) for i in range(2)]
        a_hi = place("a_hi", 32, [P, FCG, SEQ], f32r)
        a_lo = place("a_lo", 54, [P, FCG, SEQ], f32r)
        gate_in = [place(f"gate_in{i}", 76 + 2.25 * i, [P, CONV - 1 + SEQ]) for i in range(2)]
        conv = [place(f"conv{i}", 81 + 2 * i, [P, SEQ]) for i in range(2)]
        conv_silu = [place(f"conv_silu{i}", 85 + 2 * i, [P, SEQ]) for i in range(2)]
        up_s = [place(f"up_s{i}", 89 + 2 * i, [P, SEQ]) for i in range(2)]
        act = [place(f"act{i}", 93 + 2 * i, [P, SEQ]) for i in range(2)]
        rows = place("rows", R5, [P, P])
        junk = place("junk", R5 + 8.25, [P, D], bf16)
        junk_v = place("junk_v", R5 + 4.25, [P, NH, QK], bf16)
        lb_rows = place("lb_rows", 0, [DEPTH * 2, P])
        lb_t = place("lb_t", 1, [P, 8, 2, DEPTH])
        pos_i = place("pos_i", 2, [P, NT], i32)
        pos_f = place("pos_f", 3, [P, NT])
        ang = place("ang", 4, [P, NT, ROPE // 2])
        turns_i = place("turns_i", 5, [P, NT, ROPE // 2], i32)
        turns = place("turns", 6, [P, NT, ROPE // 2])
        over = place("over", 7, [P, NT, ROPE // 2])
        freq = place("freq", 8, [P, ROPE // 2])
        idx_i, idx_j = place("idx_i", 9, [P, P], i32), place("idx_j", 10, [P, P], i32)
        mk = [place(f"mk{i}", 11 + i, [P, P], i32) for i in range(3)]

        pb = [ctx.enter_context(nc.psum_tensor(f"bank{i}", [P, 512], f32)) for i in range(8)]

        names = """lo_split hi_split slab_used vectors_in spread_in mem_in rows_t gains_ready chain_v chain_a
            hT_mm x_hi_done x_lo_done ss_done r_done r_diag_done r_mm r_bc_done
            lat_mm lat_evac lat_sq_done lat_hi_done lat_lo_done lat_ss_mm r_lat_done
            rope_mm rope_evac q_mm q_evac k_mm k_evac v_mm v_evac qk_ss qk_r qk_done qkT_mm qkT_evac
            feat_mm feat_evac f_sig q_silu tok_mm tok_evac lr_t lr_evac gate_mm gate_exp gate_min gate_done
            score_mm score_max score_exp probs_done probsT_mm probsT_evac pv_mm pv_hi pv_lo
            sweep_mm swept_v swept_a level_done khat_t khat_evac u_mm state_done o_mm o_evac o_ss o_r o_done yT_mm yT_hi yT_lo
            proj_mm h_added mem_ss mem_r memT_mm m_hi_done m_lo_done ckv_mm ckv_evac ck_ss ck_r ck_done ckT_mm ckT_evac
            cq_mm cq_evac cq_ss cq_r cq_done cqT_mm cqT_evac
            ffn_mm gate_ready silu_done act_ready a_hi_done a_lo_done set_up lbT""".split()
        S = {n: ctx.enter_context(nc.semaphore(n)) for n in names}
        raw_in = [ctx.enter_context(nc.semaphore(f"raw_in{i}")) for i in range(RAW)]
        every_sem = [S[n] for n in names] + raw_in
        x_in = ctx.enter_context(nc.semaphore("x_in"))
        stored = ctx.enter_context(nc.semaphore("stored"))

        def gain(name, n):
            c = rows_of[name][0] + n
            return gains[:, c:c + 1]

        def spread_col(name):
            c, n = spread_of[name]
            return spread[:, c:c + n]

        def nope_of(tok, t):
            return tok[:, t, :].rearrange("p (r y) -> p r y", r=2)[:, :, 0:2 * NOPE].rearrange("p r (h x) -> p r h x", h=2)

        def rope_of(tok, t):
            return tok[:, t, :].rearrange("p (r y) -> p r y", r=2)[:, :, 2 * NOPE:PAIR].rearrange("p r (h x) -> p r h x", h=2)

        def chain(eng, sem):
            count = [0]

            def link(ins):
                count[0] += 1
                ins.then_inc(sem, 1)
                eng.wait_ge(sem, count[0])
            return link

        with nc.Block() as block:
            @block.sync
            def _(sp):
                for t in range(NT):
                    sp.dma_start(h[:, t, :], A["x"][0, t * P:(t + 1) * P, :]).then_inc(x_in, 16)
                sp.dma_start(pos_i[:, :], A["positions"][0].rearrange("(t p) -> p t", p=P),
                             allow_slow_non_contiguous=True).then_inc(S["mem_in"], 16)
                sp.dma_start(lb_rows[:, :], A["hgrn_lb_logits"].rearrange("l (c p) -> (l c) p", p=P)
                             ).then_inc(S["vectors_in"], 16)
                sp.wait_ge(x_in, 16 * NT)

            @block.gpsimd
            def _(pool):
                pool.memset(ident[:, :], 0.0).then_inc(S["chain_v"], 1)
                pool.iota(idx_i[:, :], pattern=[[1, P]], base=0, channel_multiplier=0).then_inc(S["feat_mm"], 1)
                pool.iota(idx_j[:, :], pattern=[[0, P]], base=0, channel_multiplier=1).then_inc(S["feat_mm"], 1)
                pool.wait_ge(S["chain_v"], 1)
                pool.affine_select(out=ident[:, :], in_=ident[:, :], compare_op=ALU.not_equal, fill=1.0,
                                   base=0, pattern=[[-1, P]], channel_multiplier=1).then_inc(S["set_up"], 1)

            @block.tensor
            def _(pe):
                pe.wait_ge(S["set_up"], 1)
                pe.wait_ge(S["vectors_in"], 16)
                pe.transpose(pb[0][:, 0:2 * DEPTH], lb_rows[:, :], ident[0:2 * DEPTH, 0:2 * DEPTH]
                             ).then_inc(S["lbT"], 1)

            @block.scalar
            def _(eng):
                eng.wait_ge(S["gate_min"], 1)
                eng.activation(lb_t[:, 2], lb_t[:, 1], ACT.Exp).then_inc(S["gate_exp"], 1)
                eng.wait_ge(S["gate_done"], 1)
                eng.activation(sin[:, :, :], ang[:, :, :], ACT.Sin).then_inc(S["r_done"], 1)
                eng.wait_ge(S["gate_done"], 2)
                eng.activation(cos[:, :, :], turns[:, :, :], ACT.Sin).then_inc(S["r_done"], 1)

            @block.vector
            def _(dve):
                link = chain(dve, S["chain_a"])
                dve.memset(ones[:, :], 1.0)
                dve.memset(eps_c[:, :], EPS)
                inv = (np.float32(THETA) ** (-np.arange(0, ROPE, 2, dtype=np.float32) / np.float32(ROPE))).astype(np.float32)
                for j in range(ROPE // 2 - 1):
                    dve.memset(freq[:, j:j + 1], float(inv[j]))
                link(dve.memset(freq[:, ROPE // 2 - 1:ROPE // 2], float(inv[-1])))
                dve.wait_ge(S["feat_mm"], 2)
                for m, mask in pair_mask.items():
                    s = m.bit_length() - 1
                    dve.tensor_scalar(mk[0][:, :], idx_i[:, :], s, None, ALU.logical_shift_right)
                    link(dve.tensor_scalar(mk[1][:, :], idx_j[:, :], s, None, ALU.logical_shift_right))
                    link(dve.tensor_tensor(mk[2][:, :], mk[0][:, :], mk[1][:, :], ALU.subtract))
                    link(dve.tensor_scalar(mk[1][:, :], mk[2][:, :], 1.0, None, ALU.is_equal))
                    link(dve.tensor_scalar(mk[2][:, :], idx_i[:, :], s, 1, ALU.logical_shift_right, ALU.bitwise_and))
                    link(dve.tensor_tensor(mask[:, :], mk[1][:, :], mk[2][:, :], ALU.mult))
                dve.wait_ge(S["lbT"], 1)
                link(dve.tensor_copy(lb_t[:, 0], pb[0][:, 0:2 * DEPTH].rearrange("p (l c) -> p c l", c=2)))
                link(dve.reduce_max(lb_t[:, 3, :, 0:1], lb_t[:, 0], AX.X))
                dve.tensor_tensor(lb_t[:, 1], lb_t[:, 0], lb_t[:, 3, :, 0:1].to_broadcast([P, 2, DEPTH]),
                                  ALU.subtract).then_inc(S["gate_min"], 1)
                dve.wait_ge(S["gate_exp"], 1)
                link(dve.reduce_sum(lb_t[:, 4, :, 0:1], lb_t[:, 2], AX.X))
                link(dve.reciprocal(lb_t[:, 5, :, 0:1], lb_t[:, 4, :, 0:1]))
                link(dve.tensor_tensor(lb_t[:, 6], lb_t[:, 2], lb_t[:, 5, :, 0:1].to_broadcast([P, 2, DEPTH]), ALU.mult))
                link(dve.tensor_copy(lb_t[:, 7, :, 0:1], lb_t[:, 6, :, 0:1]))
                for l in range(1, DEPTH):
                    link(dve.tensor_tensor(lb_t[:, 7, :, l:l + 1], lb_t[:, 7, :, l - 1:l], lb_t[:, 6, :, l:l + 1], ALU.add))
                link(dve.tensor_tensor(lb_all[:, :, :], lb_t[:, 7], lb_t[:, 6, :, 0:1].to_broadcast([P, 2, DEPTH]),
                                       ALU.subtract))
                dve.wait_ge(S["mem_in"], 16)
                link(dve.tensor_copy(pos_f[:, :], pos_i[:, :]))
                link(dve.tensor_tensor(ang[:, :, :], pos_f[:, :].unsqueeze(2).to_broadcast([P, NT, ROPE // 2]),
                                       freq[:, :].unsqueeze(1).to_broadcast([P, NT, ROPE // 2]), ALU.mult))
                link(dve.tensor_scalar(turns_i[:, :, :], ang[:, :, :], 1 / (2 * math.pi), None, ALU.mult))
                link(dve.tensor_copy(turns[:, :, :], turns_i[:, :, :]))
                c1 = 6.28125
                c2 = float(np.float32(math.floor((2 * math.pi - c1) * 2 ** 20) / 2 ** 20))
                c3 = 2 * math.pi - c1 - c2
                for c in (c1, c2, c3):
                    link(dve.scalar_tensor_tensor(ang[:, :, :], turns[:, :, :], -c, ang[:, :, :], ALU.mult, ALU.add))

                def wrap(a):
                    for cmp, lim, turn in ((ALU.is_gt, math.pi, -2 * math.pi), (ALU.is_lt, -math.pi, 2 * math.pi)):
                        link(dve.tensor_scalar(over[:, :, :], a, lim, turn, cmp, ALU.mult))
                        link(dve.tensor_tensor(a, a, over[:, :, :], ALU.add))

                wrap(ang[:, :, :])
                link(dve.tensor_scalar(turns[:, :, :], ang[:, :, :], math.pi / 2, None, ALU.add))
                wrap(turns[:, :, :])
                bound = float(np.nextafter(np.float32(math.pi), np.float32(0)))
                dve.tensor_scalar(ang[:, :, :], ang[:, :, :], bound, -bound, ALU.min, ALU.max).then_inc(S["gate_done"], 1)
                dve.tensor_scalar(turns[:, :, :], turns[:, :, :], bound, -bound, ALU.min, ALU.max).then_inc(S["gate_done"], 1)
                dve.wait_ge(S["r_done"], 2)

        def clear_semaphores():
            nc.all_engine_barrier()
            nums = sorted(s.num for s in every_sem)
            assert nums == list(range(nums[0], nums[0] + len(nums)))
            nc.gpsimd.sem_clear(range(nums[0], nums[-1] + 1))
            nc.all_engine_barrier()

        clear_semaphores()

        H_ADDS = 2 * NT
        ATT, R_MIX, R_CA, R_FFN, R_LAT, R_MEM = 0, 128, 140, 152, 164, 180
        R_CK, R_CQ = 186, 210
        R_QK, R_O = 260, 420
        LEVELS = (0, 1, 2, 4, 8, 16, 32, 64)

        def block_decay(m, rows_, f):
            buf = decay if m.bit_length() % 2 else decay_m
            return buf[rows_, f, 0:SEQ // m]

        layers = ctx.enter_context(ExitStack())
        layer = layers.enter_context(nc.Fori(0, DEPTH))
        with nc.Block() as block:

            arrivals, total = [], [0] * RAW

            @block.sync
            def _(sp):
                for name, (r0, n) in rows_of.items():
                    src = A[name][layer]
                    src = src.rearrange("t (c p) -> (t c) p", p=P) if len(src.shape) == 2 else \
                        src.rearrange("(c p) -> c p", p=P)
                    sp.dma_start(rows[r0:r0 + n, :], src).then_inc(S["vectors_in"], 16)
                for i, (nk, cols, src) in enumerate(slabs):
                    if i == 4:
                        sp.dma_start(w_gate[:, :], A["gla_w_gate"][layer]).then_inc(S["spread_in"], 16)
                        for name, (c, n) in spread_of.items():
                            sp.dma_start(spread[:, c:c + n], A[name][layer].partition_broadcast(P)
                                         ).then_inc(S["spread_in"], 16)
                    if i == slab_at["mix", 1, 0]:
                        sp.wait_ge(S["pv_mm"], NH)
                        sp.wait_ge(S["gate_done"], 1)
                        sp.wait_ge(S["probsT_mm"], NH * NT)
                        for m in range(MT):
                            sp.dma_start(mem_tok[:, m, :], A["mem"][0, m * P:(m + 1) * P, :]).then_inc(S["mem_in"], 16)
                    if i >= RAW:
                        sp.wait_ge(S["lo_split"], i - RAW + 1)
                    for dst, part in src(layer, raw[i % RAW]):
                        sp.dma_start(dst, part).then_inc(raw_in[i % RAW], 16)
                        total[i % RAW] += 16
                    arrivals.append(total[i % RAW])

            @block.gpsimd
            def _(pool):
                for i, (nk, cols, _) in enumerate(slabs):
                    n = nk * cols
                    pool.wait_ge(S["hi_split"], i + 1)
                    pool.tensor_tensor(w_lo[i % SPLIT][:, 0:n], raw[i % RAW][:, 0:n],
                                       w_hi[i % SPLIT][:, 0:n].bitcast(f32), ALU.subtract).then_inc(S["lo_split"], 1)

            released = {}

            @block.tensor
            def _(pe):
                freed, count = {}, {}

                def mark(ins, sem):
                    ins.then_inc(sem, 1)
                    count[id(sem)] = count.get(id(sem), 0) + 1
                    return sem, count[id(sem)]

                def claim(b):
                    if b in freed:
                        pe.wait_ge(*freed[b])

                def use(name):
                    i = slab_at[name]
                    nk, cols, _ = slabs[i]
                    pe.wait_ge(S["lo_split"], i + 1)
                    return [w[i % SPLIT][:, 0:nk * cols].rearrange("p (k c) -> p k c", k=nk) for w in (w_hi, w_lo)]

                def product(o, a, b, first, last):
                    (ah, al), (bh, bl) = a, b
                    pe.matmul(o, ah, bh, start=first, stop=False)
                    pe.matmul(o, ah, bl, start=False, stop=False)
                    return pe.matmul(o, al, bh, start=False, stop=last)

                def transpose_h(w):
                    if w:
                        pe.wait_ge(S["h_added"], H_ADDS * w)
                    for k in range(KD):
                        b = 4 + k % 4
                        claim(b)
                        for t in range(NT):
                            mm = pe.transpose(pb[b][:, t * P:(t + 1) * P], h[:, t, k * P:(k + 1) * P], ident[:, :])
                        mark(mm, S["hT_mm"])
                        freed[b] = (S["x_lo_done"], w * KD + k + 1)

                def spread_r(n):
                    claim(4)
                    pe.wait_ge(S["r_diag_done"], n + 1)
                    mark(pe.matmul(pb[4][:, :], ones[:, :], r_diag[:, :, :].rearrange("p t c -> p (t c)"),
                                   start=True, stop=True), S["r_mm"])
                    freed[4] = (S["r_bc_done"], n + 1)

                def feature_chunk(name, b, w, done, evac):
                    claim(b)
                    wh, wl = use(name)
                    for k in range(KD):
                        pe.wait_ge(S["x_lo_done"], w * KD + k + 1)
                        mm = product(pb[b][:, :], (wh[:, k, :], wl[:, k, :]), (x_hi[:, k, :], x_lo[:, k, :]),
                                     k == 0, k == KD - 1)
                    released[slab_at[name]] = mark(mm, done)
                    freed[b] = evac

                def token_group(names, b0, cols, x, k0, ready, done, evac, nt=NT):
                    xh, xl = x
                    nk_all = sum(slabs[slab_at[n]][0] for n in names)
                    k = 0
                    for n in names:
                        wh, wl = use(n)
                        for kk in range(slabs[slab_at[n]][0]):
                            if ready is not None:
                                pe.wait_ge(*ready(k))
                            for t in range(nt):
                                if k == 0:
                                    claim(b0 + t)
                                mm = product(pb[b0 + t][:, 0:cols],
                                             (xh[:, k0 + k, t * P:(t + 1) * P], xl[:, k0 + k, t * P:(t + 1) * P]),
                                             (wh[:, kk, :], wl[:, kk, :]), k == 0, k == nk_all - 1)
                                if k == nk_all - 1:
                                    last = mark(mm, done)
                            k += 1
                        released[slab_at[n]] = last if k == nk_all else mark(mm, S["slab_used"])
                    for t in range(nt):
                        freed[b0 + t] = (evac[0], evac[1] + t + 1)

                def attend(base, score, width, pv_rhs, values, pT):
                    items = NH * NT
                    for i in range(items + 3):
                        if i < items:
                            hd, t = divmod(i, NT)
                            claim(4 + i % 2)
                            mark(score(pb[4 + i % 2], hd, t), S["score_mm"])
                            freed[4 + i % 2] = (S["score_exp"], base + i + 1)
                        j = i - 2
                        if 0 <= j < items:
                            hd, t = divmod(j, NT)
                            b = 6 + j % 2
                            claim(b)
                            pe.wait_ge(S["probs_done"], base + j + 1)
                            src = (probs if base == 0 else cprobs)[j % 2]
                            for n in range(width(t)):
                                mm = pe.transpose(pb[b][:, n * P:(n + 1) * P], src[:, n * P:(n + 1) * P], ident[:, :])
                            mark(mm, S["probsT_mm"])
                            freed[b] = (S["probsT_evac"], base + j + 1)
                        j = i - 3
                        if 0 <= j < items and j % NT == NT - 1:
                            hd = j // NT
                            claim(hd)
                            pe.wait_ge(S["probsT_evac"], base + j + 1)
                            n_blocks = width(NT - 1)
                            for n in range(n_blocks):
                                q0 = pv_rhs(n)
                                mm = pe.matmul(pb[hd][:, q0:SEQ], values(n, hd), pT[:, n, q0:SEQ],
                                               start=(n == 0), stop=(n == n_blocks - 1))
                            mark(mm, S["pv_mm"])
                            freed[hd] = (S["pv_lo"], base // NT + hd + 1)

                pe.wait_ge(S["vectors_in"], 16 * len(rows_of))
                mark(pe.transpose(pb[0][:, 0:ROWS], rows[0:ROWS, :], ident[0:ROWS, 0:ROWS]), S["rows_t"])
                freed[0] = (S["gains_ready"], 1)
                transpose_h(0)
                spread_r(0)
                for n in range(4):
                    feature_chunk(("lat", n), n, 0, S["lat_mm"], (S["lat_evac"], n + 1))
                X = (x_hi, x_lo)
                token_group(["rope"], 4, ROPE, X, 0, None, S["rope_mm"], (S["rope_evac"], 0))
                claim(0)
                pe.wait_ge(S["lat_sq_done"], 4)
                for n in range(2):
                    for t in range(NT):
                        for c in range(2):
                            mm = pe.matmul(pb[0][:, n * NT + t:n * NT + t + 1], lat_sq[:, 2 * n + c, t * P:(t + 1) * P],
                                           ones[:, 0:1], start=(c == 0), stop=(c == 1))
                mark(mm, S["lat_ss_mm"])
                freed[0] = (S["r_lat_done"], 1)
                L = (lat_hi, lat_lo)
                for n in range(2):
                    token_group([("q_up", n)], 4 * n, 2 * QK, L, 0, lambda k: (S["lat_lo_done"], k + 1),
                                S["q_mm"], (S["q_evac"], NT * n))
                token_group([("kv_up", 0)], 0, NH * P, L, 2, lambda k: (S["lat_lo_done"], k + 3), S["k_mm"], (S["k_evac"], 0))
                token_group([("kv_up", 1)], 4, NH * P, L, 2, None, S["v_mm"], (S["v_evac"], 0))
                for n in range(len(FEATS)):
                    feature_chunk(("feat", n), n % 4, 0, S["feat_mm"], (S["feat_evac"], n + 1))

                def transpose_qk(z, src):
                    for t in range(NT):
                        pe.wait_ge(S["qk_done"], z * NT + t + 1)
                        b = 2 * (t % 2)
                        claim(b)
                        for hd in range(NH):
                            mm = pe.transpose(pb[b][:, hd * P:(hd + 1) * P], src[:, t, PAIR * (hd // 2) + P * (hd % 2):][:, 0:P], ident[:, :])
                        mark(mm, S["qkT_mm"])
                        freed[b] = (S["qkT_evac"], 2 * (z * NT + t) + 1)
                        claim(b + 1)
                        for r in range(2):
                            mm = pe.transpose(pb[b + 1][:, r * P:(r + 1) * P], src[:, t, PAIR * r + 2 * NOPE:PAIR * (r + 1)], ident[:, :])
                        mark(mm, S["qkT_mm"])
                        freed[b + 1] = (S["qkT_evac"], 2 * (z * NT + t) + 2)

                transpose_qk(0, q_tok)
                token_group([("vg", n) for n in range(3)], 4, VG, X, 0, None, S["tok_mm"], (S["tok_evac"], 0))
                transpose_qk(1, k_tok)
                token_group([("br", n) for n in range(2)], 4, NH * GDV, X, 0, None, S["tok_mm"], (S["tok_evac"], NT))
                token_group([("cig", n) for n in range(4)], 0, 2 * NH * HDV, X, 0, None, S["tok_mm"], (S["tok_evac"], 2 * NT))
                claim(4)
                pe.wait_ge(S["tok_evac"], NT)
                for t in range(NT):
                    mm = pe.transpose(pb[4][0:RANK, t * P:(t + 1) * P], vg_tok[:, t, NH * GDV:VG], ident[:, :])
                mark(mm, S["lr_t"])
                freed[4] = (S["lr_evac"], 1)
                claim(5)
                pe.wait_ge(S["lr_evac"], 1)
                pe.wait_ge(S["spread_in"], 16 * (1 + len(spread_of)))
                mark(pe.matmul(pb[5][:, :], w_gate[:, :], lrT[:, :], start=True, stop=True), S["gate_mm"])
                freed[5] = (S["gate_min"], 1)
                pe.wait_ge(S["qkT_evac"], 4 * NT)
                pe.wait_ge(S["v_evac"], NT)

                def mla_score(bank, hd, t):
                    n = (t + 1) * P
                    pe.matmul(bank[:, 0:n], qT_n[:, hd, t * P:(t + 1) * P], kT_n[:, hd, 0:n], start=True, stop=False)
                    r = slice(ROPE * (hd % 2), ROPE * (hd % 2) + ROPE)
                    return pe.matmul(bank[:, 0:n], qT_r[r, hd // 2, t * P:(t + 1) * P], kT_r[r, hd // 2, 0:n],
                                     start=False, stop=True)

                attend(0, mla_score, lambda t: t + 1, lambda n: n * P,
                       lambda n, hd: v_tok[:, n, hd * VD:(hd + 1) * VD], probsT)
                for li, m in enumerate(LEVELS):
                    for hh in range(2 * NH):
                        f, rows_ = (0, slice(GDK * hh, GDK * (hh + 1))) if hh < NH else \
                            (1 + (hh - NH) // 2, slice(HDK * (hh % 2), HDK * (hh % 2 + 1)))
                        claim(hh)
                        pe.wait_ge(S["level_done"], 2 * li + (1 if hh < NH else 2))
                        for n in range(NT):
                            j0, j1, i0 = (n * P, (n + 1) * P, n * P) if m < 64 else (n * P, n * P + 64, n * P + 64)
                            mm = pe.matmul(pb[hh][0:j1 - j0, i0:(n + 1) * P], K[rows_, f, j0:j1],
                                           Q[rows_, f, i0:(n + 1) * P], start=True, stop=True)
                        mark(mm, S["sweep_mm"])
                        freed[hh] = (S["swept_v"], 2 * NH * li + hh + 1) if m < 16 else \
                            (S["swept_a"], 2 * NH * (li - 5) + hh + 1)
                pe.wait_ge(S["level_done"], 2 * len(LEVELS) + 2)
                for f in range(3):
                    claim(f)
                    for n in range(NT):
                        mm = pe.transpose(pb[f][:, n * P:(n + 1) * P], K[:, f, n * P:(n + 1) * P], ident[:, :])
                    mark(mm, S["khat_t"])
                    freed[f] = (S["khat_evac"], f + 1)
                pe.wait_ge(S["tok_evac"], 3 * NT)
                for n in range(NT - 1):
                    claim(3 + n)
                    pe.wait_ge(S["khat_evac"], 3)
                    pe.matmul(pb[3 + n][:, 0:256], k_hat[:, 0, n, :], vg_tok[:, n, 0:256], start=True, stop=True)
                    for f in range(2):
                        mm = pe.matmul(pb[3 + n][:, 256 + f * P:256 + (f + 1) * P], k_hat[:, 1 + f, n, :],
                                       ci_tok[:, n, f * P:(f + 1) * P], start=True, stop=True)
                    mark(mm, S["u_mm"])
                    freed[3 + n] = (S["state_done"], n + 1)
                for n in range(NT):
                    b = (6, 7, 0, 1)[n]
                    claim(b)
                    pe.wait_ge(S["swept_a"], 3 * 2 * NH)
                    if n:
                        pe.wait_ge(S["state_done"], n)
                        for f in range(3):
                            c = slice(0, 256) if f == 0 else slice(P + f * P, 2 * P + f * P)
                            pe.matmul(pb[b][:, c], Q[:, f, n * P:(n + 1) * P], state[:, n - 1, c],
                                      start=(f == 0), stop=False, skip_group_check=True)
                    for hh in range(2 * NH):
                        sc, val = (scores_g, vg_tok) if hh < NH else (scores_h, ci_tok)
                        hd = hh % NH
                        mm = pe.matmul(pb[b][:, hh * 64:(hh + 1) * 64], sc[:, hd, n, :], val[:, n, hd * 64:(hd + 1) * 64],
                                       start=(n == 0 and hh == 0), stop=(hh == 2 * NH - 1), skip_group_check=True)
                    mark(mm, S["o_mm"])
                    freed[b] = (S["o_evac"], n + 1)
                for c in range(4):
                    claim(2 + c)
                    for n in range(NT):
                        pe.wait_ge(S["o_done"], n + 1)
                        mm = pe.transpose(pb[2 + c][:, n * P:(n + 1) * P], o_tok[:, n, c * P:(c + 1) * P], ident[:, :])
                    mark(mm, S["yT_mm"])
                    freed[2 + c] = (S["yT_lo"], c + 1)
                def project(name, nk, ready, x, base):
                    for half in range(2):
                        token_group([(name, half, n) for n in range((nk + 1) // 2)], 4 * half, HALF, x, 0, ready,
                                    S["proj_mm"], (S["h_added"], base + NT * half))

                project("mix", KD, lambda k: (S["pv_lo"], k + 1) if k < NH else (S["yT_lo"], k - NH + 1), X, 0)
                pe.wait_ge(S["mem_in"], 16 * MT)
                for c in range(KD // 2):
                    claim(4 + c)
                    for k in range(2):
                        for m in range(MT):
                            mm = pe.transpose(pb[4 + c][:, k * NM + m * P:k * NM + (m + 1) * P],
                                              mem_tok[:, m, (2 * c + k) * P:(2 * c + k + 1) * P], ident[:, :])
                    mark(mm, S["memT_mm"])
                    freed[4 + c] = (S["m_lo_done"], 2 * c + 2)
                for half in range(2):
                    token_group([("ckv", half, n) for n in range(KD // 2)], 2 * half, HALF, (m_hi, m_lo), 0,
                                lambda k: (S["m_lo_done"], k + 1), S["ckv_mm"], (S["ckv_evac"], MT * half), nt=MT)
                    if half == 0:
                        transpose_h(1)
                token_group([("caq", n) for n in range(KD // 2)], 4, NH * P, X, 0, lambda k: (S["x_lo_done"], KD + k + 1),
                            S["cq_mm"], (S["cq_evac"], 0))
                pe.wait_ge(S["ck_done"], 1)
                for r in range(2):
                    claim(r)
                    for hd in range(2):
                        for m in range(MT):
                            c = (2 * r + hd) * 2 * P
                            mm = pe.transpose(pb[r][:, hd * NM + m * P:hd * NM + (m + 1) * P], ckv_tok[:, m, c:c + P], ident[:, :])
                    mark(mm, S["ckT_mm"])
                    freed[r] = (S["ckT_evac"], r + 1)
                for t in range(NT):
                    claim(2 + t % 2)
                    pe.wait_ge(S["cq_done"], t + 1)
                    for hd in range(NH):
                        mm = pe.transpose(pb[2 + t % 2][:, hd * P:(hd + 1) * P], cq_tok[:, t, hd * P:(hd + 1) * P], ident[:, :])
                    mark(mm, S["cqT_mm"])
                    freed[2 + t % 2] = (S["cqT_evac"], t + 1)
                pe.wait_ge(S["ckT_evac"], 2)
                pe.wait_ge(S["cqT_evac"], NT)

                def ca_score(bank, hd, t):
                    return pe.matmul(bank[:, 0:NM], cqT[:, hd, t * P:(t + 1) * P], ckT[:, hd, :], start=True, stop=True)

                attend(NH * NT, ca_score, lambda t: MT, lambda n: 0,
                       lambda n, hd: ckv_tok[:, n, hd * 2 * P + P:(hd + 1) * 2 * P], cprobsT)
                project("cao", NH, lambda k: (S["pv_lo"], NH + k + 1), X, H_ADDS)
                transpose_h(2)
                spread_r(1)
                for g in range(FG):
                    for c in range(FCG):
                        n = g * FCG + c
                        feature_chunk(("gate", g, c), 2 * (n % 2), 2, S["ffn_mm"], (S["gate_ready"], n + 1))
                        feature_chunk(("up", g, c), 2 * (n % 2) + 1, 2, S["ffn_mm"], (S["act_ready"], n + 1))
                    project(("ffo", g), FCG, lambda k: (S["a_lo_done"], g * FCG + k + 1), (a_hi, a_lo), (2 + g) * H_ADDS)

            @block.scalar
            def _(act_):
                link = chain(act_, S["chain_a"])
                nsplit = [0]

                def split_through(i):
                    while nsplit[0] <= min(i, NS - 1):
                        k = nsplit[0]
                        n = slabs[k][0] * slabs[k][1]
                        act_.wait_ge(raw_in[k % RAW], arrivals[k])
                        if k >= SPLIT:
                            act_.wait_ge(*released[k - SPLIT])
                        act_.activation(w_hi[k % SPLIT][:, 0:n], raw[k % RAW][:, 0:n], ACT.Copy).then_inc(S["hi_split"], 1)
                        nsplit[0] += 1

                def ahead(name):
                    split_through(slab_at[name] + SPLIT - 1)

                def inverse_rms(dst, tmp, ss, n, done):
                    link(act_.activation(tmp, ss, ACT.Ln, bias=eps_c[:, 0:1], scale=1.0 / n))
                    act_.activation(dst, tmp, ACT.Exp, scale=-0.5).then_inc(done, 1)

                def norm(w, name, r_col):
                    for k in range(KD):
                        act_.wait_ge(S["hT_mm"], w * KD + k + 1)
                        act_.activation(x_hi[:, k, :], pb[4 + k % 4][:, :], ACT.Copy, scale=gain(name, k)).then_inc(S["x_hi_done"], 1)
                        if k % 2 == 1:
                            t = k // 2
                            link(act_.activation(junk[:, :], h[:, t, :], ACT.Square, accum_out=small[:, r_col + t:r_col + t + 1]))
                    inverse_rms(small[:, r_col + 8:r_col + 12], small[:, r_col + 4:r_col + 8], small[:, r_col:r_col + 4], D, S["r_done"])

                def attend(base, n_keys, scale, pT, pr):
                    items = NH * NT
                    for i in range(items + 3):
                        if i < items:
                            hd, t = divmod(i, NT)
                            n = n_keys(t)
                            c = ATT + base + i
                            act_.wait_ge(S["score_max"], base + i + 1)
                            if i >= 2:
                                act_.wait_ge(S["probsT_mm"], base + i - 1)
                            act_.activation(pr[i % 2][:, 0:n], pb[4 + i % 2][:, 0:n], ACT.Exp, bias=small[:, c + 32:c + 33],
                                            scale=scale, accum_out=small[:, c + 64:c + 65]).then_inc(S["score_exp"], 1)
                        j = i - 2
                        if 0 <= j < items:
                            hd, t = divmod(j, NT)
                            nb = n_keys(t) // P
                            act_.wait_ge(S["probsT_mm"], base + j + 1)
                            if t == 0 and hd:
                                act_.wait_ge(S["pv_mm"], base // NT + hd)
                            act_.activation(pT[:, 0:nb, t * P:(t + 1) * P],
                                            pb[6 + j % 2][:, 0:nb * P].rearrange("p (n q) -> p n q", n=nb),
                                            ACT.Copy).then_inc(S["probsT_evac"], 1)
                        j = i - 3
                        if 0 <= j < items and j % NT == NT - 1:
                            hd = j // NT
                            act_.wait_ge(S["pv_mm"], base // NT + hd + 1)
                            act_.activation(x_hi[:, hd, :], pb[hd][:, :], ACT.Copy).then_inc(S["pv_hi"], 1)

                split_through(SPLIT - 1)
                act_.wait_ge(S["rows_t"], 1)
                act_.activation(gains[:, 0:ROWS], pb[0][:, 0:ROWS], ACT.Copy).then_inc(S["gains_ready"], 1)
                act_.wait_ge(S["gains_ready"], 1)
                norm(0, "norm_mix", R_MIX)
                for n in range(4):
                    ahead(("lat", n))
                    act_.wait_ge(S["lat_evac"], n + 1)
                    act_.activation(lat_sq[:, n, :], lat[:, n, :], ACT.Square).then_inc(S["lat_sq_done"], 1)
                    g_ = gain("mla_q_lat_norm", n) if n < 2 else gain("mla_kv_lat_norm", n - 2)
                    act_.activation(lat_hi[:, n, :], lat[:, n, :], ACT.Copy, scale=g_).then_inc(S["lat_hi_done"], 1)
                ahead("rope")
                act_.wait_ge(S["r_done"], 1)
                for t in range(NT):
                    act_.wait_ge(S["rope_mm"], t + 1)
                    act_.activation(kr_tok[:, t, :], pb[4 + t][:, 0:ROPE], ACT.Copy,
                                    scale=small[:, R_MIX + 8 + t:R_MIX + 9 + t]).then_inc(S["rope_evac"], 1)
                act_.wait_ge(S["lat_ss_mm"], 1)
                inverse_rms(small[:, R_LAT + 8:R_LAT + 16], small[:, R_LAT:R_LAT + 8], pb[0][:, 0:8], QL, S["r_lat_done"])
                act_.wait_ge(S["r_lat_done"], 1)
                for n in range(2):
                    ahead(("q_up", n))
                    for t in range(NT):
                        act_.wait_ge(S["q_mm"], NT * n + t + 1)
                        act_.activation(q_tok[:, t, n * 2 * QK:(n + 1) * 2 * QK], pb[4 * n + t][:, 0:2 * QK], ACT.Copy,
                                        scale=small[:, R_LAT + 8 + t:R_LAT + 9 + t]).then_inc(S["q_evac"], 1)
                ahead(("kv_up", 0))
                for t in range(NT):
                    act_.wait_ge(S["k_mm"], t + 1)
                    act_.activation(nope_of(k_tok, t), pb[t][:, :].rearrange("p (r h x) -> p r h x", r=2, h=2), ACT.Copy,
                                    scale=small[:, R_LAT + 12 + t:R_LAT + 13 + t]).then_inc(S["k_evac"], 1)
                ahead(("kv_up", 1))
                for t in range(NT):
                    act_.wait_ge(S["v_mm"], t + 1)
                    act_.activation(v_tok[:, t, :], pb[4 + t][:, :], ACT.Copy,
                                    scale=small[:, R_LAT + 12 + t:R_LAT + 13 + t]).then_inc(S["v_evac"], 1)
                for n in range(2 * NT):
                    if n < len(FEATS):
                        ahead(("feat", n))
                    c = R_QK + 4 * n
                    act_.wait_ge(S["qk_ss"], n + 1)
                    inverse_rms(small[:, c + 128:c + 132], small[:, c + 96:c + 100], small[:, c + 64:c + 68], QK, S["qk_r"])

                def qkT(z, dn, dr):
                    for t in range(NT):
                        b = 2 * (t % 2)
                        act_.wait_ge(S["qkT_mm"], 2 * (z * NT + t) + 1)
                        act_.activation(dn[:, :, t * P:(t + 1) * P], pb[b][:, :].rearrange("p (h q) -> p h q", h=NH),
                                        ACT.Copy).then_inc(S["qkT_evac"], 1)
                        act_.wait_ge(S["qkT_mm"], 2 * (z * NT + t) + 2)
                        act_.activation(dr[:, :, t * P:(t + 1) * P], pb[b + 1][:, 0:2 * P].rearrange("p (r q) -> p r q", r=2),
                                        ACT.Copy).then_inc(S["qkT_evac"], 1)

                qkT(0, qT_n, qT_r)
                act_.wait_ge(S["feat_evac"], 2)
                link(act_.activation(K[:, 1:3, :], decay[:, 1:3, :], ACT.Sigmoid, scale=-1.0))
                act_.activation(decay[:, 1:3, :], decay[:, 1:3, :], ACT.Sigmoid).then_inc(S["f_sig"], 1)
                ahead(("vg", 2))
                act_.wait_ge(S["feat_evac"], 4)
                act_.activation(Q[:, 1:3, :], Q[:, 1:3, :], ACT.Silu).then_inc(S["q_silu"], 1)

                def r_mix(t):
                    return small[:, R_MIX + 8 + t:R_MIX + 9 + t]

                for t in range(NT):
                    act_.wait_ge(S["tok_mm"], t + 1)
                    act_.activation(vg_tok[:, t, :], pb[4 + t][:, 0:VG], ACT.Copy, scale=r_mix(t)).then_inc(S["tok_evac"], 1)
                qkT(1, kT_n, kT_r)
                ahead(("br", 1))
                for t in range(NT):
                    act_.wait_ge(S["tok_mm"], NT + t + 1)
                    act_.activation(sg_tok[:, t, 0:256], pb[4 + t][:, 0:256], ACT.Silu, scale=r_mix(t)).then_inc(S["tok_evac"], 1)
                ahead(("cig", 3))
                for t in range(NT):
                    act_.wait_ge(S["tok_mm"], 2 * NT + t + 1)
                    act_.activation(ci_tok[:, t, :], pb[t][:, 0:256], ACT.Copy, scale=r_mix(t))
                    act_.activation(sg_tok[:, t, 256:512], pb[t][:, 256:512], ACT.Silu, scale=r_mix(t)).then_inc(S["tok_evac"], 1)
                act_.wait_ge(S["gate_mm"], 1)
                link(act_.activation(gate_tmp[:, :], pb[5][:, :], ACT.Abs, bias=gain("gla_b_gate", 0)))
                link(act_.activation(gate_tmp[:, :], gate_tmp[:, :], ACT.Exp, scale=-1.0))
                act_.activation(gate_tmp[:, :], gate_tmp[:, :], ACT.Ln, bias=ones[:, 0:1]).then_inc(S["gate_exp"], 1)
                act_.wait_ge(S["gate_min"], 1)
                act_.activation(decay[:, 0, :], decay[:, 0, :], ACT.Exp, scale=1.0 / TAU).then_inc(S["gate_done"], 1)
                attend(0, lambda t: (t + 1) * P, QK ** -0.5, probsT, probs)
                act_.wait_ge(S["swept_v"], 5 * 2 * NH)
                for li, m in enumerate(LEVELS):
                    if m < 16:
                        continue
                    for hh in range(2 * NH):
                        sc = scores_g if hh < NH else scores_h
                        act_.wait_ge(S["sweep_mm"], 2 * NH * li + hh + 1)
                        src = pb[hh][:, :].rearrange("p (n q) -> p n q", n=NT)
                        for b in range(64 // m):
                            j, i = 2 * m * b, 2 * m * b + m
                            cp = act_.activation(sc[j:j + m, hh % NH, :, i:i + m], src[j:j + m, :, i:i + m], ACT.Copy)
                        cp.then_inc(S["swept_a"], 1)
                for f in range(3):
                    act_.wait_ge(S["khat_t"], f + 1)
                    act_.activation(k_hat[:, f], pb[f][:, :].rearrange("p (n q) -> p n q", n=NT), ACT.Copy).then_inc(S["khat_evac"], 1)
                for n in range(NT):
                    act_.wait_ge(S["o_mm"], n + 1)
                    act_.activation(o_tok[:, n, :], pb[(6, 7, 0, 1)[n]][:, :], ACT.Copy).then_inc(S["o_evac"], 1)
                    c = R_O + 8 * n
                    act_.wait_ge(S["o_ss"], n + 1)
                    inverse_rms(small[:, c + 64:c + 72], small[:, c + 32:c + 40], small[:, c:c + 8], GDV, S["o_r"])
                for c in range(4):
                    act_.wait_ge(S["yT_mm"], c + 1)
                    act_.activation(y_hi[:, NH + c, :], pb[2 + c][:, :], ACT.Copy).then_inc(S["yT_hi"], 1)
                act_.wait_ge(S["mem_in"], 16 * MT)
                ahead(("mix", 1, 3))
                for m in range(MT):
                    link(act_.activation(junk[:, :], mem_tok[:, m, :], ACT.Square, accum_out=small[:, R_MEM + m:R_MEM + m + 1]))
                inverse_rms(small[:, R_MEM + 4:R_MEM + 6], small[:, R_MEM + 2:R_MEM + 4], small[:, R_MEM:R_MEM + 2], D, S["mem_r"])
                for k in range(KD):
                    act_.wait_ge(S["memT_mm"], k // 2 + 1)
                    act_.activation(m_hi[:, k, :], pb[4 + k // 2][:, (k % 2) * NM:(k % 2 + 1) * NM], ACT.Copy,
                                    scale=gain("norm_mem", k)).then_inc(S["m_hi_done"], 1)
                act_.wait_ge(S["mem_r"], 1)
                for half in range(2):
                    ahead(("ckv", half, 3))
                    for m in range(MT):
                        act_.wait_ge(S["ckv_mm"], MT * half + m + 1)
                        act_.activation(ckv_tok[:, m, half * HALF:(half + 1) * HALF], pb[2 * half + m][:, :], ACT.Copy,
                                        scale=small[:, R_MEM + 4 + m:R_MEM + 5 + m]).then_inc(S["ckv_evac"], 1)
                    if half == 0:
                        norm(1, "norm_ca", R_CA)
                act_.wait_ge(S["ck_ss"], 1)
                inverse_rms(small[:, R_CK + 16:R_CK + 24], small[:, R_CK + 8:R_CK + 16], small[:, R_CK:R_CK + 8], P, S["ck_r"])
                ahead(("caq", 3))
                act_.wait_ge(S["r_done"], 2)
                for t in range(NT):
                    act_.wait_ge(S["cq_mm"], t + 1)
                    act_.activation(cq_tok[:, t, :], pb[4 + t][:, :], ACT.Copy,
                                    scale=small[:, R_CA + 8 + t:R_CA + 9 + t]).then_inc(S["cq_evac"], 1)
                for t in range(NT):
                    c = R_CQ + 4 * t
                    act_.wait_ge(S["cq_ss"], t + 1)
                    inverse_rms(small[:, c + 32:c + 36], small[:, c + 16:c + 20], small[:, c:c + 4], P, S["cq_r"])
                for r in range(2):
                    act_.wait_ge(S["ckT_mm"], r + 1)
                    act_.activation(ckT[:, 2 * r:2 * r + 2, :], pb[r][:, :].rearrange("p (h q) -> p h q", h=2), ACT.Copy
                                    ).then_inc(S["ckT_evac"], 1)
                for t in range(NT):
                    act_.wait_ge(S["cqT_mm"], t + 1)
                    act_.activation(cqT[:, :, t * P:(t + 1) * P], pb[2 + t % 2][:, :].rearrange("p (h q) -> p h q", h=NH),
                                    ACT.Copy).then_inc(S["cqT_evac"], 1)
                attend(NH * NT, lambda t: NM, P ** -0.5, cprobsT, cprobs)
                ahead(("cao", 1, 1))
                norm(2, "norm_ffn", R_FFN)
                for g in range(FG):
                    for c in range(FCG):
                        n = g * FCG + c
                        ahead(("gate", g, c))
                        ahead(("up", g, c))
                        act_.wait_ge(S["silu_done"], 2 * n + 1)
                        act_.activation(conv_silu[n % 2][:, :], conv[n % 2][:, :], ACT.Silu).then_inc(S["silu_done"], 1)
                        act_.wait_ge(S["act_ready"], n + 1)
                        act_.activation(a_hi[:, c, :], act[n % 2][:, :], ACT.Copy).then_inc(S["a_hi_done"], 1)
                    ahead((("ffo", g), 1, FCG // 2))

            @block.vector
            def _(dve):
                link = chain(dve, S["chain_v"])

                def scaled(ap, n, col, like):
                    return small[:, col:col + n].unsqueeze(2).to_broadcast(like)

                def norm(w, name, r_col, n_spread):
                    for k in range(KD):
                        dve.wait_ge(S["x_hi_done"], w * KD + k + 1)
                        dve.scalar_tensor_tensor(x_lo[:, k, :], pb[4 + k % 4][:, :], gain(name, k), x_hi[:, k, :].bitcast(f32),
                                                 ALU.mult, ALU.subtract).then_inc(S["x_lo_done"], 1)
                    if n_spread is None:
                        return
                    dve.wait_ge(S["r_done"], w + 1)
                    dve.tensor_tensor(r_diag[:, :, :], ident[:, :].unsqueeze(1).to_broadcast([P, NT, P]),
                                      small[:, r_col + 8:r_col + 12].unsqueeze(2).to_broadcast([P, NT, P]),
                                      ALU.mult).then_inc(S["r_diag_done"], 1)
                    dve.wait_ge(S["r_mm"], n_spread + 1)
                    dve.tensor_copy(r_bc[:, :], pb[4][:, :]).then_inc(S["r_bc_done"], 1)
                    dve.wait_ge(S["r_bc_done"], n_spread + 1)

                def attend(base, n_keys, scale, causal, pr):
                    items = NH * NT
                    for i in range(items + 3):
                        if i < items:
                            hd, t = divmod(i, NT)
                            n = n_keys(t)
                            bank = pb[4 + i % 2]
                            c = ATT + base + i
                            dve.wait_ge(S["score_mm"], base + i + 1)
                            if causal:
                                link(dve.memset(bank[0:BLOCK, n - BLOCK:n], MASKED))
                            link(dve.reduce_max(small[:, c:c + 1], bank[:, 0:n], AX.X))
                            dve.tensor_scalar(small[:, c + 32:c + 33], small[:, c:c + 1], -scale, None, ALU.mult
                                              ).then_inc(S["score_max"], 1)
                        j = i - 1
                        if 0 <= j < items:
                            n = n_keys(j % NT)
                            c = ATT + base + j
                            dve.wait_ge(S["score_exp"], base + j + 1)
                            link(dve.reciprocal(small[:, c + 96:c + 97], small[:, c + 64:c + 65]))
                            dve.tensor_scalar(pr[j % 2][:, 0:n], pr[j % 2][:, 0:n], small[:, c + 96:c + 97], None, ALU.mult
                                              ).then_inc(S["probs_done"], 1)
                        j = i - 3
                        if 0 <= j < items and j % NT == NT - 1:
                            hd = j // NT
                            dve.wait_ge(S["pv_hi"], base // NT + hd + 1)
                            dve.tensor_tensor(x_lo[:, hd, :], pb[hd][:, :], x_hi[:, hd, :].bitcast(f32), ALU.subtract
                                              ).then_inc(S["pv_lo"], 1)

                def add_to_h(base):
                    for half in range(2):
                        for t in range(NT):
                            dve.wait_ge(S["proj_mm"], base + half * NT + t + 1)
                            c = slice(half * HALF, (half + 1) * HALF)
                            dve.tensor_tensor(h[:, t, c], h[:, t, c], pb[4 * half + t][:, :], ALU.add).then_inc(S["h_added"], 1)

                link(dve.tensor_scalar(lb_floor[:, :], lb_all[:, :, bass.ds(layer, 1)].squeeze(2), 1.0, None, ALU.mult))
                dve.tensor_scalar(lb_rest[:, :], lb_floor[:, :], -1.0, 1.0, ALU.mult, ALU.add)
                link(dve.memset(small[:, 519:520], 0.0))
                link(dve.tensor_scalar(lb_floor[:, :], lb_floor[:, :], LB_FLOOR, None, ALU.max))
                dve.wait_ge(S["gains_ready"], 1)
                norm(0, "norm_mix", R_MIX, 0)

                def lat_lo_part(n):
                    g_ = gain("mla_q_lat_norm", n) if n < 2 else gain("mla_kv_lat_norm", n - 2)
                    dve.wait_ge(S["lat_hi_done"], n + 1)
                    dve.scalar_tensor_tensor(lat_lo[:, n, :], lat[:, n, :], g_, lat_hi[:, n, :].bitcast(f32),
                                             ALU.mult, ALU.subtract).then_inc(S["lat_lo_done"], 1)

                for n in range(4):
                    dve.wait_ge(S["lat_mm"], n + 1)
                    dve.tensor_tensor(lat[:, n, :], pb[n][:, :], r_bc[:, :], ALU.mult).then_inc(S["lat_evac"], 1)
                    if n:
                        lat_lo_part(n - 1)
                lat_lo_part(3)
                dve.wait_ge(S["spread_in"], 16 * (1 + len(spread_of)))

                def prepare(z, t):
                    tok, name = (q_tok, "mla_q_norm") if z == 0 else (k_tok, "mla_k_norm")
                    nope, rope = nope_of(tok, t), rope_of(tok, t)
                    c = R_QK + 4 * (z * NT + t)
                    if z:
                        dve.wait_ge(S["k_evac"], t + 1)
                        dve.wait_ge(S["rope_evac"], t + 1)
                        link(dve.tensor_copy(rope, kr_tok[:, t, :].unsqueeze(1).unsqueeze(1).to_broadcast([P, 2, 2, ROPE])))
                    else:
                        dve.wait_ge(S["q_evac"], NT + t + 1)
                    for hd in range(NH):
                        for part, x, n in ((nope, 0, NOPE), (rope, NOPE, ROPE)):
                            head = part[:, hd // 2, hd % 2, :]
                            col = c + hd + (32 if x else 0)
                            last = dve.tensor_tensor_reduce(out=junk_v[:, hd, x:x + n], in0=head, in1=head, scale=1.0, scalar=0.0,
                                                            op0=ALU.mult, op1=ALU.add, accum_out=small[:, col:col + 1])
                    link(last)
                    dve.tensor_tensor(small[:, c + 64:c + 68], small[:, c:c + 4], small[:, c + 32:c + 36], ALU.add
                                      ).then_inc(S["qk_ss"], 1)
                    dve.wait_ge(S["qk_r"], z * NT + t + 1)
                    factor = small[:, c + 128:c + 132].rearrange("p (r h) -> p r h", r=2).unsqueeze(3)
                    dve.tensor_tensor(nope, nope, factor.to_broadcast([P, 2, 2, NOPE]), ALU.mult)
                    link(dve.tensor_tensor(rope, rope, factor.to_broadcast([P, 2, 2, ROPE]), ALU.mult))
                    g_ = spread_col(name).unsqueeze(1).unsqueeze(1)
                    dve.tensor_tensor(nope, nope, g_[:, :, :, 0:NOPE].to_broadcast([P, 2, 2, NOPE]), ALU.mult)
                    link(dve.tensor_tensor(rope, rope, g_[:, :, :, NOPE:QK].to_broadcast([P, 2, 2, ROPE]), ALU.mult))
                    R2_ = ROPE // 2
                    x1, x2 = rope[:, :, :, 0:R2_], rope[:, :, :, R2_:ROPE]
                    cs, sn = (a[:, t, :].unsqueeze(1).unsqueeze(1).to_broadcast([P, 2, 2, R2_]) for a in (cos, sin))
                    rot = r_diag[:, :, :].rearrange("p a (r h x) -> p a r h x", r=2, h=2)
                    dve.tensor_tensor(rot[:, 0], x1, cs, ALU.mult)
                    dve.tensor_tensor(rot[:, 1], x2, sn, ALU.mult)
                    dve.tensor_tensor(rot[:, 2], x2, cs, ALU.mult)
                    link(dve.tensor_tensor(rot[:, 3], x1, sn, ALU.mult))
                    dve.tensor_tensor(x1, rot[:, 0], rot[:, 1], ALU.subtract)
                    dve.tensor_tensor(x2, rot[:, 2], rot[:, 3], ALU.add).then_inc(S["qk_done"], 1)
                    dve.wait_ge(S["qk_done"], z * NT + t + 1)

                dests = [decay[:, 1, :], decay[:, 2, :], Q[:, 1, :], Q[:, 2, :], Q[:, 0, :], K[:, 0, :]]

                def feature(n):
                    dve.wait_ge(S["feat_mm"], n + 1)
                    dve.scalar_tensor_tensor(dests[n], pb[n % 4][:, :], GDK ** -0.5 if n == 4 else 1.0, r_bc[:, :],
                                             ALU.mult, ALU.mult).then_inc(S["feat_evac"], 1)

                prepare(0, 0)
                prepare(0, 1)
                feature(0)
                feature(1)
                prepare(0, 2)
                feature(2)
                prepare(0, 3)
                feature(3)
                prepare(1, 0)
                feature(4)
                prepare(1, 1)
                feature(5)
                prepare(1, 2)
                prepare(1, 3)
                dve.wait_ge(S["f_sig"], 1)
                for n in range(2):
                    r, fl = lb_rest[:, n:n + 1], lb_floor[:, n:n + 1]
                    dve.tensor_scalar(K[:, 1 + n, :], K[:, 1 + n, :], r, None, ALU.mult)
                    link(dve.tensor_scalar(decay[:, 1 + n, :], decay[:, 1 + n, :], r, fl, ALU.mult, ALU.add))
                    dve.tensor_scalar(decay[:, 1 + n, :], decay[:, 1 + n, :], 1.0, None, ALU.min)
                dve.wait_ge(S["feat_evac"], 6)
                dve.wait_ge(S["q_silu"], 1)
                link(dve.tensor_scalar(Q[:, 1:3, :], Q[:, 1:3, :], HDK ** -0.5, None, ALU.mult))
                dve.wait_ge(S["lr_t"], 1)
                dve.tensor_copy(lrT[:, :], pb[4][0:RANK, :]).then_inc(S["lr_evac"], 1)
                dve.wait_ge(S["gate_exp"], 1)
                link(dve.tensor_scalar(decay[:, 0, :], pb[5][:, :], gain("gla_b_gate", 0), 0.0, ALU.add, ALU.min))
                dve.tensor_tensor(decay[:, 0, :], decay[:, 0, :], gate_tmp[:, :], ALU.subtract).then_inc(S["gate_min"], 1)
                attend(0, lambda t: (t + 1) * P, QK ** -0.5, True, probs)
                dve.wait_ge(S["gate_done"], 1)
                dve.wait_ge(S["qkT_mm"], 4 * NT)
                dve.memset(state[:, 0, :], 0.0).then_inc(S["level_done"], 1)
                dve.memset(state[:, 1:, :], 0.0).then_inc(S["level_done"], 1)

                def next_level(li, f0, f1):
                    m = LEVELS[li]
                    if m == 0:
                        return dve.tensor_tensor(Q[:, f0:f1, :], Q[:, f0:f1, :], decay[:, f0:f1, :], ALU.mult)
                    nb = SEQ // (2 * m)
                    for f in range(f0, f1):
                        d = block_decay(m, slice(0, P), f).rearrange("p (b two) -> p b two", two=2)
                        q = Q[:, f, :].rearrange("p (b two m) -> p b two m", two=2, m=m)
                        k = K[:, f, :].rearrange("p (b two m) -> p b two m", two=2, m=m)
                        dve.tensor_tensor(q[:, :, 1, :], q[:, :, 1, :], d[:, :, 0:1].to_broadcast([P, nb, m]), ALU.mult)
                        dve.tensor_tensor(k[:, :, 0, :], k[:, :, 0, :], d[:, :, 1:2].to_broadcast([P, nb, m]), ALU.mult)
                        last = dve.tensor_tensor(block_decay(2 * m, slice(0, P), f), d[:, :, 0], d[:, :, 1], ALU.mult)
                    return last

                for li, m in enumerate(LEVELS):
                    for x in range(2):
                        dve.wait_ge(S["sweep_mm"], 2 * NH * li + NH * (x + 1))
                        next_level(li, *((0, 1) if x == 0 else (1, 3))).then_inc(S["level_done"], 1)
                        dve.wait_ge(S["level_done"], 2 * li + x + 3)
                        if m >= 16:
                            continue
                        sc = scores_g if x == 0 else scores_h
                        for hd in range(NH):
                            bank = pb[x * NH + hd][:, :].rearrange("p (n q) -> p n q", n=NT)
                            if m == 0:
                                cp = dve.tensor_tensor(sc[:, hd], bank, ident[:, :].unsqueeze(1).to_broadcast([P, NT, P]), ALU.mult)
                            else:
                                cp = dve.copy_predicated(sc[:, hd], pair_mask[m][:, :].unsqueeze(1).to_broadcast([P, NT, P]), bank)
                            cp.then_inc(S["swept_v"], 1)
                for n in range(NT - 1):
                    dve.wait_ge(S["u_mm"], n + 1)
                    for hh in range(2 * NH):
                        f, r0, dk = (0, GDK * hh, GDK) if hh < NH else (1 + (hh - NH) // 2, HDK * (hh % 2), HDK)
                        r, c = slice(r0, r0 + dk), slice(64 * hh, 64 * hh + 64)
                        u = pb[3 + n][r, c]
                        if n == 0:
                            st = dve.tensor_copy(state[r, n, c], u)
                        else:
                            st = dve.scalar_tensor_tensor(state[r, n, c], state[r, n - 1, c], block_decay(P, r, f)[:, n:n + 1],
                                                          u, ALU.mult, ALU.add)
                    st.then_inc(S["state_done"], 1)
                    dve.wait_ge(S["state_done"], n + 1)
                for n in range(NT):
                    c = R_O + 8 * n
                    o = o_tok[:, n, :].rearrange("p (h x) -> p h x", x=64)
                    sq = o_sq[:, :].rearrange("p (h x) -> p h x", x=64)
                    dve.wait_ge(S["o_evac"], n + 1)
                    link(dve.tensor_tensor(sq, o, o, ALU.mult))
                    dve.reduce_sum(small[:, c:c + 8], sq, AX.X).then_inc(S["o_ss"], 1)
                    dve.wait_ge(S["o_r"], n + 1)
                    link(dve.tensor_tensor(o, o, scaled(small, 8, c + 64, [P, 8, 64]), ALU.mult))
                    g0 = spread_of["gla_out_norm"][0]
                    link(dve.tensor_tensor(o_tok[:, n, :].rearrange("p (m h x) -> p m h x", m=2, x=64),
                                           o_tok[:, n, :].rearrange("p (m h x) -> p m h x", m=2, x=64),
                                           spread[:, g0:g0 + 128].rearrange("p (m x) -> p m x", m=2).unsqueeze(2)
                                           .to_broadcast([P, 2, NH, 64]), ALU.mult))
                    dve.tensor_tensor(o_tok[:, n, :], o_tok[:, n, :], sg_tok[:, n, :], ALU.mult).then_inc(S["o_done"], 1)
                for c in range(4):
                    dve.wait_ge(S["yT_hi"], c + 1)
                    dve.tensor_tensor(y_lo[:, NH + c, :], pb[2 + c][:, :], y_hi[:, NH + c, :].bitcast(f32), ALU.subtract
                                      ).then_inc(S["yT_lo"], 1)
                add_to_h(0)
                for k in range(KD):
                    dve.wait_ge(S["m_hi_done"], k // 2 * 2 + 2)
                    dve.scalar_tensor_tensor(m_lo[:, k, :], pb[4 + k // 2][:, (k % 2) * NM:(k % 2 + 1) * NM], gain("norm_mem", k),
                                             m_hi[:, k, :].bitcast(f32), ALU.mult, ALU.subtract).then_inc(S["m_lo_done"], 1)
                norm(1, "norm_ca", R_CA, None)
                dve.wait_ge(S["ckv_evac"], 2 * MT)
                keys = ckv_tok[:, :, :].rearrange("p m (h x) -> p m h x", h=NH)[:, :, :, 0:P]
                link(dve.tensor_tensor(ckv_sq[:, :, :, :], keys, keys, ALU.mult))
                dve.reduce_sum(small[:, R_CK:R_CK + 8], ckv_sq[:, :, :, :].rearrange("p m h x -> p (m h) x"), AX.X).then_inc(S["ck_ss"], 1)
                dve.wait_ge(S["ck_r"], 1)
                link(dve.tensor_tensor(keys, keys, small[:, R_CK + 16:R_CK + 24].rearrange("p (m h) -> p m h", m=MT).unsqueeze(3)
                                       .to_broadcast([P, MT, NH, P]), ALU.mult))
                dve.tensor_tensor(keys, keys, spread_col("ca_k_norm").unsqueeze(1).unsqueeze(1).to_broadcast([P, MT, NH, P]),
                                  ALU.mult).then_inc(S["ck_done"], 1)
                for t in range(NT):
                    c = R_CQ + 4 * t
                    q = cq_tok[:, t, :].rearrange("p (h x) -> p h x", h=NH)
                    sq = cq_sq[:, t, :].rearrange("p (h x) -> p h x", h=NH)
                    dve.wait_ge(S["cq_evac"], t + 1)
                    link(dve.tensor_tensor(sq, q, q, ALU.mult))
                    dve.reduce_sum(small[:, c:c + 4], sq, AX.X).then_inc(S["cq_ss"], 1)
                for t in range(NT):
                    c = R_CQ + 4 * t
                    q = cq_tok[:, t, :].rearrange("p (h x) -> p h x", h=NH)
                    dve.wait_ge(S["cq_r"], t + 1)
                    link(dve.tensor_tensor(q, q, scaled(small, NH, c + 32, [P, NH, P]), ALU.mult))
                    dve.tensor_tensor(q, q, spread_col("ca_q_norm").unsqueeze(1).to_broadcast([P, NH, P]), ALU.mult
                                      ).then_inc(S["cq_done"], 1)
                attend(NH * NT, lambda t: NM, P ** -0.5, False, cprobs)
                add_to_h(H_ADDS)
                for i in range(2):
                    dve.memset(gate_in[i][:, 0:CONV - 1], 0.0)
                norm(2, "norm_ffn", R_FFN, 1)
                for g in range(FG):
                    for c in range(FCG):
                        n = g * FCG + c
                        gi, cv = gate_in[n % 2], conv[n % 2]

                        def w_(t):
                            return gain("ffn_conv_w", t * FC + n)

                        dve.wait_ge(S["ffn_mm"], 2 * n + 1)
                        dve.tensor_tensor(gi[:, CONV - 1:], pb[2 * (n % 2)][:, :], r_bc[:, :], ALU.mult).then_inc(S["gate_ready"], 1)
                        dve.wait_ge(S["gate_ready"], n + 1)
                        link(dve.tensor_scalar(cv[:, :], gi[:, 0:SEQ], w_(0), gain("ffn_conv_b", n), ALU.mult, ALU.add))
                        for t in range(1, CONV - 1):
                            link(dve.scalar_tensor_tensor(cv[:, :], gi[:, t:t + SEQ], w_(t), cv[:, :], ALU.mult, ALU.add))
                        dve.scalar_tensor_tensor(cv[:, :], gi[:, CONV - 1:], w_(CONV - 1), cv[:, :], ALU.mult, ALU.add
                                                 ).then_inc(S["silu_done"], 1)
                        dve.wait_ge(S["ffn_mm"], 2 * n + 2)
                        link(dve.tensor_tensor(up_s[n % 2][:, :], pb[2 * (n % 2) + 1][:, :], r_bc[:, :], ALU.mult))
                        dve.wait_ge(S["silu_done"], 2 * n + 2)
                        dve.tensor_tensor(act[n % 2][:, :], conv_silu[n % 2][:, :], up_s[n % 2][:, :], ALU.mult).then_inc(S["act_ready"], 1)
                        dve.wait_ge(S["a_hi_done"], n + 1)
                        dve.tensor_tensor(a_lo[:, c, :], act[n % 2][:, :], a_hi[:, c, :].bitcast(f32), ALU.subtract
                                          ).then_inc(S["a_lo_done"], 1)
                    add_to_h((2 + g) * H_ADDS)

        clear_semaphores()
        layers.close()

        with nc.Block() as block:
            @block.sync
            def _(sp):
                for t in range(NT):
                    sp.dma_start(out[0, t * P:(t + 1) * P, :], h[:, t, :]).then_inc(stored, 16)
                sp.wait_ge(stored, 16 * NT)


_INS = ['x', 'mem', 'positions', 'norm_mix', 'w_in', 'mla_q_lat_norm', 'w_q_up', 'mla_kv_lat_norm', 'w_kv_up',
        'mla_q_norm', 'mla_k_norm', 'gla_w_gate', 'gla_b_gate', 'gla_out_norm', 'hgrn_lb_logits', 'hgrn_out_norm',
        'w_mix_out', 'norm_ca', 'norm_mem', 'w_ca_q', 'w_ca_kv', 'ca_q_norm', 'ca_k_norm', 'w_ca_out',
        'norm_ffn', 'w_ffn_in', 'ffn_conv_w', 'ffn_conv_b', 'w_ffn_out']


def kernel(**inputs):
    import numpy as np
    import concourse.bacc as bacc
    from concourse import mybir
    from concourse.bass_utils import run_bass_kernel_spmd

    nc = bacc.Bacc("TRN2", target_bir_lowering=False, num_devices=1)
    arrays, aps = {}, {}
    for name in _INS:
        a = np.ascontiguousarray(inputs[name])
        arrays[f"in_{name}"] = a
        aps[name] = nc.dram_tensor(f"in_{name}", a.shape, mybir.dt.from_np(a.dtype), kind="ExternalInput").ap()
    out = nc.dram_tensor("out_h", inputs['x'].shape, mybir.dt.float32, kind="ExternalOutput").ap()
    build_trunk(nc, aps, out)
    r = run_bass_kernel_spmd(nc, [arrays], core_ids=[0])
    return r.results[0]["out_h"]
```

```python
def build_trunk(nc, A, out):
    import concourse.bass as bass
    from concourse import mybir
    from contextlib import ExitStack
    import math
    import numpy as np

    f32, f32r, bf16 = mybir.dt.float32, mybir.dt.float32r, mybir.dt.bfloat16
    i32, u8 = mybir.dt.int32, mybir.dt.uint8
    ACT, ALU, AX = mybir.ActivationFunctionType, mybir.AluOpType, mybir.AxisListType

    P = 128
    DEPTH, D, P_IN = A["w_in"].shape
    SEQ = A["x"].shape[1]
    NM = A["mem"].shape[1]
    NT, KD, MT = SEQ // P, D // P, NM // P
    QL, KVL = A["w_q_up"].shape[1], A["w_kv_up"].shape[1]
    NH = 4
    NOPE = VD = P
    QK = A["w_q_up"].shape[2] // NH
    ROPE = QK - NOPE
    GDK, GDV = A["gla_w_gate"].shape[2] // NH, A["gla_out_norm"].shape[1]
    RANK = A["gla_w_gate"].shape[1]
    HDK, HDV = A["hgrn_lb_logits"].shape[1] // NH, A["hgrn_out_norm"].shape[1]
    DFF = A["w_ffn_out"].shape[1]
    CONV = A["ffn_conv_w"].shape[1]
    FC = DFF // P
    FG = 2
    FCG = FC // FG
    EPS, MASKED, TAU, THETA, LB_FLOOR, BLOCK = 1e-6, -1e30, 16.0, 10000.0, 1e-30, 64
    C_QL, C_KVL = 0, QL
    C_ROPE = C_KVL + KVL
    C_BQ = C_ROPE + ROPE
    C_BK = C_BQ + NH * GDK
    C_BV = C_BK + NH * GDK
    C_LR = C_BV + NH * GDV
    C_BR = C_LR + RANK
    C_CQ = C_BR + NH * GDV
    C_CF = C_CQ + NH * HDK
    C_CI = C_CF + NH * HDK
    C_CG = C_CI + NH * HDV
    HALF = D // 2
    VG = NH * GDV + RANK

    rows_of, at = {}, 0
    for name, n in (("norm_mix", KD), ("mla_q_lat_norm", QL // P), ("mla_kv_lat_norm", KVL // P),
                    ("gla_b_gate", 1), ("norm_ca", KD), ("norm_mem", KD), ("norm_ffn", KD),
                    ("ffn_conv_w", CONV * FC), ("ffn_conv_b", FC)):
        rows_of[name] = (at, n)
        at += n
    ROWS = at
    spread_of, at = {}, 0
    for name, n in (("mla_q_norm", QK), ("mla_k_norm", QK), ("gla_out_norm", GDV), ("hgrn_out_norm", HDV),
                    ("ca_q_norm", P), ("ca_k_norm", P)):
        spread_of[name] = (at, n)
        at += n
    SPREAD = at

    slabs, slab_at = [], {}

    def slab(name, nk, cols, src):
        slab_at[name] = len(slabs)
        slabs.append((nk, cols, src))

    def cut(w, k0, nk, c0, cols):
        def parts(l, dst):
            yield (dst[:, 0:nk * cols].rearrange("p (k c) -> p k c", k=nk),
                   w[l, k0 * P:(k0 + nk) * P, c0:c0 + cols].rearrange("(k p) c -> p k c", p=P))
        return parts

    for n in range(4):
        slab(("lat", n), KD, P, cut(A["w_in"], 0, KD, n * P, P))
    slab("rope", KD, ROPE, cut(A["w_in"], 0, KD, C_ROPE, ROPE))
    FEATS = [C_CF, C_CF + P, C_CQ, C_CQ + P, C_BQ, C_BK]
    slab(("feat", 0), KD, P, cut(A["w_in"], 0, KD, FEATS[0], P))
    PAIR = 2 * QK

    def q_up_parts(n):
        def parts(l, dst):
            for k in range(2):
                src = A["w_q_up"][l, k * P:(k + 1) * P, n * PAIR:(n + 1) * PAIR].rearrange("p (h x) -> p h x", h=2)
                for x0, x1 in ((0, NOPE), (NOPE, QK)):
                    d = dst[:, k * PAIR + 2 * x0:k * PAIR + 2 * x1].rearrange("p (h x) -> p h x", h=2)
                    yield d, src[:, :, x0:x1]
        return parts

    def kv_up_parts(n):
        def parts(l, dst):
            for k in range(2):
                src = A["w_kv_up"][l, k * P:(k + 1) * P].rearrange("p (h x) -> p h x", h=NH)
                yield (dst[:, k * NH * P:(k + 1) * NH * P].rearrange("p (h x) -> p h x", h=NH),
                       src[:, :, n * P:(n + 1) * P])
        return parts

    for n in range(2):
        slab(("q_up", n), 2, PAIR, q_up_parts(n))
    for n in range(2):
        slab(("kv_up", n), 2, NH * P, kv_up_parts(n))
    for n, c in enumerate(FEATS[1:]):
        slab(("feat", n + 1), KD, P, cut(A["w_in"], 0, KD, c, P))
    TOKS = {"vg": (C_BV, VG, (3, 3, 2)), "br": (C_BR, NH * GDV, (4, 4)),
            "cig": (C_CI, NH * HDV * 2, (2, 2, 2, 2))}
    for name, (c, cols, ks) in TOKS.items():
        for n, nk in enumerate(ks):
            slab((name, n), nk, cols, cut(A["w_in"], sum(ks[:n]), nk, c, cols))

    def half_of(name, w, nk_all, half, k0=0):
        for n in range((nk_all + 1) // 2):
            nk = min(2, nk_all - 2 * n)
            slab((name, half, n), nk, HALF, cut(w, k0 + 2 * n, nk, half * HALF, HALF))

    for half in range(2):
        half_of("mix", A["w_mix_out"], KD, half)
    half_of("ckv", A["w_ca_kv"], KD, 0)
    for n in range(KD // 2):
        slab(("caq", n), 2, NH * P, cut(A["w_ca_q"], 2 * n, 2, 0, NH * P))
    half_of("ckv", A["w_ca_kv"], KD, 1)
    for half in range(2):
        half_of("cao", A["w_ca_out"], NH, half)
    for g in range(FG):
        for c in range(FCG):
            slab(("gate", g, c), KD, P, cut(A["w_ffn_in"], 0, KD, (g * FCG + c) * P, P))
            slab(("up", g, c), KD, P, cut(A["w_ffn_in"], 0, KD, DFF + (g * FCG + c) * P, P))
        for half in range(2):
            half_of(("ffo", g), A["w_ffn_out"], FCG, half, k0=g * FCG)
    NS = len(slabs)
    RAW, SPLIT, SLAB = 3, 3, 1024

    with ExitStack() as ctx:
        def sb(name, shape, dt=f32):
            return ctx.enter_context(nc.sbuf_tensor(name, shape, dt))

        h = sb("h", [P, NT, D])
        raw = [sb(f"raw{i}", [P, SLAB]) for i in range(RAW)]
        w_hi = [sb(f"w_hi{i}", [P, SLAB], f32r) for i in range(SPLIT)]
        w_lo = [sb(f"w_lo{i}", [P, SLAB], f32r) for i in range(SPLIT)]
        ident = sb("ident", [P, P])
        ones = sb("ones", [P, P])
        pair_mask = {m: sb(f"pair_mask{m}", [P, P], u8) for m in (1, 2, 4, 8)}
        cos, sin = sb("cos", [P, NT, ROPE // 2]), sb("sin", [P, NT, ROPE // 2])
        eps_c = sb("eps_c", [P, 1])
        bounds = sb("bounds", [P, 2 * DEPTH + 4])
        lb_all = bounds[:, 0:2 * DEPTH].rearrange("p (c l) -> p c l", l=DEPTH)
        lb_floor, lb_rest = bounds[:, 2 * DEPTH:2 * DEPTH + 2], bounds[:, 2 * DEPTH + 2:2 * DEPTH + 4]
        gains_all = sb("gains_all", [P, DEPTH, ROWS])
        gains = sb("gains", [P, ROWS])
        spread = sb("spread", [P, SPREAD])
        w_gate = sb("w_gate", [RANK, NH * GDK])
        r_bc = sb("r_bc", [P, SEQ])
        r_diag = sb("r_diag", [P, NT, P])
        kr_tok = sb("kr_tok", [P, NT, ROPE])
        small = sb("small", [P, 516])

        KB = 1024
        ARENA = 141 * KB + 256
        arena = sb("arena", [P, ARENA // 4])
        base = nc.sbuf_base - ARENA

        def place(name, kb, shape, dt=f32):
            size = 4 * int(np.prod(shape[1:]))
            assert int(kb * KB) + size <= ARENA, name
            return nc.alloc_sbuf_tensor_at(name, shape, dt, offset=base + int(kb * KB))

        x_hi = place("x_hi", 0, [P, KD, SEQ], f32r)
        x_lo = place("x_lo", 16, [P, KD, SEQ], f32r)
        y_hi, y_lo = x_hi, x_lo
        scores_g = place("scores_g", 8, [P, NT, NH, P])
        scores_h = place("scores_h", 24, [P, NT, NH, P])
        R0, R1, R2, R3, R4, R5, R6 = 32, 48, 72, 80, 104, 125, 141.25
        lat_hi = place("lat_hi", R0, [P, 4, SEQ], f32r)
        lat_lo = place("lat_lo", R0 + 8, [P, 4, SEQ], f32r)
        probsT = place("probsT", R0, [P, NT, SEQ])
        probs = [place(f"probs{i}", R0 + 8 + 2 * i, [P, SEQ]) for i in range(2)]
        lrT = place("lrT", R0 + 12, [RANK, SEQ])
        gate_tmp = place("gate_tmp", R0 + 14, [P, SEQ])
        lat = place("lat", R1, [P, 4, SEQ])
        lat_sq = place("lat_sq", R1 + 8, [P, 4, SEQ])
        qT_n, kT_n = place("qT_n", R1, [P, NH, SEQ]), place("kT_n", R1 + 8, [P, NH, SEQ])
        qT_r = place("qT_r", R1 + 16, [P, NH, SEQ])
        kT_r = place("kT_r", R3, [P, 2, SEQ])
        v_tok = place("v_tok", R2, [P, NT, NH * VD])
        q_tok, k_tok = place("q_tok", R3, [P, NT, NH * QK]), place("k_tok", R3 + 12, [P, NT, NH * QK])
        Qx = [place(f"Qx{x}", R3 + 4 + 8 * x, [P, NH, SEQ]) for x in range(2)]
        o_tok = place("o_tok", R1, [P, NT, 512])
        k_hat = place("k_hat", R1 + 8, [P, 3, NT, P])
        state = place("state", R1 + 14, [P, NT - 1, 512])
        o_sq = place("o_sq", R1 + 20, [P, 512])
        Q, K = place("Q", R4, [P, 3, SEQ]), place("K", R4 + 6, [P, 3, SEQ])
        decay = place("decay", R4 + 12, [P, 3, SEQ])
        decay_m = place("decay_m", R4 + 18, [P, 3, SEQ // 2])
        vg_tok = place("vg_tok", R5, [P, NT, VG])
        ci_tok = place("ci_tok", R5 + 4.25, [P, NT, NH * HDV])
        sg_tok = place("sg_tok", R5 + 8.25, [P, NT, 512])
        mem_tok = place("mem_tok", R0, [P, MT, D])
        m_hi, m_lo = place("m_hi", R1, [P, KD, NM], f32r), place("m_lo", R1 + 8, [P, KD, NM], f32r)
        ckv_tok = place("ckv_tok", R2, [P, MT, D])
        ckv_sq = place("ckv_sq", R3, [P, MT, NH, P])
        ckT = place("ckT", R3 + 4, [P, NH, NM])
        cq_tok = place("cq_tok", R3 + 8, [P, NT, NH * P])
        cqT = place("cqT", R3 + 16, [P, NH, SEQ])
        cq_sq = place("cq_sq", R4, [P, NT, NH * P])
        cprobsT = place("cprobsT", R4 + 8, [P, MT, SEQ])
        cprobs = [place(f"cprobs{i}", R4 + 12 + 2 * i, [P, SEQ]) for i in range(2)]
        a_hi = place("a_hi", 32, [P, FCG, SEQ], f32r)
        a_lo = place("a_lo", 54, [P, FCG, SEQ], f32r)
        gate_in = [place(f"gate_in{i}", 76 + 2.25 * i, [P, CONV - 1 + SEQ]) for i in range(2)]
        conv = [place(f"conv{i}", 81 + 2 * i, [P, SEQ]) for i in range(2)]
        conv_silu = [place(f"conv_silu{i}", 85 + 2 * i, [P, SEQ]) for i in range(2)]
        up_s = [place(f"up_s{i}", 89 + 2 * i, [P, SEQ]) for i in range(2)]
        act = [place(f"act{i}", 93 + 2 * i, [P, SEQ]) for i in range(2)]
        rows = [place(f"rows{l}", 20 + l, [P, P]) for l in range(DEPTH)]
        junk = place("junk", R5 + 8.25, [P, D], bf16)
        junk_v = place("junk_v", R5 + 4.25, [P, NH, QK], bf16)
        lb_rows = place("lb_rows", 0, [DEPTH * 2, P])
        lb_t = place("lb_t", 1, [P, 8, 2, DEPTH])
        pos_i = place("pos_i", 2, [P, NT], i32)
        pos_f = place("pos_f", 3, [P, NT])
        ang = place("ang", 4, [P, NT, ROPE // 2])
        turns_i = place("turns_i", 5, [P, NT, ROPE // 2], i32)
        turns = place("turns", 6, [P, NT, ROPE // 2])
        over = place("over", 7, [P, NT, ROPE // 2])
        freq = place("freq", 8, [P, ROPE // 2])
        idx_i, idx_j = place("idx_i", 9, [P, P], i32), place("idx_j", 10, [P, P], i32)
        mk = [place(f"mk{i}", 11 + i, [P, P], i32) for i in range(3)]

        pb = [ctx.enter_context(nc.psum_tensor(f"bank{i}", [P, 512], f32)) for i in range(8)]

        names = """lo_split hi_split slab_used vectors_in spread_in mem_in rows_t gains_ready chain_v chain_a
            hT_mm x_hi_done x_lo_done ss_done r_done r_diag_done r_mm r_bc_done
            lat_mm lat_evac lat_sq_done lat_hi_done lat_lo_done lat_ss_mm r_lat_done
            rope_mm rope_evac q_mm q_evac k_mm k_evac v_mm v_evac qk_ss qk_r qk_done qkT_mm qkT_evac
            feat_mm feat_evac f_sig q_silu tok_mm tok_evac lr_t lr_evac gate_mm gate_exp gate_min gate_done
            score_mm score_max score_exp probs_done probsT_mm probsT_evac pv_mm pv_hi pv_lo
            sweep_mm swept_v swept_a level_done khat_t khat_evac u_mm state_done o_mm o_evac o_ss o_r o_done yT_mm yT_hi yT_lo
            proj_mm h_added mem_ss mem_r memT_mm m_hi_done m_lo_done ckv_mm ckv_evac ck_ss ck_r ck_done ckT_mm ckT_evac
            cq_mm cq_evac cq_ss cq_r cq_done cqT_mm cqT_evac
            ffn_mm gate_ready silu_done act_ready a_hi_done a_lo_done set_up lbT zeroed qx_done q_scaled""".split()
        S = {n: ctx.enter_context(nc.semaphore(n)) for n in names}
        raw_in = [ctx.enter_context(nc.semaphore(f"raw_in{i}")) for i in range(RAW)]
        every_sem = [S[n] for n in names] + raw_in
        x_in = ctx.enter_context(nc.semaphore("x_in"))
        stored = ctx.enter_context(nc.semaphore("stored"))

        def gain(name, n):
            c = rows_of[name][0] + n
            return gains[:, c:c + 1]

        def spread_col(name):
            c, n = spread_of[name]
            return spread[:, c:c + n]

        def nope_of(tok, t):
            return tok[:, t, :].rearrange("p (r y) -> p r y", r=2)[:, :, 0:2 * NOPE].rearrange("p r (h x) -> p r h x", h=2)

        def rope_of(tok, t):
            return tok[:, t, :].rearrange("p (r y) -> p r y", r=2)[:, :, 2 * NOPE:PAIR].rearrange("p r (h x) -> p r h x", h=2)

        def chain(eng, sem):
            count = [0]

            def link(ins):
                count[0] += 1
                ins.then_inc(sem, 1)
                eng.wait_ge(sem, count[0])
            return link

        with nc.Block() as block:
            @block.sync
            def _(sp):
                for t in range(NT):
                    sp.dma_start(h[:, t, :], A["x"][0, t * P:(t + 1) * P, :]).then_inc(x_in, 16)
                sp.dma_start(pos_i[:, :], A["positions"][0].rearrange("(t p) -> p t", p=P),
                             allow_slow_non_contiguous=True).then_inc(S["mem_in"], 16)
                sp.dma_start(lb_rows[:, :], A["hgrn_lb_logits"].rearrange("l (c p) -> (l c) p", p=P)
                             ).then_inc(S["vectors_in"], 16)
                for l in range(DEPTH):
                    for name, (r0, n) in rows_of.items():
                        src = A[name][l]
                        src = src.rearrange("t (c p) -> (t c) p", p=P) if len(src.shape) == 2 else \
                            src.rearrange("(c p) -> c p", p=P)
                        sp.dma_start(rows[l][r0:r0 + n, :], src).then_inc(S["spread_in"], 16)
                sp.wait_ge(x_in, 16 * NT)

            @block.gpsimd
            def _(pool):
                pool.memset(ident[:, :], 0.0).then_inc(S["chain_v"], 1)
                pool.iota(idx_i[:, :], pattern=[[1, P]], base=0, channel_multiplier=0).then_inc(S["feat_mm"], 1)
                pool.iota(idx_j[:, :], pattern=[[0, P]], base=0, channel_multiplier=1).then_inc(S["feat_mm"], 1)
                pool.wait_ge(S["chain_v"], 1)
                pool.affine_select(out=ident[:, :], in_=ident[:, :], compare_op=ALU.not_equal, fill=1.0,
                                   base=0, pattern=[[-1, P]], channel_multiplier=1).then_inc(S["set_up"], 1)

            @block.tensor
            def _(pe):
                pe.wait_ge(S["set_up"], 1)
                pe.wait_ge(S["vectors_in"], 16)
                pe.transpose(pb[0][:, 0:2 * DEPTH], lb_rows[:, :], ident[0:2 * DEPTH, 0:2 * DEPTH]
                             ).then_inc(S["lbT"], 1)
                pe.wait_ge(S["spread_in"], 16 * DEPTH * len(rows_of))
                for l in range(DEPTH):
                    pe.transpose(pb[1 + l][:, 0:ROWS], rows[l][0:ROWS, :], ident[0:ROWS, 0:ROWS]).then_inc(S["rows_t"], 1)

            @block.scalar
            def _(eng):
                for l in range(DEPTH):
                    eng.wait_ge(S["rows_t"], l + 1)
                    eng.activation(gains_all[:, l, :], pb[1 + l][:, 0:ROWS], ACT.Copy)
                eng.wait_ge(S["gate_min"], 1)
                eng.activation(lb_t[:, 2], lb_t[:, 1], ACT.Exp).then_inc(S["gate_exp"], 1)
                eng.wait_ge(S["gate_done"], 1)
                eng.activation(sin[:, :, :], ang[:, :, :], ACT.Sin).then_inc(S["r_done"], 1)
                eng.wait_ge(S["gate_done"], 2)
                eng.activation(cos[:, :, :], turns[:, :, :], ACT.Sin).then_inc(S["r_done"], 1)

            @block.vector
            def _(dve):
                link = chain(dve, S["chain_a"])
                dve.memset(ones[:, :], 1.0)
                dve.memset(eps_c[:, :], EPS)
                inv = (np.float32(THETA) ** (-np.arange(0, ROPE, 2, dtype=np.float32) / np.float32(ROPE))).astype(np.float32)
                for j in range(ROPE // 2 - 1):
                    dve.memset(freq[:, j:j + 1], float(inv[j]))
                link(dve.memset(freq[:, ROPE // 2 - 1:ROPE // 2], float(inv[-1])))
                dve.wait_ge(S["feat_mm"], 2)
                for m, mask in pair_mask.items():
                    s = m.bit_length() - 1
                    dve.tensor_scalar(mk[0][:, :], idx_i[:, :], s, None, ALU.logical_shift_right)
                    link(dve.tensor_scalar(mk[1][:, :], idx_j[:, :], s, None, ALU.logical_shift_right))
                    link(dve.tensor_tensor(mk[2][:, :], mk[0][:, :], mk[1][:, :], ALU.subtract))
                    link(dve.tensor_scalar(mk[1][:, :], mk[2][:, :], 1.0, None, ALU.is_equal))
                    link(dve.tensor_scalar(mk[2][:, :], idx_i[:, :], s, 1, ALU.logical_shift_right, ALU.bitwise_and))
                    link(dve.tensor_tensor(mask[:, :], mk[1][:, :], mk[2][:, :], ALU.mult))
                dve.wait_ge(S["lbT"], 1)
                link(dve.tensor_copy(lb_t[:, 0], pb[0][:, 0:2 * DEPTH].rearrange("p (l c) -> p c l", c=2)))
                link(dve.reduce_max(lb_t[:, 3, :, 0:1], lb_t[:, 0], AX.X))
                dve.tensor_tensor(lb_t[:, 1], lb_t[:, 0], lb_t[:, 3, :, 0:1].to_broadcast([P, 2, DEPTH]),
                                  ALU.subtract).then_inc(S["gate_min"], 1)
                dve.wait_ge(S["gate_exp"], 1)
                link(dve.reduce_sum(lb_t[:, 4, :, 0:1], lb_t[:, 2], AX.X))
                link(dve.reciprocal(lb_t[:, 5, :, 0:1], lb_t[:, 4, :, 0:1]))
                link(dve.tensor_tensor(lb_t[:, 6], lb_t[:, 2], lb_t[:, 5, :, 0:1].to_broadcast([P, 2, DEPTH]), ALU.mult))
                link(dve.tensor_copy(lb_t[:, 7, :, 0:1], lb_t[:, 6, :, 0:1]))
                for l in range(1, DEPTH):
                    link(dve.tensor_tensor(lb_t[:, 7, :, l:l + 1], lb_t[:, 7, :, l - 1:l], lb_t[:, 6, :, l:l + 1], ALU.add))
                link(dve.tensor_tensor(lb_all[:, :, :], lb_t[:, 7], lb_t[:, 6, :, 0:1].to_broadcast([P, 2, DEPTH]),
                                       ALU.subtract))
                dve.wait_ge(S["mem_in"], 16)
                link(dve.tensor_copy(pos_f[:, :], pos_i[:, :]))
                link(dve.tensor_tensor(ang[:, :, :], pos_f[:, :].unsqueeze(2).to_broadcast([P, NT, ROPE // 2]),
                                       freq[:, :].unsqueeze(1).to_broadcast([P, NT, ROPE // 2]), ALU.mult))
                link(dve.tensor_scalar(turns_i[:, :, :], ang[:, :, :], 1 / (2 * math.pi), None, ALU.mult))
                link(dve.tensor_copy(turns[:, :, :], turns_i[:, :, :]))
                c1 = 6.28125
                c2 = float(np.float32(math.floor((2 * math.pi - c1) * 2 ** 20) / 2 ** 20))
                c3 = 2 * math.pi - c1 - c2
                for c in (c1, c2, c3):
                    link(dve.scalar_tensor_tensor(ang[:, :, :], turns[:, :, :], -c, ang[:, :, :], ALU.mult, ALU.add))

                def wrap(a):
                    for cmp, lim, turn in ((ALU.is_gt, math.pi, -2 * math.pi), (ALU.is_lt, -math.pi, 2 * math.pi)):
                        link(dve.tensor_scalar(over[:, :, :], a, lim, turn, cmp, ALU.mult))
                        link(dve.tensor_tensor(a, a, over[:, :, :], ALU.add))

                wrap(ang[:, :, :])
                link(dve.tensor_scalar(turns[:, :, :], ang[:, :, :], math.pi / 2, None, ALU.add))
                wrap(turns[:, :, :])
                bound = float(np.nextafter(np.float32(math.pi), np.float32(0)))
                dve.tensor_scalar(ang[:, :, :], ang[:, :, :], bound, -bound, ALU.min, ALU.max).then_inc(S["gate_done"], 1)
                dve.tensor_scalar(turns[:, :, :], turns[:, :, :], bound, -bound, ALU.min, ALU.max).then_inc(S["gate_done"], 1)
                dve.wait_ge(S["r_done"], 2)

        def clear_semaphores():
            nc.all_engine_barrier()
            nums = sorted(s.num for s in every_sem)
            assert nums == list(range(nums[0], nums[0] + len(nums)))
            nc.gpsimd.sem_clear(range(nums[0], nums[-1] + 1))
            nc.all_engine_barrier()

        clear_semaphores()

        MLA_GROUPS, CA_GROUPS = ((0, 1), (2,), (3,)), ((0, 1), (2, 3))
        MLA_ITEMS = NH * len(MLA_GROUPS)
        H_ADDS = 2 * NT
        ATT, R_MIX, R_CA, R_FFN, R_LAT, R_MEM = 0, 128, 140, 152, 164, 180
        R_CK, R_CQ = 186, 210
        R_QK, R_O = 260, 420
        LEVELS = (0, 1, 2, 4, 8, 16, 32, 64)

        def block_decay(m, rows_, f):
            buf = decay if m.bit_length() % 2 else decay_m
            return buf[rows_, f, 0:SEQ // m]

        layers = ctx.enter_context(ExitStack())
        layer = layers.enter_context(nc.Fori(0, DEPTH))
        with nc.Block() as block:

            arrivals, total = [], [0] * RAW

            @block.sync
            def _(sp):
                for i, (nk, cols, src) in enumerate(slabs):
                    if i == slab_at["q_up", 0]:
                        sp.dma_start(w_gate[:, :], A["gla_w_gate"][layer]).then_inc(S["spread_in"], 16)
                        for name, (c, n) in spread_of.items():
                            sp.dma_start(spread[:, c:c + n], A[name][layer].partition_broadcast(P)
                                         ).then_inc(S["spread_in"], 16)
                    if i == slab_at["mix", 1, 0]:
                        sp.wait_ge(S["pv_mm"], NH)
                        sp.wait_ge(S["gate_done"], 1)
                        sp.wait_ge(S["probsT_mm"], MLA_ITEMS)
                        for m in range(MT):
                            sp.dma_start(mem_tok[:, m, :], A["mem"][0, m * P:(m + 1) * P, :]).then_inc(S["mem_in"], 16)
                    if i >= RAW:
                        sp.wait_ge(S["lo_split"], i - RAW + 1)
                    for dst, part in src(layer, raw[i % RAW]):
                        sp.dma_start(dst, part).then_inc(raw_in[i % RAW], 16)
                        total[i % RAW] += 16
                    arrivals.append(total[i % RAW])

            @block.gpsimd
            def _(pool):
                for i, (nk, cols, _) in enumerate(slabs):
                    n = nk * cols
                    pool.wait_ge(S["hi_split"], i + 1)
                    pool.tensor_tensor(w_lo[i % SPLIT][:, 0:n], raw[i % RAW][:, 0:n],
                                       w_hi[i % SPLIT][:, 0:n].bitcast(f32), ALU.subtract).then_inc(S["lo_split"], 1)
                    if i == SPLIT - 1:
                        for half in range(2):
                            pool.memset(qT_r[:, 2 * half:2 * half + 2, :], 0.0).then_inc(S["zeroed"], 1)
                    if i == slab_at["mix", 0, 1]:
                        pool.wait_ge(S["qkT_mm"], 4 * NT)
                        for x in range(2):
                            pool.memset(Qx[x][:, :, :], 0.0).then_inc(S["zeroed"], 1)

            released = {}

            @block.tensor
            def _(pe):
                freed, count = {}, {}

                def mark(ins, sem):
                    ins.then_inc(sem, 1)
                    count[id(sem)] = count.get(id(sem), 0) + 1
                    return sem, count[id(sem)]

                def claim(b):
                    if b in freed:
                        pe.wait_ge(*freed[b])

                def use(name):
                    i = slab_at[name]
                    nk, cols, _ = slabs[i]
                    pe.wait_ge(S["lo_split"], i + 1)
                    return [w[i % SPLIT][:, 0:nk * cols].rearrange("p (k c) -> p k c", k=nk) for w in (w_hi, w_lo)]

                def product(o, a, b, first, last):
                    (ah, al), (bh, bl) = a, b
                    pe.matmul(o, ah, bh, start=first, stop=False)
                    pe.matmul(o, ah, bl, start=False, stop=False)
                    return pe.matmul(o, al, bh, start=False, stop=last)

                def transpose_h(w, ks):
                    if w:
                        pe.wait_ge(S["h_added"], H_ADDS * w)
                    for k in ks:
                        b = 4 + k % 4
                        claim(b)
                        for t in range(NT):
                            mm = pe.transpose(pb[b][:, t * P:(t + 1) * P], h[:, t, k * P:(k + 1) * P], ident[:, :])
                        mark(mm, S["hT_mm"])
                        freed[b] = (S["x_lo_done"], w * KD + k + 1)

                def spread_r(n):
                    claim(4)
                    pe.wait_ge(S["r_diag_done"], n + 1)
                    mark(pe.matmul(pb[4][:, :], ones[:, :], r_diag[:, :, :].rearrange("p t c -> p (t c)"),
                                   start=True, stop=True), S["r_mm"])
                    freed[4] = (S["r_bc_done"], n + 1)

                def feature_chunk(name, b, w, done, evac):
                    claim(b)
                    wh, wl = use(name)
                    for k in range(KD):
                        pe.wait_ge(S["x_lo_done"], w * KD + k + 1)
                        mm = product(pb[b][:, :], (wh[:, k, :], wl[:, k, :]), (x_hi[:, k, :], x_lo[:, k, :]),
                                     k == 0, k == KD - 1)
                    released[slab_at[name]] = mark(mm, done)
                    freed[b] = evac

                def token_group(names, b0, cols, x, k0, ready, done, evac, nt=NT):
                    xh, xl = x
                    nk_all = sum(slabs[slab_at[n]][0] for n in names)
                    k = 0
                    for n in names:
                        wh, wl = use(n)
                        for kk in range(slabs[slab_at[n]][0]):
                            if ready is not None:
                                pe.wait_ge(*ready(k))
                            for t in range(nt):
                                if k == 0:
                                    claim(b0 + t)
                                mm = product(pb[b0 + t][:, 0:cols],
                                             (xh[:, k0 + k, t * P:(t + 1) * P], xl[:, k0 + k, t * P:(t + 1) * P]),
                                             (wh[:, kk, :], wl[:, kk, :]), k == 0, k == nk_all - 1)
                                if k == nk_all - 1:
                                    last = mark(mm, done)
                            k += 1
                        released[slab_at[n]] = last if k == nk_all else mark(mm, S["slab_used"])
                    for t in range(nt):
                        freed[b0 + t] = (evac[0], evac[1] + t + 1)

                def attend(base, groups, score, n_keys, q_from, values, pT, pr):
                    n_groups = len(groups)
                    items = NH * n_groups
                    for i in range(items + 3):
                        if i < items:
                            hd, b = i // n_groups, 4 + i % 2
                            claim(b)
                            c = 0
                            for t in groups[i % n_groups]:
                                n = n_keys(t)
                                mm = score(pb[b][:, c:c + n], hd, t, n)
                                c += n
                            mark(mm, S["score_mm"])
                            freed[b] = (S["score_exp"], base + i + 1)
                        j = i - 2
                        if 0 <= j < items:
                            b = 6 + j % 2
                            claim(b)
                            pe.wait_ge(S["probs_done"], base + j + 1)
                            for c in range(0, sum(n_keys(t) for t in groups[j % n_groups]), P):
                                mm = pe.transpose(pb[b][:, c:c + P], pr[j % 2][:, c:c + P], ident[:, :])
                            mark(mm, S["probsT_mm"])
                            freed[b] = (S["probsT_evac"], base + j + 1)
                        j = i - 3
                        if 0 <= j < items and j % n_groups == n_groups - 1:
                            hd = j // n_groups
                            claim(hd)
                            pe.wait_ge(S["probsT_evac"], base + j + 1)
                            n_blocks = n_keys(NT - 1) // P
                            for n in range(n_blocks):
                                q0 = q_from(n)
                                mm = pe.matmul(pb[hd][:, q0:SEQ], values(n, hd), pT[:, n, q0:SEQ],
                                               start=(n == 0), stop=(n == n_blocks - 1))
                            mark(mm, S["pv_mm"])
                            freed[hd] = (S["pv_lo"], base // MLA_ITEMS * NH + hd + 1)

                transpose_h(0, range(KD))
                for n in range(4):
                    feature_chunk(("lat", n), n, 0, S["lat_mm"], (S["lat_evac"], n + 1))
                    if n == 0:
                        spread_r(0)
                X = (x_hi, x_lo)
                token_group(["rope"], 4, ROPE, X, 0, None, S["rope_mm"], (S["rope_evac"], 0))
                feature_chunk(("feat", 0), 0, 0, S["feat_mm"], (S["feat_evac"], 1))
                claim(1)
                pe.wait_ge(S["lat_sq_done"], 4)
                for n in range(2):
                    for t in range(NT):
                        for c in range(2):
                            mm = pe.matmul(pb[1][:, n * NT + t:n * NT + t + 1], lat_sq[:, 2 * n + c, t * P:(t + 1) * P],
                                           ones[:, 0:1], start=(c == 0), stop=(c == 1))
                mark(mm, S["lat_ss_mm"])
                freed[1] = (S["r_lat_done"], 1)
                L = (lat_hi, lat_lo)
                for n in range(2):
                    token_group([("q_up", n)], 4 * n, 2 * QK, L, 0, lambda k: (S["lat_lo_done"], k + 1),
                                S["q_mm"], (S["q_evac"], NT * n))
                token_group([("kv_up", 0)], 0, NH * P, L, 2, lambda k: (S["lat_lo_done"], k + 3), S["k_mm"], (S["k_evac"], 0))
                token_group([("kv_up", 1)], 4, NH * P, L, 2, None, S["v_mm"], (S["v_evac"], 0))
                for n in range(1, len(FEATS)):
                    feature_chunk(("feat", n), n % 4, 0, S["feat_mm"], (S["feat_evac"], n + 1))

                def transpose_qk(z, src):
                    for t in range(NT):
                        pe.wait_ge(S["qk_done"], z * NT + t + 1)
                        b = 2 * (t % 2)
                        claim(b)
                        for hd in range(NH):
                            mm = pe.transpose(pb[b][:, hd * P:(hd + 1) * P], src[:, t, PAIR * (hd // 2) + P * (hd % 2):][:, 0:P], ident[:, :])
                        mark(mm, S["qkT_mm"])
                        freed[b] = (S["qkT_evac"], 2 * (z * NT + t) + 1)
                        claim(b + 1)
                        for r in range(2):
                            mm = pe.transpose(pb[b + 1][:, r * P:(r + 1) * P], src[:, t, PAIR * r + 2 * NOPE:PAIR * (r + 1)], ident[:, :])
                        mark(mm, S["qkT_mm"])
                        freed[b + 1] = (S["qkT_evac"], 2 * (z * NT + t) + 2)

                token_group([("vg", n) for n in range(3)], 4, VG, X, 0, None, S["tok_mm"], (S["tok_evac"], 0))
                token_group([("br", n) for n in range(2)], 4, NH * GDV, X, 0, None, S["tok_mm"], (S["tok_evac"], NT))
                token_group([("cig", n) for n in range(4)], 0, 2 * NH * HDV, X, 0, None, S["tok_mm"], (S["tok_evac"], 2 * NT))
                transpose_qk(0, q_tok)
                transpose_qk(1, k_tok)
                claim(4)
                pe.wait_ge(S["tok_evac"], NT)
                for t in range(NT):
                    mm = pe.transpose(pb[4][0:RANK, t * P:(t + 1) * P], vg_tok[:, t, NH * GDV:VG], ident[:, :])
                mark(mm, S["lr_t"])
                freed[4] = (S["lr_evac"], 1)
                claim(5)
                pe.wait_ge(S["lr_evac"], 1)
                pe.wait_ge(S["spread_in"], 16 * (1 + len(spread_of)))
                mark(pe.matmul(pb[5][:, :], w_gate[:, :], lrT[:, :], start=True, stop=True), S["gate_mm"])
                freed[5] = (S["gate_min"], 1)
                pe.wait_ge(S["qkT_evac"], 4 * NT)
                pe.wait_ge(S["v_evac"], NT)

                pe.wait_ge(S["zeroed"], 2)

                def mla_score(o, hd, t, n):
                    pe.matmul(o, qT_n[:, hd, t * P:(t + 1) * P], kT_n[:, hd, 0:n], start=True, stop=False)
                    return pe.matmul(o, qT_r[:, hd, t * P:(t + 1) * P], kT_r[:, hd // 2, 0:n], start=False, stop=True)

                attend(0, MLA_GROUPS, mla_score, lambda t: (t + 1) * P, lambda n: n * P,
                       lambda n, hd: v_tok[:, n, hd * VD:(hd + 1) * VD], probsT, probs)
                for li, m in enumerate(LEVELS):
                    for x in range(2):
                        pe.wait_ge(S["level_done"], 2 * li + x + 1)
                        pe.wait_ge(S["qx_done"], 2 * li + x + 1)
                        for n in range(NT):
                            b = NT * x + n
                            claim(b)
                            bank = pb[b][:, :].rearrange("p (h q) -> p h q", h=NH)
                            parts = [(2 * m * c, m, 2 * m * c + m, m) for c in range(P // (2 * m))] if m >= 32 else [(0, P, 0, P)]
                            for j, nj, i, ni in parts:
                                for f in range(1 + x):
                                    hs = slice(0, NH) if x == 0 else slice(2 * f, 2 * f + 2)
                                    mm = pe.matmul(bank[j:j + nj, hs, i:i + ni], K[:, x + f, n * P + j:n * P + j + nj],
                                                   Qx[x][:, hs, n * P + i:n * P + i + ni], start=True, stop=True)
                            mark(mm, S["sweep_mm"])
                            freed[b] = (S["swept_v"], 2 * NT * li + b + 1) if m < 16 else \
                                (S["swept_a"], 2 * NT * (li - 5) + b + 1)
                pe.wait_ge(S["level_done"], 2 * len(LEVELS) + 2)
                for f in range(3):
                    claim(f)
                    for n in range(NT):
                        mm = pe.transpose(pb[f][:, n * P:(n + 1) * P], K[:, f, n * P:(n + 1) * P], ident[:, :])
                    mark(mm, S["khat_t"])
                    freed[f] = (S["khat_evac"], f + 1)
                pe.wait_ge(S["tok_evac"], 3 * NT)
                for n in range(NT - 1):
                    claim(3 + n)
                    pe.wait_ge(S["khat_evac"], 3)
                    pe.matmul(pb[3 + n][:, 0:256], k_hat[:, 0, n, :], vg_tok[:, n, 0:256], start=True, stop=True)
                    for f in range(2):
                        mm = pe.matmul(pb[3 + n][:, 256 + f * P:256 + (f + 1) * P], k_hat[:, 1 + f, n, :],
                                       ci_tok[:, n, f * P:(f + 1) * P], start=True, stop=True)
                    mark(mm, S["u_mm"])
                    freed[3 + n] = (S["state_done"], n + 1)
                for n in range(NT):
                    b = (6, 7, 4, 5)[n]
                    claim(b)
                    pe.wait_ge(S["swept_a"], 3 * 2 * NT)
                    if n:
                        pe.wait_ge(S["state_done"], n)
                        for f in range(3):
                            c = slice(0, 256) if f == 0 else slice(P + f * P, 2 * P + f * P)
                            pe.matmul(pb[b][:, c], Q[:, f, n * P:(n + 1) * P], state[:, n - 1, c],
                                      start=(f == 0), stop=False, skip_group_check=True)
                    for hh in range(2 * NH):
                        sc, val = (scores_g, vg_tok) if hh < NH else (scores_h, ci_tok)
                        hd = hh % NH
                        mm = pe.matmul(pb[b][:, hh * 64:(hh + 1) * 64], sc[:, n, hd, :], val[:, n, hd * 64:(hd + 1) * 64],
                                       start=(n == 0 and hh == 0), stop=(hh == 2 * NH - 1), skip_group_check=True)
                    mark(mm, S["o_mm"])
                    freed[b] = (S["o_evac"], n + 1)
                def project(name, nk, ready, x, base, half):
                    token_group([(name, half, n) for n in range((nk + 1) // 2)], 4 * half, HALF, x, 0, ready,
                                S["proj_mm"], (S["h_added"], base + NT * half))

                def y_ready(k):
                    if k == NH:
                        for c in range(4):
                            claim(4 + c)
                            for n in range(NT):
                                pe.wait_ge(S["o_done"], n + 1)
                                mm = pe.transpose(pb[4 + c][:, n * P:(n + 1) * P], o_tok[:, n, c * P:(c + 1) * P], ident[:, :])
                            mark(mm, S["yT_mm"])
                            freed[4 + c] = (S["yT_lo"], c + 1)
                    return (S["pv_lo"], k + 1) if k < NH else (S["yT_lo"], k - NH + 1)

                project("mix", KD, y_ready, X, 0, 0)
                project("mix", KD, None, X, 0, 1)
                pe.wait_ge(S["mem_in"], 16 * MT)
                for c in range(KD // 2):
                    claim(4 + c)
                    for k in range(2):
                        for m in range(MT):
                            mm = pe.transpose(pb[4 + c][:, k * NM + m * P:k * NM + (m + 1) * P],
                                              mem_tok[:, m, (2 * c + k) * P:(2 * c + k + 1) * P], ident[:, :])
                    mark(mm, S["memT_mm"])
                    freed[4 + c] = (S["m_lo_done"], 2 * c + 2)
                transpose_h(1, range(KD // 2))

                def memory_half(half):
                    token_group([("ckv", half, n) for n in range(KD // 2)], 2 * half, HALF, (m_hi, m_lo), 0,
                                lambda k: (S["m_lo_done"], k + 1), S["ckv_mm"], (S["ckv_evac"], MT * half), nt=MT)

                memory_half(0)
                transpose_h(1, range(KD // 2, KD))
                token_group([("caq", n) for n in range(KD // 2)], 4, NH * P, X, 0, lambda k: (S["x_lo_done"], KD + k + 1),
                            S["cq_mm"], (S["cq_evac"], 0))
                memory_half(1)
                for t in range(NT):
                    claim(4 + t)
                    pe.wait_ge(S["cq_done"], t + 1)
                    for hd in range(NH):
                        mm = pe.transpose(pb[4 + t][:, hd * P:(hd + 1) * P], cq_tok[:, t, hd * P:(hd + 1) * P], ident[:, :])
                    mark(mm, S["cqT_mm"])
                    freed[4 + t] = (S["cqT_evac"], t + 1)
                for r in range(2):
                    claim(r)
                    pe.wait_ge(S["ck_done"], r + 1)
                    for hd in range(2):
                        for m in range(MT):
                            c = (2 * r + hd) * 2 * P
                            mm = pe.transpose(pb[r][:, hd * NM + m * P:hd * NM + (m + 1) * P], ckv_tok[:, m, c:c + P], ident[:, :])
                    mark(mm, S["ckT_mm"])
                    freed[r] = (S["ckT_evac"], r + 1)
                pe.wait_ge(S["ckT_evac"], 2)
                pe.wait_ge(S["cqT_evac"], NT)

                def ca_score(o, hd, t, n):
                    return pe.matmul(o, cqT[:, hd, t * P:(t + 1) * P], ckT[:, hd, :], start=True, stop=True)

                attend(MLA_ITEMS, CA_GROUPS, ca_score, lambda t: NM, lambda n: 0,
                       lambda n, hd: ckv_tok[:, n, hd * 2 * P + P:(hd + 1) * 2 * P], cprobsT, cprobs)
                for half in range(2):
                    project("cao", NH, lambda k: (S["pv_lo"], NH + k + 1), X, H_ADDS, half)
                transpose_h(2, range(KD))
                for g in range(FG):
                    for c in range(FCG):
                        n = g * FCG + c
                        feature_chunk(("gate", g, c), 2 * (n % 2), 2, S["ffn_mm"], (S["gate_ready"], n + 1))
                        if n == 0:
                            spread_r(1)
                        feature_chunk(("up", g, c), 2 * (n % 2) + 1, 2, S["ffn_mm"], (S["act_ready"], n + 1))
                    for half in range(2):
                        project(("ffo", g), FCG, lambda k: (S["a_lo_done"], g * FCG + k + 1), (a_hi, a_lo),
                                (2 + g) * H_ADDS, half)

            @block.scalar
            def _(act_):
                link = chain(act_, S["chain_a"])
                nsplit = [0]

                def split_through(i):
                    while nsplit[0] <= min(i, NS - 1):
                        k = nsplit[0]
                        n = slabs[k][0] * slabs[k][1]
                        act_.wait_ge(raw_in[k % RAW], arrivals[k])
                        if k >= SPLIT:
                            act_.wait_ge(*released[k - SPLIT])
                        act_.activation(w_hi[k % SPLIT][:, 0:n], raw[k % RAW][:, 0:n], ACT.Copy).then_inc(S["hi_split"], 1)
                        nsplit[0] += 1

                def ahead(name):
                    split_through(slab_at[name] + SPLIT - 1)

                def inverse_rms(dst, tmp, ss, n, done):
                    link(act_.activation(tmp, ss, ACT.Ln, bias=eps_c[:, 0:1], scale=1.0 / n))
                    act_.activation(dst, tmp, ACT.Exp, scale=-0.5).then_inc(done, 1)

                LOG_EXP = "natural_log_exp_and_others"

                def norm(w, name, r_col):
                    for k in range(KD):
                        if w == 1 and k == KD // 2:
                            ahead(("ckv", 0, 3))
                        act_.wait_ge(S["hT_mm"], w * KD + k + 1)
                        act_.activation(x_hi[:, k, :], pb[4 + k % 4][:, :], ACT.Copy, scale=gain(name, k)).then_inc(S["x_hi_done"], 1)
                        if k % 2 == 1:
                            t = k // 2
                            link(act_.activation(junk[:, :], h[:, t, :], ACT.Square, accum_out=small[:, r_col + t:r_col + t + 1]))
                    inverse_rms(small[:, r_col + 8:r_col + 12], small[:, r_col + 4:r_col + 8], small[:, r_col:r_col + 4], D, S["r_done"])

                def attend(base, groups, n_keys, scale, pT, pr, between):
                    n_groups = len(groups)
                    items = NH * n_groups
                    for i in range(items + 3):
                        if i < items:
                            hd, c = i // n_groups, 0
                            act_.wait_ge(S["score_max"], base + i + 1)
                            if i >= 2:
                                act_.wait_ge(S["probsT_mm"], base + i - 1)
                            for t in groups[i % n_groups]:
                                n, st = n_keys(t), ATT + base // MLA_ITEMS * NH * NT + hd * NT + t
                                ex = act_.activation(pr[i % 2][:, c:c + n], pb[4 + i % 2][:, c:c + n], ACT.Exp,
                                                     bias=small[:, st + 32:st + 33], scale=scale,
                                                     accum_out=small[:, st + 64:st + 65])
                                c += n
                            ex.then_inc(S["score_exp"], 1)
                        j = i - 2
                        if 0 <= j < items:
                            hd, c = j // n_groups, 0
                            act_.wait_ge(S["probsT_mm"], base + j + 1)
                            if j % n_groups == 0 and hd:
                                act_.wait_ge(S["pv_mm"], base // MLA_ITEMS * NH + hd)
                            for t in groups[j % n_groups]:
                                nb = n_keys(t) // P
                                ev = act_.activation(pT[:, 0:nb, t * P:(t + 1) * P],
                                                     pb[6 + j % 2][:, c:c + nb * P].rearrange("p (n q) -> p n q", n=nb), ACT.Copy)
                                c += nb * P
                            ev.then_inc(S["probsT_evac"], 1)
                        j = i - 3
                        if 0 <= j < items and j % n_groups == n_groups - 1:
                            hd = j // n_groups
                            act_.wait_ge(S["pv_mm"], base // MLA_ITEMS * NH + hd + 1)
                            act_.activation(x_hi[:, hd, :], pb[hd][:, :], ACT.Copy).then_inc(S["pv_hi"], 1)
                        between(i)

                def expand(li, x, hd):
                    f, r0, dk = (0, GDK * hd, GDK) if x == 0 else (1 + hd // 2, HDK * (hd % 2), HDK)
                    r, m = slice(r0, r0 + dk), LEVELS[li - 1] if li else 0
                    dst, src = Qx[x][r, hd, :], Q[r, f, :]
                    if m:
                        dst, src = (a.rearrange("p (b two m) -> p b two m", two=2, m=m)[:, :, 1, :] for a in (dst, src))
                    return act_.activation(dst, src, ACT.Copy)

                split_through(SPLIT - 1)
                act_.activation(gains[:, :], gains_all[:, bass.ds(layer, 1), :].rearrange("p l r -> p (l r)"), ACT.Copy
                                ).then_inc(S["gains_ready"], 1)
                act_.wait_ge(S["gains_ready"], 1)
                act_.preload_act_table_set(LOG_EXP)
                norm(0, "norm_mix", R_MIX)
                for n in range(4):
                    ahead(("lat", n))
                    act_.wait_ge(S["lat_evac"], n + 1)
                    act_.activation(lat_sq[:, n, :], lat[:, n, :], ACT.Square).then_inc(S["lat_sq_done"], 1)
                    g_ = gain("mla_q_lat_norm", n) if n < 2 else gain("mla_kv_lat_norm", n - 2)
                    act_.activation(lat_hi[:, n, :], lat[:, n, :], ACT.Copy, scale=g_).then_inc(S["lat_hi_done"], 1)
                ahead("rope")
                act_.wait_ge(S["r_done"], 1)
                for t in range(NT):
                    act_.wait_ge(S["rope_mm"], t + 1)
                    act_.activation(kr_tok[:, t, :], pb[4 + t][:, 0:ROPE], ACT.Copy,
                                    scale=small[:, R_MIX + 8 + t:R_MIX + 9 + t]).then_inc(S["rope_evac"], 1)
                ahead(("feat", 0))
                act_.wait_ge(S["lat_ss_mm"], 1)
                inverse_rms(small[:, R_LAT + 8:R_LAT + 16], small[:, R_LAT:R_LAT + 8], pb[1][:, 0:8], QL, S["r_lat_done"])
                act_.wait_ge(S["r_lat_done"], 1)
                for n in range(2):
                    ahead(("q_up", n))
                    for t in range(NT):
                        act_.wait_ge(S["q_mm"], NT * n + t + 1)
                        act_.activation(q_tok[:, t, n * 2 * QK:(n + 1) * 2 * QK], pb[4 * n + t][:, 0:2 * QK], ACT.Copy,
                                        scale=small[:, R_LAT + 8 + t:R_LAT + 9 + t]).then_inc(S["q_evac"], 1)
                ahead(("kv_up", 0))
                for t in range(NT):
                    act_.wait_ge(S["k_mm"], t + 1)
                    act_.activation(nope_of(k_tok, t), pb[t][:, :].rearrange("p (r h x) -> p r h x", r=2, h=2), ACT.Copy,
                                    scale=small[:, R_LAT + 12 + t:R_LAT + 13 + t]).then_inc(S["k_evac"], 1)
                ahead(("kv_up", 1))
                for t in range(NT):
                    act_.wait_ge(S["v_mm"], t + 1)
                    act_.activation(v_tok[:, t, :], pb[4 + t][:, :], ACT.Copy,
                                    scale=small[:, R_LAT + 12 + t:R_LAT + 13 + t]).then_inc(S["v_evac"], 1)
                for n in range(2 * NT):
                    if n + 1 < len(FEATS):
                        ahead(("feat", n + 1))
                    c = R_QK + 4 * n
                    act_.wait_ge(S["qk_ss"], n + 1)
                    inverse_rms(small[:, c + 128:c + 132], small[:, c + 96:c + 100], small[:, c + 64:c + 68], QK, S["qk_r"])

                def qkT(z, dn, dr):
                    for t in range(NT):
                        b = 2 * (t % 2)
                        act_.wait_ge(S["qkT_mm"], 2 * (z * NT + t) + 1)
                        act_.activation(dn[:, :, t * P:(t + 1) * P], pb[b][:, :].rearrange("p (h q) -> p h q", h=NH),
                                        ACT.Copy).then_inc(S["qkT_evac"], 1)
                        act_.wait_ge(S["qkT_mm"], 2 * (z * NT + t) + 2)
                        two = pb[b + 1][:, 0:2 * P].rearrange("p (r q) -> p r q", r=2)
                        if z:
                            ev = act_.activation(dr[:, :, t * P:(t + 1) * P], two, ACT.Copy)
                        else:
                            for r in range(2):
                                half = slice(ROPE * r, ROPE * (r + 1))
                                ev = act_.activation(dr[half, r::2, t * P:(t + 1) * P], two[half], ACT.Copy)
                        ev.then_inc(S["qkT_evac"], 1)

                act_.wait_ge(S["feat_evac"], 2)
                link(act_.activation(K[:, 1:3, :], decay[:, 1:3, :], ACT.Sigmoid, scale=-1.0))
                act_.activation(decay[:, 1:3, :], decay[:, 1:3, :], ACT.Sigmoid).then_inc(S["f_sig"], 1)
                ahead(("vg", 2))
                act_.wait_ge(S["feat_evac"], 4)
                act_.activation(Q[:, 1:3, :], Q[:, 1:3, :], ACT.Silu).then_inc(S["q_silu"], 1)

                def r_mix(t):
                    return small[:, R_MIX + 8 + t:R_MIX + 9 + t]

                for t in range(NT):
                    act_.wait_ge(S["tok_mm"], t + 1)
                    act_.activation(vg_tok[:, t, :], pb[4 + t][:, 0:VG], ACT.Copy, scale=r_mix(t)).then_inc(S["tok_evac"], 1)
                ahead(("br", 1))
                for t in range(NT):
                    act_.wait_ge(S["tok_mm"], NT + t + 1)
                    act_.activation(sg_tok[:, t, 0:256], pb[4 + t][:, 0:256], ACT.Silu, scale=r_mix(t)).then_inc(S["tok_evac"], 1)
                ahead(("cig", 3))
                for t in range(NT):
                    act_.wait_ge(S["tok_mm"], 2 * NT + t + 1)
                    act_.activation(ci_tok[:, t, :], pb[t][:, 0:256], ACT.Copy, scale=r_mix(t))
                    act_.activation(sg_tok[:, t, 256:512], pb[t][:, 256:512], ACT.Silu, scale=r_mix(t)).then_inc(S["tok_evac"], 1)
                qkT(0, qT_n, qT_r)
                qkT(1, kT_n, kT_r)
                act_.wait_ge(S["gate_mm"], 1)
                act_.preload_act_table_set(LOG_EXP)
                link(act_.activation(gate_tmp[:, :], pb[5][:, :], ACT.Abs, bias=gain("gla_b_gate", 0)))
                link(act_.activation(gate_tmp[:, :], gate_tmp[:, :], ACT.Exp, scale=-1.0))
                act_.activation(gate_tmp[:, :], gate_tmp[:, :], ACT.Ln, bias=ones[:, 0:1]).then_inc(S["gate_exp"], 1)
                act_.wait_ge(S["gate_min"], 1)
                act_.activation(decay[:, 0, :], decay[:, 0, :], ACT.Exp, scale=1.0 / TAU).then_inc(S["gate_done"], 1)
                def first_queries(i):
                    if i == 4:
                        act_.wait_ge(S["zeroed"], 4)
                        act_.wait_ge(S["q_scaled"], 1)
                    if 4 <= i < 4 + 2 * NH:
                        ex = expand(0, (i - 4) // NH, (i - 4) % NH)
                        if (i - 4) % NH == NH - 1:
                            ex.then_inc(S["qx_done"], 1)

                attend(0, MLA_GROUPS, lambda t: (t + 1) * P, QK ** -0.5, probsT, probs, first_queries)
                for li, m in enumerate(LEVELS):
                    for x in range(2):
                        if li + 1 < len(LEVELS):
                            act_.wait_ge(S["level_done"], 2 * li + x + 3)
                            for hd in range(NH):
                                ex = expand(li + 1, x, hd)
                            ex.then_inc(S["qx_done"], 1)
                        if m < 16:
                            continue
                        sc = scores_h if x else scores_g
                        act_.wait_ge(S["swept_v"], 5 * 2 * NT)
                        for n in range(NT):
                            act_.wait_ge(S["sweep_mm"], 2 * NT * li + NT * x + n + 1)
                            src = pb[NT * x + n][:, :].rearrange("p (h q) -> p h q", h=NH)
                            for b in range(64 // m):
                                j, i = 2 * m * b, 2 * m * b + m
                                cp = act_.activation(sc[j:j + m, n, :, i:i + m], src[j:j + m, :, i:i + m], ACT.Copy)
                            cp.then_inc(S["swept_a"], 1)
                for f in range(3):
                    act_.wait_ge(S["khat_t"], f + 1)
                    act_.activation(k_hat[:, f], pb[f][:, :].rearrange("p (n q) -> p n q", n=NT), ACT.Copy).then_inc(S["khat_evac"], 1)
                for n in range(NT):
                    act_.wait_ge(S["o_mm"], n + 1)
                    act_.activation(o_tok[:, n, :], pb[(6, 7, 4, 5)[n]][:, :], ACT.Copy).then_inc(S["o_evac"], 1)
                    c = R_O + 8 * n
                    act_.wait_ge(S["o_ss"], n + 1)
                    inverse_rms(small[:, c + 64:c + 72], small[:, c + 32:c + 40], small[:, c:c + 8], GDV, S["o_r"])
                ahead(("mix", 0, 1))
                for c in range(4):
                    act_.wait_ge(S["yT_mm"], c + 1)
                    act_.activation(y_hi[:, NH + c, :], pb[4 + c][:, :], ACT.Copy).then_inc(S["yT_hi"], 1)
                act_.wait_ge(S["mem_in"], 16 * MT)
                ahead(("mix", 1, 3))
                for m in range(MT):
                    link(act_.activation(junk[:, :], mem_tok[:, m, :], ACT.Square, accum_out=small[:, R_MEM + m:R_MEM + m + 1]))
                inverse_rms(small[:, R_MEM + 4:R_MEM + 6], small[:, R_MEM + 2:R_MEM + 4], small[:, R_MEM:R_MEM + 2], D, S["mem_r"])
                for k in range(KD):
                    act_.wait_ge(S["memT_mm"], k // 2 + 1)
                    act_.activation(m_hi[:, k, :], pb[4 + k // 2][:, (k % 2) * NM:(k % 2 + 1) * NM], ACT.Copy,
                                    scale=gain("norm_mem", k)).then_inc(S["m_hi_done"], 1)
                act_.wait_ge(S["mem_r"], 1)
                norm(1, "norm_ca", R_CA)

                def memory_half(half):
                    ahead(("ckv", half, 3))
                    for m in range(MT):
                        act_.wait_ge(S["ckv_mm"], MT * half + m + 1)
                        act_.activation(ckv_tok[:, m, half * HALF:(half + 1) * HALF], pb[2 * half + m][:, :], ACT.Copy,
                                        scale=small[:, R_MEM + 4 + m:R_MEM + 5 + m]).then_inc(S["ckv_evac"], 1)
                    c = R_CK + 4 * half
                    act_.wait_ge(S["ck_ss"], half + 1)
                    inverse_rms(small[:, c + 16:c + 20], small[:, c + 8:c + 12], small[:, c:c + 4], P, S["ck_r"])

                memory_half(0)
                ahead(("caq", 3))
                act_.wait_ge(S["r_done"], 2)
                for t in range(NT):
                    act_.wait_ge(S["cq_mm"], t + 1)
                    act_.activation(cq_tok[:, t, :], pb[4 + t][:, :], ACT.Copy,
                                    scale=small[:, R_CA + 8 + t:R_CA + 9 + t]).then_inc(S["cq_evac"], 1)
                for t in range(NT):
                    c = R_CQ + 4 * t
                    act_.wait_ge(S["cq_ss"], t + 1)
                    inverse_rms(small[:, c + 32:c + 36], small[:, c + 16:c + 20], small[:, c:c + 4], P, S["cq_r"])
                memory_half(1)
                for t in range(NT):
                    act_.wait_ge(S["cqT_mm"], t + 1)
                    act_.activation(cqT[:, :, t * P:(t + 1) * P], pb[4 + t][:, :].rearrange("p (h q) -> p h q", h=NH),
                                    ACT.Copy).then_inc(S["cqT_evac"], 1)
                for r in range(2):
                    act_.wait_ge(S["ckT_mm"], r + 1)
                    act_.activation(ckT[:, 2 * r:2 * r + 2, :], pb[r][:, :].rearrange("p (h q) -> p h q", h=2), ACT.Copy
                                    ).then_inc(S["ckT_evac"], 1)
                attend(MLA_ITEMS, CA_GROUPS, lambda t: NM, P ** -0.5, cprobsT, cprobs, lambda i: None)
                ahead(("cao", 1, 1))
                norm(2, "norm_ffn", R_FFN)
                for g in range(FG):
                    for c in range(FCG):
                        n = g * FCG + c
                        ahead(("gate", g, c))
                        ahead(("up", g, c))
                        act_.wait_ge(S["silu_done"], 2 * n + 1)
                        act_.activation(conv_silu[n % 2][:, :], conv[n % 2][:, :], ACT.Silu).then_inc(S["silu_done"], 1)
                        act_.wait_ge(S["act_ready"], n + 1)
                        act_.activation(a_hi[:, c, :], act[n % 2][:, :], ACT.Copy).then_inc(S["a_hi_done"], 1)
                    ahead((("ffo", g), 1, FCG // 2))

            @block.vector
            def _(dve):
                link = chain(dve, S["chain_v"])

                def scaled(ap, n, col, like):
                    return small[:, col:col + n].unsqueeze(2).to_broadcast(like)

                def norm(w, name, r_col, n_spread):
                    for k in range(KD):
                        dve.wait_ge(S["x_hi_done"], w * KD + k + 1)
                        dve.scalar_tensor_tensor(x_lo[:, k, :], pb[4 + k % 4][:, :], gain(name, k), x_hi[:, k, :].bitcast(f32),
                                                 ALU.mult, ALU.subtract).then_inc(S["x_lo_done"], 1)
                    if n_spread is None:
                        return
                    dve.wait_ge(S["r_done"], w + 1)
                    dve.tensor_tensor(r_diag[:, :, :], ident[:, :].unsqueeze(1).to_broadcast([P, NT, P]),
                                      small[:, r_col + 8:r_col + 12].unsqueeze(2).to_broadcast([P, NT, P]),
                                      ALU.mult).then_inc(S["r_diag_done"], 1)
                    dve.wait_ge(S["r_mm"], n_spread + 1)
                    dve.tensor_copy(r_bc[:, :], pb[4][:, :]).then_inc(S["r_bc_done"], 1)
                    dve.wait_ge(S["r_bc_done"], n_spread + 1)

                def attend(base, groups, n_keys, scale, causal, pr):
                    n_groups = len(groups)
                    items = NH * n_groups
                    for i in range(items + 3):
                        if i < items:
                            g_ = groups[i % n_groups]
                            bank, c = pb[4 + i % 2], 0
                            st = ATT + base // MLA_ITEMS * NH * NT + i // n_groups * NT + g_[0]
                            dve.wait_ge(S["score_mm"], base + i + 1)
                            if causal:
                                for t in g_:
                                    c += n_keys(t)
                                    last = dve.memset(bank[0:BLOCK, c - BLOCK:c], MASKED)
                                link(last)
                            c = 0
                            if causal or len(g_) == 1:
                                for k, t in enumerate(g_):
                                    last = dve.reduce_max(small[:, st + k:st + k + 1], bank[:, c:c + n_keys(t)], AX.X)
                                    c += n_keys(t)
                            else:
                                last = dve.reduce_max(small[:, st:st + len(g_)], bank[:, :].rearrange("p (t k) -> p t k", t=len(g_)), AX.X)
                            link(last)
                            dve.tensor_scalar(small[:, st + 32:st + 32 + len(g_)], small[:, st:st + len(g_)], -scale, None, ALU.mult
                                              ).then_inc(S["score_max"], 1)
                        j = i - 1
                        if 0 <= j < items:
                            g_, c = groups[j % n_groups], 0
                            st = ATT + base // MLA_ITEMS * NH * NT + j // n_groups * NT + g_[0]
                            dve.wait_ge(S["score_exp"], base + j + 1)
                            link(dve.reciprocal(small[:, st + 96:st + 96 + len(g_)], small[:, st + 64:st + 64 + len(g_)]))
                            for k, t in enumerate(g_):
                                n = n_keys(t)
                                last = dve.tensor_scalar(pr[j % 2][:, c:c + n], pr[j % 2][:, c:c + n],
                                                         small[:, st + 96 + k:st + 97 + k], None, ALU.mult)
                                c += n
                            last.then_inc(S["probs_done"], 1)
                        j = i - 3
                        if 0 <= j < items and j % n_groups == n_groups - 1:
                            hd = j // n_groups
                            dve.wait_ge(S["pv_hi"], base // MLA_ITEMS * NH + hd + 1)
                            dve.tensor_tensor(x_lo[:, hd, :], pb[hd][:, :], x_hi[:, hd, :].bitcast(f32), ALU.subtract
                                              ).then_inc(S["pv_lo"], 1)

                def add_to_h(base):
                    for half in range(2):
                        for t in range(NT):
                            dve.wait_ge(S["proj_mm"], base + half * NT + t + 1)
                            c = slice(half * HALF, (half + 1) * HALF)
                            dve.tensor_tensor(h[:, t, c], h[:, t, c], pb[4 * half + t][:, :], ALU.add).then_inc(S["h_added"], 1)

                link(dve.tensor_scalar(lb_floor[:, :], lb_all[:, :, bass.ds(layer, 1)].squeeze(2), 1.0, None, ALU.mult))
                dve.tensor_scalar(lb_rest[:, :], lb_floor[:, :], -1.0, 1.0, ALU.mult, ALU.add)
                link(dve.memset(small[:, 515:516], 0.0))
                link(dve.tensor_scalar(lb_floor[:, :], lb_floor[:, :], LB_FLOOR, None, ALU.max))
                dve.wait_ge(S["gains_ready"], 1)
                norm(0, "norm_mix", R_MIX, 0)

                def lat_lo_part(n):
                    g_ = gain("mla_q_lat_norm", n) if n < 2 else gain("mla_kv_lat_norm", n - 2)
                    dve.wait_ge(S["lat_hi_done"], n + 1)
                    dve.scalar_tensor_tensor(lat_lo[:, n, :], lat[:, n, :], g_, lat_hi[:, n, :].bitcast(f32),
                                             ALU.mult, ALU.subtract).then_inc(S["lat_lo_done"], 1)

                for n in range(4):
                    dve.wait_ge(S["lat_mm"], n + 1)
                    dve.tensor_tensor(lat[:, n, :], pb[n][:, :], r_bc[:, :], ALU.mult).then_inc(S["lat_evac"], 1)
                    if n:
                        lat_lo_part(n - 1)
                lat_lo_part(3)
                dve.wait_ge(S["spread_in"], 16 * (1 + len(spread_of)))

                def prepare(z, t):
                    tok, name = (q_tok, "mla_q_norm") if z == 0 else (k_tok, "mla_k_norm")
                    nope, rope = nope_of(tok, t), rope_of(tok, t)
                    c = R_QK + 4 * (z * NT + t)
                    if z:
                        dve.wait_ge(S["k_evac"], t + 1)
                        dve.wait_ge(S["rope_evac"], t + 1)
                        link(dve.tensor_copy(rope, kr_tok[:, t, :].unsqueeze(1).unsqueeze(1).to_broadcast([P, 2, 2, ROPE])))
                    else:
                        dve.wait_ge(S["q_evac"], NT + t + 1)
                    for hd in range(NH):
                        for part, x, n in ((nope, 0, NOPE), (rope, NOPE, ROPE)):
                            head = part[:, hd // 2, hd % 2, :]
                            col = c + hd + (32 if x else 0)
                            last = dve.tensor_tensor_reduce(out=junk_v[:, hd, x:x + n], in0=head, in1=head, scale=1.0, scalar=0.0,
                                                            op0=ALU.mult, op1=ALU.add, accum_out=small[:, col:col + 1])
                    link(last)
                    dve.tensor_tensor(small[:, c + 64:c + 68], small[:, c:c + 4], small[:, c + 32:c + 36], ALU.add
                                      ).then_inc(S["qk_ss"], 1)
                    dve.wait_ge(S["qk_r"], z * NT + t + 1)
                    factor = small[:, c + 128:c + 132].rearrange("p (r h) -> p r h", r=2).unsqueeze(3)
                    dve.tensor_tensor(nope, nope, factor.to_broadcast([P, 2, 2, NOPE]), ALU.mult)
                    link(dve.tensor_tensor(rope, rope, factor.to_broadcast([P, 2, 2, ROPE]), ALU.mult))
                    g_ = spread_col(name).unsqueeze(1).unsqueeze(1)
                    dve.tensor_tensor(nope, nope, g_[:, :, :, 0:NOPE].to_broadcast([P, 2, 2, NOPE]), ALU.mult)
                    link(dve.tensor_tensor(rope, rope, g_[:, :, :, NOPE:QK].to_broadcast([P, 2, 2, ROPE]), ALU.mult))
                    R2_ = ROPE // 2
                    x1, x2 = rope[:, :, :, 0:R2_], rope[:, :, :, R2_:ROPE]
                    cs, sn = (a[:, t, :].unsqueeze(1).unsqueeze(1).to_broadcast([P, 2, 2, R2_]) for a in (cos, sin))
                    rot = r_diag[:, :, :].rearrange("p a (r h x) -> p a r h x", r=2, h=2)
                    dve.tensor_tensor(rot[:, 0], x1, cs, ALU.mult)
                    dve.tensor_tensor(rot[:, 1], x2, sn, ALU.mult)
                    dve.tensor_tensor(rot[:, 2], x2, cs, ALU.mult)
                    link(dve.tensor_tensor(rot[:, 3], x1, sn, ALU.mult))
                    dve.tensor_tensor(x1, rot[:, 0], rot[:, 1], ALU.subtract)
                    dve.tensor_tensor(x2, rot[:, 2], rot[:, 3], ALU.add).then_inc(S["qk_done"], 1)
                    dve.wait_ge(S["qk_done"], z * NT + t + 1)

                dests = [decay[:, 1, :], decay[:, 2, :], Q[:, 1, :], Q[:, 2, :], Q[:, 0, :], K[:, 0, :]]

                def feature(n):
                    dve.wait_ge(S["feat_mm"], n + 1)
                    dve.scalar_tensor_tensor(dests[n], pb[n % 4][:, :], GDK ** -0.5 if n == 4 else 1.0, r_bc[:, :],
                                             ALU.mult, ALU.mult).then_inc(S["feat_evac"], 1)

                feature(0)
                for n in range(2 * NT):
                    prepare(n // NT, n % NT)
                    if n + 1 < len(FEATS):
                        feature(n + 1)
                dve.wait_ge(S["f_sig"], 1)
                for n in range(2):
                    r, fl = lb_rest[:, n:n + 1], lb_floor[:, n:n + 1]
                    dve.tensor_scalar(K[:, 1 + n, :], K[:, 1 + n, :], r, None, ALU.mult)
                    link(dve.tensor_scalar(decay[:, 1 + n, :], decay[:, 1 + n, :], r, fl, ALU.mult, ALU.add))
                    dve.tensor_scalar(decay[:, 1 + n, :], decay[:, 1 + n, :], 1.0, None, ALU.min)
                dve.wait_ge(S["feat_evac"], 6)
                dve.wait_ge(S["q_silu"], 1)
                dve.tensor_scalar(Q[:, 1:3, :], Q[:, 1:3, :], HDK ** -0.5, None, ALU.mult).then_inc(S["q_scaled"], 1)
                dve.wait_ge(S["lr_t"], 1)
                dve.tensor_copy(lrT[:, :], pb[4][0:RANK, :]).then_inc(S["lr_evac"], 1)
                dve.wait_ge(S["gate_exp"], 1)
                link(dve.tensor_scalar(decay[:, 0, :], pb[5][:, :], gain("gla_b_gate", 0), 0.0, ALU.add, ALU.min))
                dve.tensor_tensor(decay[:, 0, :], decay[:, 0, :], gate_tmp[:, :], ALU.subtract).then_inc(S["gate_min"], 1)
                attend(0, MLA_GROUPS, lambda t: (t + 1) * P, QK ** -0.5, True, probs)
                dve.wait_ge(S["gate_done"], 1)
                dve.memset(state[:, 0, :], 0.0).then_inc(S["level_done"], 1)
                dve.memset(state[:, 1:, :], 0.0).then_inc(S["level_done"], 1)

                def next_level(li, f0, f1):
                    m = LEVELS[li]
                    if m == 0:
                        return dve.tensor_tensor(Q[:, f0:f1, :], Q[:, f0:f1, :], decay[:, f0:f1, :], ALU.mult)
                    nb = SEQ // (2 * m)
                    for f in range(f0, f1):
                        d = block_decay(m, slice(0, P), f).rearrange("p (b two) -> p b two", two=2)
                        q = Q[:, f, :].rearrange("p (b two m) -> p b two m", two=2, m=m)
                        k = K[:, f, :].rearrange("p (b two m) -> p b two m", two=2, m=m)
                        dve.tensor_tensor(q[:, :, 1, :], q[:, :, 1, :], d[:, :, 0:1].to_broadcast([P, nb, m]), ALU.mult)
                        dve.tensor_tensor(k[:, :, 0, :], k[:, :, 0, :], d[:, :, 1:2].to_broadcast([P, nb, m]), ALU.mult)
                        last = dve.tensor_tensor(block_decay(2 * m, slice(0, P), f), d[:, :, 0], d[:, :, 1], ALU.mult)
                    return last

                for li, m in enumerate(LEVELS):
                    for x in range(2):
                        dve.wait_ge(S["sweep_mm"], 2 * NT * li + NT * (x + 1))
                        dve.wait_ge(S["qx_done"], 2 * li + x + 1)
                        next_level(li, *((0, 1) if x == 0 else (1, 3))).then_inc(S["level_done"], 1)
                        dve.wait_ge(S["level_done"], 2 * li + x + 3)
                        if m >= 16:
                            continue
                        sc = scores_g if x == 0 else scores_h
                        for n in range(NT):
                            bank = pb[x * NT + n][:, :].rearrange("p (h q) -> p h q", h=NH)
                            if m == 0:
                                cp = dve.tensor_tensor(sc[:, n], bank, ident[:, :].unsqueeze(1).to_broadcast([P, NH, P]), ALU.mult)
                            else:
                                cp = dve.copy_predicated(sc[:, n], pair_mask[m][:, :].unsqueeze(1).to_broadcast([P, NH, P]), bank)
                            cp.then_inc(S["swept_v"], 1)
                for n in range(NT - 1):
                    dve.wait_ge(S["u_mm"], n + 1)
                    for hh in range(2 * NH):
                        f, r0, dk = (0, GDK * hh, GDK) if hh < NH else (1 + (hh - NH) // 2, HDK * (hh % 2), HDK)
                        r, c = slice(r0, r0 + dk), slice(64 * hh, 64 * hh + 64)
                        u = pb[3 + n][r, c]
                        if n == 0:
                            st = dve.tensor_copy(state[r, n, c], u)
                        else:
                            st = dve.scalar_tensor_tensor(state[r, n, c], state[r, n - 1, c], block_decay(P, r, f)[:, n:n + 1],
                                                          u, ALU.mult, ALU.add)
                    st.then_inc(S["state_done"], 1)
                    dve.wait_ge(S["state_done"], n + 1)
                for n in range(NT):
                    c = R_O + 8 * n
                    o = o_tok[:, n, :].rearrange("p (h x) -> p h x", x=64)
                    sq = o_sq[:, :].rearrange("p (h x) -> p h x", x=64)
                    dve.wait_ge(S["o_evac"], n + 1)
                    link(dve.tensor_tensor(sq, o, o, ALU.mult))
                    dve.reduce_sum(small[:, c:c + 8], sq, AX.X).then_inc(S["o_ss"], 1)
                    dve.wait_ge(S["o_r"], n + 1)
                    link(dve.tensor_tensor(o, o, scaled(small, 8, c + 64, [P, 8, 64]), ALU.mult))
                    g0 = spread_of["gla_out_norm"][0]
                    link(dve.tensor_tensor(o_tok[:, n, :].rearrange("p (m h x) -> p m h x", m=2, x=64),
                                           o_tok[:, n, :].rearrange("p (m h x) -> p m h x", m=2, x=64),
                                           spread[:, g0:g0 + 128].rearrange("p (m x) -> p m x", m=2).unsqueeze(2)
                                           .to_broadcast([P, 2, NH, 64]), ALU.mult))
                    dve.tensor_tensor(o_tok[:, n, :], o_tok[:, n, :], sg_tok[:, n, :], ALU.mult).then_inc(S["o_done"], 1)
                for c in range(4):
                    dve.wait_ge(S["yT_hi"], c + 1)
                    dve.tensor_tensor(y_lo[:, NH + c, :], pb[4 + c][:, :], y_hi[:, NH + c, :].bitcast(f32), ALU.subtract
                                      ).then_inc(S["yT_lo"], 1)
                add_to_h(0)
                for k in range(KD):
                    dve.wait_ge(S["m_hi_done"], k // 2 * 2 + 2)
                    dve.scalar_tensor_tensor(m_lo[:, k, :], pb[4 + k // 2][:, (k % 2) * NM:(k % 2 + 1) * NM], gain("norm_mem", k),
                                             m_hi[:, k, :].bitcast(f32), ALU.mult, ALU.subtract).then_inc(S["m_lo_done"], 1)
                norm(1, "norm_ca", R_CA, None)

                def memory_keys(half):
                    dve.wait_ge(S["ckv_evac"], (half + 1) * MT)
                    keys = ckv_tok[:, :, half * HALF:(half + 1) * HALF].rearrange("p m (h x) -> p m h x", h=2)[:, :, :, 0:P]
                    sq = ckv_sq[:, :, 2 * half:2 * half + 2, :]
                    c = R_CK + 4 * half
                    link(dve.tensor_tensor(sq, keys, keys, ALU.mult))
                    dve.tensor_reduce(small[:, c:c + 4].rearrange("p (m h) -> p m h", m=MT), sq, AX.X, ALU.add).then_inc(S["ck_ss"], 1)
                    dve.wait_ge(S["ck_r"], half + 1)
                    link(dve.tensor_tensor(keys, keys, small[:, c + 16:c + 20].rearrange("p (m h) -> p m h", m=MT).unsqueeze(3)
                                           .to_broadcast([P, MT, 2, P]), ALU.mult))
                    dve.tensor_tensor(keys, keys, spread_col("ca_k_norm").unsqueeze(1).unsqueeze(1).to_broadcast([P, MT, 2, P]),
                                      ALU.mult).then_inc(S["ck_done"], 1)

                memory_keys(0)
                for t in range(NT):
                    c = R_CQ + 4 * t
                    q = cq_tok[:, t, :].rearrange("p (h x) -> p h x", h=NH)
                    sq = cq_sq[:, t, :].rearrange("p (h x) -> p h x", h=NH)
                    dve.wait_ge(S["cq_evac"], t + 1)
                    link(dve.tensor_tensor(sq, q, q, ALU.mult))
                    dve.reduce_sum(small[:, c:c + 4], sq, AX.X).then_inc(S["cq_ss"], 1)
                for t in range(NT):
                    c = R_CQ + 4 * t
                    q = cq_tok[:, t, :].rearrange("p (h x) -> p h x", h=NH)
                    dve.wait_ge(S["cq_r"], t + 1)
                    link(dve.tensor_tensor(q, q, scaled(small, NH, c + 32, [P, NH, P]), ALU.mult))
                    dve.tensor_tensor(q, q, spread_col("ca_q_norm").unsqueeze(1).to_broadcast([P, NH, P]), ALU.mult
                                      ).then_inc(S["cq_done"], 1)
                memory_keys(1)
                attend(MLA_ITEMS, CA_GROUPS, lambda t: NM, P ** -0.5, False, cprobs)
                add_to_h(H_ADDS)
                for i in range(2):
                    dve.memset(gate_in[i][:, 0:CONV - 1], 0.0)
                norm(2, "norm_ffn", R_FFN, 1)
                for g in range(FG):
                    for c in range(FCG):
                        n = g * FCG + c
                        gi, cv = gate_in[n % 2], conv[n % 2]

                        def w_(t):
                            return gain("ffn_conv_w", t * FC + n)

                        dve.wait_ge(S["ffn_mm"], 2 * n + 1)
                        dve.tensor_tensor(gi[:, CONV - 1:], pb[2 * (n % 2)][:, :], r_bc[:, :], ALU.mult).then_inc(S["gate_ready"], 1)
                        dve.wait_ge(S["gate_ready"], n + 1)
                        link(dve.tensor_scalar(cv[:, :], gi[:, 0:SEQ], w_(0), gain("ffn_conv_b", n), ALU.mult, ALU.add))
                        for t in range(1, CONV - 1):
                            link(dve.scalar_tensor_tensor(cv[:, :], gi[:, t:t + SEQ], w_(t), cv[:, :], ALU.mult, ALU.add))
                        dve.scalar_tensor_tensor(cv[:, :], gi[:, CONV - 1:], w_(CONV - 1), cv[:, :], ALU.mult, ALU.add
                                                 ).then_inc(S["silu_done"], 1)
                        dve.wait_ge(S["ffn_mm"], 2 * n + 2)
                        link(dve.tensor_tensor(up_s[n % 2][:, :], pb[2 * (n % 2) + 1][:, :], r_bc[:, :], ALU.mult))
                        dve.wait_ge(S["silu_done"], 2 * n + 2)
                        dve.tensor_tensor(act[n % 2][:, :], conv_silu[n % 2][:, :], up_s[n % 2][:, :], ALU.mult).then_inc(S["act_ready"], 1)
                        dve.wait_ge(S["a_hi_done"], n + 1)
                        dve.tensor_tensor(a_lo[:, c, :], act[n % 2][:, :], a_hi[:, c, :].bitcast(f32), ALU.subtract
                                          ).then_inc(S["a_lo_done"], 1)
                    add_to_h((2 + g) * H_ADDS)

        clear_semaphores()
        layers.close()

        with nc.Block() as block:
            @block.sync
            def _(sp):
                for t in range(NT):
                    sp.dma_start(out[0, t * P:(t + 1) * P, :], h[:, t, :]).then_inc(stored, 16)
                sp.wait_ge(stored, 16 * NT)


_INS = ['x', 'mem', 'positions', 'norm_mix', 'w_in', 'mla_q_lat_norm', 'w_q_up', 'mla_kv_lat_norm', 'w_kv_up',
        'mla_q_norm', 'mla_k_norm', 'gla_w_gate', 'gla_b_gate', 'gla_out_norm', 'hgrn_lb_logits', 'hgrn_out_norm',
        'w_mix_out', 'norm_ca', 'norm_mem', 'w_ca_q', 'w_ca_kv', 'ca_q_norm', 'ca_k_norm', 'w_ca_out',
        'norm_ffn', 'w_ffn_in', 'ffn_conv_w', 'ffn_conv_b', 'w_ffn_out']


def kernel(**inputs):
    import numpy as np
    import concourse.bacc as bacc
    from concourse import mybir
    from concourse.bass_utils import run_bass_kernel_spmd

    nc = bacc.Bacc("TRN2", target_bir_lowering=False, num_devices=1)
    arrays, aps = {}, {}
    for name in _INS:
        a = np.ascontiguousarray(inputs[name])
        arrays[f"in_{name}"] = a
        aps[name] = nc.dram_tensor(f"in_{name}", a.shape, mybir.dt.from_np(a.dtype), kind="ExternalInput").ap()
    out = nc.dram_tensor("out_h", inputs['x'].shape, mybir.dt.float32, kind="ExternalOutput").ap()
    build_trunk(nc, aps, out)
    r = run_bass_kernel_spmd(nc, [arrays], core_ids=[0])
    return r.results[0]["out_h"]
```

```python
def build_trunk(nc, A, out):
    import concourse.bass as bass
    from concourse import mybir
    from contextlib import ExitStack
    import math
    import numpy as np

    f32, f32r, bf16 = mybir.dt.float32, mybir.dt.float32r, mybir.dt.bfloat16
    i32, u8 = mybir.dt.int32, mybir.dt.uint8
    ACT, ALU, AX = mybir.ActivationFunctionType, mybir.AluOpType, mybir.AxisListType

    P = 128
    DEPTH, D, P_IN = A["w_in"].shape
    SEQ = A["x"].shape[1]
    NM = A["mem"].shape[1]
    NT, KD, MT = SEQ // P, D // P, NM // P
    QL, KVL = A["w_q_up"].shape[1], A["w_kv_up"].shape[1]
    NH = 4
    NOPE = VD = P
    QK = A["w_q_up"].shape[2] // NH
    ROPE = QK - NOPE
    GDK, GDV = A["gla_w_gate"].shape[2] // NH, A["gla_out_norm"].shape[1]
    RANK = A["gla_w_gate"].shape[1]
    HDK, HDV = A["hgrn_lb_logits"].shape[1] // NH, A["hgrn_out_norm"].shape[1]
    DFF = A["w_ffn_out"].shape[1]
    CONV = A["ffn_conv_w"].shape[1]
    FC = DFF // P
    FG = 2
    FCG = FC // FG
    EPS, MASKED, TAU, THETA, LB_FLOOR, BLOCK = 1e-6, -1e30, 16.0, 10000.0, 1e-30, 64
    C_QL, C_KVL = 0, QL
    C_ROPE = C_KVL + KVL
    C_BQ = C_ROPE + ROPE
    C_BK = C_BQ + NH * GDK
    C_BV = C_BK + NH * GDK
    C_LR = C_BV + NH * GDV
    C_BR = C_LR + RANK
    C_CQ = C_BR + NH * GDV
    C_CF = C_CQ + NH * HDK
    C_CI = C_CF + NH * HDK
    C_CG = C_CI + NH * HDV
    HALF = D // 2
    ROPE_LR = ROPE + RANK

    rows_of, at = {}, 0
    for name, n in (("norm_mix", KD), ("mla_q_lat_norm", QL // P), ("mla_kv_lat_norm", KVL // P),
                    ("gla_b_gate", 1), ("norm_ca", KD), ("norm_mem", KD), ("norm_ffn", KD),
                    ("ffn_conv_w", CONV * FC), ("ffn_conv_b", FC), ("ca_q_norm", 1), ("ca_k_norm", 1)):
        rows_of[name] = (at, n)
        at += n
    ROWS = at
    spread_of, at = {}, 0
    for name, n in (("mla_q_norm", QK), ("mla_k_norm", QK), ("gla_out_norm", GDV), ("hgrn_out_norm", HDV)):
        spread_of[name] = (at, n)
        at += n
    SPREAD = at

    slabs, slab_at = [], {}

    def slab(name, nk, cols, src):
        slab_at[name] = len(slabs)
        slabs.append((nk, cols, src))

    def cut(w, k0, nk, c0, cols):
        def parts(l, dst):
            yield (dst[:, 0:nk * cols].rearrange("p (k c) -> p k c", k=nk),
                   w[l, k0 * P:(k0 + nk) * P, c0:c0 + cols].rearrange("(k p) c -> p k c", p=P))
        return parts

    def rope_lr_parts(l, dst):
        d = dst[:, 0:KD * ROPE_LR].rearrange("p (k c) -> p k c", k=KD)
        for c0, c, n in ((0, C_ROPE, ROPE), (ROPE, C_LR, RANK)):
            yield d[:, :, c0:c0 + n], A["w_in"][l, :, c:c + n].rearrange("(k p) c -> p k c", p=P)

    slab("rope", KD, ROPE_LR, rope_lr_parts)
    for n in range(4):
        slab(("lat", n), KD, P, cut(A["w_in"], 0, KD, n * P, P))
    FEATS = [C_CF, C_CF + P, C_CQ, C_CQ + P, C_BQ, C_BK]
    slab(("feat", 0), KD, P, cut(A["w_in"], 0, KD, FEATS[0], P))
    PAIR = 2 * QK

    def q_up_parts(n):
        def parts(l, dst):
            for k in range(2):
                src = A["w_q_up"][l, k * P:(k + 1) * P, n * PAIR:(n + 1) * PAIR].rearrange("p (h x) -> p h x", h=2)
                for x0, x1 in ((0, NOPE), (NOPE, QK)):
                    d = dst[:, k * PAIR + 2 * x0:k * PAIR + 2 * x1].rearrange("p (h x) -> p h x", h=2)
                    yield d, src[:, :, x0:x1]
        return parts

    def kv_up_parts(n):
        def parts(l, dst):
            for k in range(2):
                src = A["w_kv_up"][l, k * P:(k + 1) * P].rearrange("p (h x) -> p h x", h=NH)
                yield (dst[:, k * NH * P:(k + 1) * NH * P].rearrange("p (h x) -> p h x", h=NH),
                       src[:, :, n * P:(n + 1) * P])
        return parts

    for n in range(2):
        slab(("q_up", n), 2, PAIR, q_up_parts(n))
    for n in range(2):
        slab(("kv_up", n), 2, NH * P, kv_up_parts(n))
    for n, c in enumerate(FEATS[1:]):
        slab(("feat", n + 1), KD, P, cut(A["w_in"], 0, KD, c, P))
    TOKS = {"bv": (C_BV, NH * GDV, (4, 4)), "br": (C_BR, NH * GDV, (4, 4)),
            "cig": (C_CI, NH * HDV * 2, (2, 2, 2, 2))}
    for name, (c, cols, ks) in TOKS.items():
        for n, nk in enumerate(ks):
            slab((name, n), nk, cols, cut(A["w_in"], sum(ks[:n]), nk, c, cols))

    def half_of(name, w, nk_all, half, k0=0):
        for n in range((nk_all + 1) // 2):
            nk = min(2, nk_all - 2 * n)
            slab((name, half, n), nk, HALF, cut(w, k0 + 2 * n, nk, half * HALF, HALF))

    for half in range(2):
        half_of("mix", A["w_mix_out"], KD, half)
    def ckv_parts(half, n):
        def parts(l, dst):
            for k in range(2):
                r0 = (2 * n + k) * P
                src = A["w_ca_kv"][l, r0:r0 + P, :].rearrange("p (h two x) -> p h two x", two=2, x=P)[:, :, half, :]
                yield dst[:, k * NH * P:(k + 1) * NH * P].rearrange("p (h x) -> p h x", h=NH), src
        return parts

    def memory_slabs(half):
        for n in range(KD // 2):
            slab(("ckv", half, n), 2, NH * P, ckv_parts(half, n))

    memory_slabs(0)
    for n in range(KD // 2):
        slab(("caq", n), 2, NH * P, cut(A["w_ca_q"], 2 * n, 2, 0, NH * P))
    memory_slabs(1)
    for half in range(2):
        half_of("cao", A["w_ca_out"], NH, half)
    for g in range(FG):
        for c in range(FCG):
            slab(("gate", g, c), KD, P, cut(A["w_ffn_in"], 0, KD, (g * FCG + c) * P, P))
            slab(("up", g, c), KD, P, cut(A["w_ffn_in"], 0, KD, DFF + (g * FCG + c) * P, P))
        for half in range(2):
            half_of(("ffo", g), A["w_ffn_out"], FCG, half, k0=g * FCG)
    NS = len(slabs)
    RAW, SPLIT, SLAB = 3, 3, 1024

    with ExitStack() as ctx:
        def sb(name, shape, dt=f32):
            return ctx.enter_context(nc.sbuf_tensor(name, shape, dt))

        h = sb("h", [P, NT, D])
        raw = [sb(f"raw{i}", [P, SLAB]) for i in range(RAW)]
        w_hi = [sb(f"w_hi{i}", [P, SLAB], f32r) for i in range(SPLIT)]
        w_lo = [sb(f"w_lo{i}", [P, SLAB], f32r) for i in range(SPLIT)]
        ident = sb("ident", [P, P])
        ones = sb("ones", [P, P])
        LEVELS = (1, 2, 4, 8, 16, 32, 64)
        pair_mask = sb("pair_mask", [P, len(LEVELS), P // 2], u8)
        head_of = sb("head_of", [P, NH + 2])
        cos, sin = sb("cos", [P, NT, ROPE // 2]), sb("sin", [P, NT, ROPE // 2])
        eps_c = sb("eps_c", [P, 2])
        bounds = sb("bounds", [P, 2 * DEPTH + 4])
        lb_all = bounds[:, 0:2 * DEPTH].rearrange("p (c l) -> p c l", l=DEPTH)
        lb_floor, lb_rest = bounds[:, 2 * DEPTH:2 * DEPTH + 2], bounds[:, 2 * DEPTH + 2:2 * DEPTH + 4]
        gains_all = sb("gains_all", [P, DEPTH, ROWS])
        gains = sb("gains", [P, ROWS])
        spread = sb("spread", [P, SPREAD])
        w_gate = sb("w_gate", [ROPE_LR, NH * GDK])
        r_bc = sb("r_bc", [P, SEQ])
        r_diag = sb("r_diag", [P, NT, P])
        kr_tok = sb("kr_tok", [P, NT, ROPE])
        small = sb("small", [P, 548])

        KB = 1024
        ARENA = 141 * KB
        arena = sb("arena", [P, ARENA // 4])
        base = nc.sbuf_base - ARENA

        def place(name, kb, shape, dt=f32):
            size = 4 * int(np.prod(shape[1:]))
            assert int(kb * KB) + size <= ARENA, name
            return nc.alloc_sbuf_tensor_at(name, shape, dt, offset=base + int(kb * KB))

        x_hi = place("x_hi", 0, [P, KD, SEQ], f32r)
        x_lo = place("x_lo", 16, [P, KD, SEQ], f32r)
        y_hi, y_lo = x_hi, x_lo
        scores_g = place("scores_g", 8, [P, NT, NH, P])
        scores_h = place("scores_h", 24, [P, NT, NH, P])
        R0, R1, R2, R3, R4, R5 = 32, 48, 72, 80, 104, 125
        lat_hi = place("lat_hi", R0, [P, 4, SEQ], f32r)
        lat_lo = place("lat_lo", R0 + 8, [P, 4, SEQ], f32r)
        probsT = place("probsT", R0, [P, NT, SEQ])
        probs = [place(f"probs{i}", R0 + 8 + 2 * i, [P, SEQ]) for i in range(3)]
        gate_tmp = place("gate_tmp", R0 + 14, [P, SEQ])
        lat = place("lat", R1, [P, 4, SEQ])
        lat_sq = place("lat_sq", R1 + 8, [P, 4, SEQ])
        qT_n, kT_n = place("qT_n", R1, [P, NH, SEQ]), place("kT_n", R1 + 8, [P, NH, SEQ])
        qT_r = place("qT_r", R1 + 16, [P, NH, SEQ])
        kT_r = place("kT_r", R3, [P, 2, SEQ])
        v_tok = place("v_tok", R2, [P, NT, NH * VD])
        q_tok, k_tok = place("q_tok", R3, [P, NT, NH * QK]), place("k_tok", R3 + 12, [P, NT, NH * QK])
        Qx = [[place(f"Qx{x}_{i}", kb + 8 * x, [P, NH, SEQ]) for i, kb in enumerate((R3 + 4, R0))] for x in range(2)]
        qk = place("qk", R0, [P, 3, SEQ])
        decay_x = place("decay_x", R3 + 20, [P, 3, SEQ // 2])
        o_tok = place("o_tok", R1, [P, NT, 512])
        k_hat = place("k_hat", R1 + 8, [P, 3, NT, P])
        state = place("state", R1 + 14, [P, NT - 1, 512])
        o_sq = place("o_sq", R1 + 20, [P, 512])
        Q, K = place("Q", R4, [P, 3, SEQ]), place("K", R4 + 6, [P, 3, SEQ])
        decay = place("decay", R4 + 12, [P, 3, SEQ])
        decay_m = place("decay_m", R4 + 18, [P, 3, SEQ // 2])
        rope_lr = place("rope_lr", R4 + 18, [ROPE_LR, SEQ])
        bv_tok = place("bv_tok", R5, [P, NT, NH * GDV])
        ci_tok = place("ci_tok", R5 + 4, [P, NT, NH * HDV])
        sg_tok = place("sg_tok", R5 + 8, [P, NT, 512])
        mem_tok = place("mem_tok", R0, [P, MT, D])
        m_hi, m_lo = place("m_hi", R1, [P, KD, NM], f32r), place("m_lo", R1 + 8, [P, KD, NM], f32r)
        ckv_tok = place("ckv_tok", R2, [P, MT, D])
        ckv_sq = place("ckv_sq", R3, [P, MT, NH, P])
        ckT = place("ckT", R3 + 4, [P, NH, NM])
        cq_tok = place("cq_tok", R3 + 8, [P, NT, NH * P])
        cqT = place("cqT", R3 + 16, [P, NH, SEQ])
        cq_sq = place("cq_sq", R4, [P, NT, NH * P])
        cprobsT = [place(f"cprobsT{i}", R4 + 8 + 10 * i, [P, MT, SEQ]) for i in range(2)]
        cprobs = [place(f"cprobs{i}", R4 + 12 + 2 * i, [P, SEQ]) for i in range(3)]
        a_hi = place("a_hi", 32, [P, FCG, SEQ], f32r)
        a_lo = place("a_lo", 54, [P, FCG, SEQ], f32r)
        gate_in = [place(f"gate_in{i}", 76 + 2.25 * i, [P, CONV - 1 + SEQ]) for i in range(2)]
        conv = [place(f"conv{i}", 81 + 2 * i, [P, SEQ]) for i in range(2)]
        conv_silu = [place(f"conv_silu{i}", 85 + 2 * i, [P, SEQ]) for i in range(2)]
        up_s = [place(f"up_s{i}", 89 + 2 * i, [P, SEQ]) for i in range(2)]
        act = [place(f"act{i}", 93 + 2 * i, [P, SEQ]) for i in range(2)]
        rows = place("rows", 20, [P, DEPTH, P])
        junk = place("junk", R5 + 8, [P, D], bf16)
        junk_v = place("junk_v", R5 + 4, [P, NH, QK], bf16)
        lb_rows = place("lb_rows", 0, [DEPTH * 2, P])
        lb_t = place("lb_t", 1, [P, 8, 2, DEPTH])
        pos_i = place("pos_i", 2, [P, NT], i32)
        pos_f = place("pos_f", 3, [P, NT])
        ang = place("ang", 4, [P, NT, ROPE // 2])
        turns_i = place("turns_i", 5, [P, NT, ROPE // 2], i32)
        turns = place("turns", 6, [P, NT, ROPE // 2])
        over = place("over", 7, [P, NT, ROPE // 2])
        freq = place("freq", 8, [P, ROPE // 2])
        pairs = place("pairs", 9, [P, len(LEVELS), P // 2])

        pb = [ctx.enter_context(nc.psum_tensor(f"bank{i}", [P, 512], f32)) for i in range(8)]

        names = """lo_split hi_split slab_used spread_in mem_in rows_t gains_ready chain_v chain_a chain_p
            hT_mm x_hi_done x_lo_done r_done r_diag_done r_mm r_bc_done
            lat_mm lat_evac lat_sq_done lat_sq_sum lat_hi_done lat_lo_done lat_ss_mm r_lat_done
            rope_mm rope_lr_done rope_t rope_evac q_mm q_evac k_mm k_evac v_mm v_evac qk_ss qk_r qk_done qkT_mm qkT_evac
            feat_mm feat_evac f_sig q_silu tok_mm tok_evac gate_mm gate_exp gate_min gate_done
            score_mm score_max score_exp probs_done probsT_mm probsT_evac pv_mm pv_hi pv_lo
            qk_prod diag_mm diag_evac decays_done scores_base q_level k_level sweep_mm swept khat_t khat_evac u_mm state_done o_mm o_evac o_ss o_r o_done yT_mm yT_hi yT_lo
            proj_mm h_added mem_r memT_mm m_hi_done m_lo_done ckv_mm ckv_evac ck_ss ck_r ck_done ckT_mm ckT_evac
            cq_mm cq_evac cq_ss cq_r cqT_mm cqT_evac
            ffn_mm gate_ready silu_done act_ready a_hi_done a_lo_done lbT zeroed qx_done q_scaled
            identity_done pos_in logits_in rows_in pairs_made logits_shifted logits_exp angles_done tables_done""".split()
        S = {n: ctx.enter_context(nc.semaphore(n)) for n in names}
        raw_in = [ctx.enter_context(nc.semaphore(f"raw_in{i}")) for i in range(RAW)]
        every_sem = [S[n] for n in names] + raw_in
        x_in = ctx.enter_context(nc.semaphore("x_in"))
        stored = ctx.enter_context(nc.semaphore("stored"))

        def gain(name, n):
            c = rows_of[name][0] + n
            return gains[:, c:c + 1]

        def spread_col(name):
            c, n = spread_of[name]
            return spread[:, c:c + n]

        def nope_of(tok, t):
            return tok[:, t, :].rearrange("p (r y) -> p r y", r=2)[:, :, 0:2 * NOPE].rearrange("p r (h x) -> p r h x", h=2)

        def rope_of(tok, t):
            return tok[:, t, :].rearrange("p (r y) -> p r y", r=2)[:, :, 2 * NOPE:PAIR].rearrange("p r (h x) -> p r h x", h=2)

        def chain(eng, sem):
            count = [0]

            def link(ins):
                count[0] += 1
                ins.then_inc(sem, 1)
                eng.wait_ge(sem, count[0])
            return link

        with nc.Block() as block:
            @block.sync
            def _(sp):
                sp.dma_start(pos_i[:, :], A["positions"][0].rearrange("(t p) -> p t", p=P),
                             allow_slow_non_contiguous=True).then_inc(S["pos_in"], 16)
                sp.dma_start(lb_rows[:, :], A["hgrn_lb_logits"].rearrange("l (c p) -> (l c) p", p=P)
                             ).then_inc(S["logits_in"], 16)
                for name, (r0, n) in rows_of.items():
                    src = A[name]
                    src = src.rearrange("l t (c p) -> (t c) l p", p=P) if len(src.shape) == 3 else \
                        src.rearrange("l (c p) -> c l p", p=P)
                    sp.dma_start(rows[r0:r0 + n, :, :], src).then_inc(S["rows_in"], 16)
                    if r0 == 0:
                        for t in range(NT):
                            sp.dma_start(h[:, t, :], A["x"][0, t * P:(t + 1) * P, :]).then_inc(x_in, 16)
                sp.wait_ge(x_in, 16 * NT)

            @block.gpsimd
            def _(pool):
                link = chain(pool, S["chain_p"])
                link(pool.memset(ident[:, :], 0.0))
                pool.affine_select(out=ident[:, :], in_=ident[:, :], compare_op=ALU.not_equal, fill=1.0,
                                   base=0, pattern=[[-1, P]], channel_multiplier=1).then_inc(S["identity_done"], 1)
                link(pool.memset(pairs[:, :, :], 1.0))
                for li, m in enumerate(LEVELS):
                    c = P // (2 * m)
                    level = pairs[:, li, :].rearrange("p (c m) -> p c m", m=m)
                    link(pool.affine_select(out=level, in_=level, compare_op=ALU.is_ge, fill=0.0, base=0,
                                            pattern=[[-2 * m, c], [0, m]], channel_multiplier=1))
                    link(pool.affine_select(out=level, in_=level, compare_op=ALU.is_ge, fill=0.0, base=m - 1,
                                            pattern=[[2 * m, c], [0, m]], channel_multiplier=-1))
                link(pool.memset(head_of[:, :], 0.0))
                for hd in range(NH):
                    link(pool.memset(head_of[GDK * hd:GDK * (hd + 1), hd:hd + 1], 1.0))
                for r in range(2):
                    link(pool.memset(head_of[HDK * r:HDK * (r + 1), NH + r:NH + r + 1], 1.0))
                pool.memset(eps_c[:, 0:1], EPS)
                pool.memset(eps_c[:, 1:2], P * EPS).then_inc(S["pairs_made"], 1)

            @block.tensor
            def _(pe):
                pe.wait_ge(S["identity_done"], 1)
                pe.wait_ge(S["logits_in"], 16)
                pe.transpose(pb[0][:, 0:2 * DEPTH], lb_rows[:, :], ident[0:2 * DEPTH, 0:2 * DEPTH]
                             ).then_inc(S["lbT"], 1)
                pe.wait_ge(S["rows_in"], 16 * len(rows_of))
                for l in range(DEPTH):
                    pe.transpose(pb[1 + l][:, 0:ROWS], rows[0:ROWS, l, :], ident[0:ROWS, 0:ROWS]).then_inc(S["rows_t"], 1)

            @block.scalar
            def _(eng):
                eng.wait_ge(S["logits_shifted"], 1)
                eng.activation(lb_t[:, 2], lb_t[:, 1], ACT.Exp).then_inc(S["logits_exp"], 1)
                eng.wait_ge(S["angles_done"], 1)
                eng.activation(sin[:, :, :], ang[:, :, :], ACT.Sin).then_inc(S["tables_done"], 1)
                eng.wait_ge(S["angles_done"], 2)
                eng.activation(cos[:, :, :], turns[:, :, :], ACT.Sin).then_inc(S["tables_done"], 1)
                for l in range(DEPTH):
                    eng.wait_ge(S["rows_t"], l + 1)
                    eng.activation(gains_all[:, l, :], pb[1 + l][:, 0:ROWS], ACT.Copy).then_inc(S["tables_done"], 1)

            @block.vector
            def _(dve):
                link = chain(dve, S["chain_v"])
                dve.memset(ones[:, :], 1.0)
                inv = (np.float32(THETA) ** (-np.arange(0, ROPE, 2, dtype=np.float32) / np.float32(ROPE))).astype(np.float32)
                for j in range(ROPE // 2 - 1):
                    dve.memset(freq[:, j:j + 1], float(inv[j]))
                link(dve.memset(freq[:, ROPE // 2 - 1:ROPE // 2], float(inv[-1])))
                dve.wait_ge(S["lbT"], 1)
                link(dve.tensor_copy(lb_t[:, 0], pb[0][:, 0:2 * DEPTH].rearrange("p (l c) -> p c l", c=2)))
                link(dve.reduce_max(lb_t[:, 3, :, 0:1], lb_t[:, 0], AX.X))
                dve.tensor_tensor(lb_t[:, 1], lb_t[:, 0], lb_t[:, 3, :, 0:1].to_broadcast([P, 2, DEPTH]),
                                  ALU.subtract).then_inc(S["logits_shifted"], 1)
                dve.wait_ge(S["logits_exp"], 1)
                link(dve.reduce_sum(lb_t[:, 4, :, 0:1], lb_t[:, 2], AX.X))
                link(dve.reciprocal(lb_t[:, 5, :, 0:1], lb_t[:, 4, :, 0:1]))
                link(dve.tensor_tensor(lb_t[:, 6], lb_t[:, 2], lb_t[:, 5, :, 0:1].to_broadcast([P, 2, DEPTH]), ALU.mult))
                link(dve.tensor_copy(lb_t[:, 7, :, 0:1], lb_t[:, 6, :, 0:1]))
                for l in range(1, DEPTH):
                    link(dve.tensor_tensor(lb_t[:, 7, :, l:l + 1], lb_t[:, 7, :, l - 1:l], lb_t[:, 6, :, l:l + 1], ALU.add))
                link(dve.tensor_tensor(lb_all[:, :, :], lb_t[:, 7], lb_t[:, 6, :, 0:1].to_broadcast([P, 2, DEPTH]),
                                       ALU.subtract))
                dve.wait_ge(S["pos_in"], 16)
                link(dve.tensor_copy(pos_f[:, :], pos_i[:, :]))
                link(dve.tensor_tensor(ang[:, :, :], pos_f[:, :].unsqueeze(2).to_broadcast([P, NT, ROPE // 2]),
                                       freq[:, :].unsqueeze(1).to_broadcast([P, NT, ROPE // 2]), ALU.mult))
                link(dve.tensor_scalar(turns_i[:, :, :], ang[:, :, :], 1 / (2 * math.pi), None, ALU.mult))
                link(dve.tensor_copy(turns[:, :, :], turns_i[:, :, :]))
                c1 = 6.28125
                c2 = float(np.float32(math.floor((2 * math.pi - c1) * 2 ** 20) / 2 ** 20))
                c3 = 2 * math.pi - c1 - c2
                for c in (c1, c2, c3):
                    link(dve.scalar_tensor_tensor(ang[:, :, :], turns[:, :, :], -c, ang[:, :, :], ALU.mult, ALU.add))

                def wrap(a):
                    for cmp, lim, turn in ((ALU.is_gt, math.pi, -2 * math.pi), (ALU.is_lt, -math.pi, 2 * math.pi)):
                        link(dve.tensor_scalar(over[:, :, :], a, lim, turn, cmp, ALU.mult))
                        link(dve.tensor_tensor(a, a, over[:, :, :], ALU.add))

                wrap(ang[:, :, :])
                link(dve.tensor_scalar(turns[:, :, :], ang[:, :, :], math.pi / 2, None, ALU.add))
                wrap(turns[:, :, :])
                bound = float(np.nextafter(np.float32(math.pi), np.float32(0)))
                dve.tensor_scalar(ang[:, :, :], ang[:, :, :], bound, -bound, ALU.min, ALU.max).then_inc(S["angles_done"], 1)
                dve.tensor_scalar(turns[:, :, :], turns[:, :, :], bound, -bound, ALU.min, ALU.max).then_inc(S["angles_done"], 1)
                dve.wait_ge(S["pairs_made"], 1)
                dve.tensor_copy(pair_mask[:, :, :], pairs[:, :, :])

        def clear_semaphores():
            nc.all_engine_barrier()
            nums = sorted(s.num for s in every_sem)
            assert nums == list(range(nums[0], nums[0] + len(nums)))
            nc.gpsimd.sem_clear(range(nums[0], nums[-1] + 1))
            nc.all_engine_barrier()

        clear_semaphores()

        MLA_GROUPS, CA_GROUPS = ((0, 1), (2,), (3,)), ((0, 1), (2, 3))
        MLA_ITEMS = NH * len(MLA_GROUPS)
        H_ADDS = 2 * NT
        ATT, R_MIX, R_CA, R_FFN, R_LAT, R_MEM = 0, 128, 140, 152, 164, 180
        R_CK, R_CQ = 186, 210
        R_QK, R_O = 260, 420
        H_BANKS = ((4, 5, 6, 7, 0, 1, 2, 3), (0, 1, 2, 3, 6, 7, 2, 3), (0, 1, 2, 3, 4, 5, 6, 7))
        DIAG = 516

        FLIGHT = 3

        def pv_after(base):
            return FLIGHT + (2 if base else 1)

        PROJ_BANKS = ((0, 4), (0, 4), (4, 0), (0, 4))
        SCORE_BANKS, TURN_BANKS, PV_BANKS = (4, 5, 3), (6, 7), (0, 1)


        def block_decay(m, rows_, f):
            n = SEQ // m
            if m <= 2:
                return (decay if m == 1 else decay_m)[rows_, f, 0:n]
            return decay_x[rows_, f, SEQ // 2 - 2 * n:SEQ // 2 - n]

        def odd_blocks(a, m):
            return a.rearrange("p f (b two m) -> p f b two m", two=2, m=m)[:, :, :, 1, :]

        layers = ctx.enter_context(ExitStack())
        layer = layers.enter_context(nc.Fori(0, DEPTH))
        with nc.Block() as block:

            arrivals, total = [], [0] * RAW

            @block.sync
            def _(sp):
                for i, (nk, cols, src) in enumerate(slabs):
                    if i == slab_at["q_up", 0]:
                        sp.dma_start(w_gate[ROPE:ROPE_LR, :], A["gla_w_gate"][layer]).then_inc(S["spread_in"], 16)
                        for name, (c, n) in spread_of.items():
                            sp.dma_start(spread[:, c:c + n], A[name][layer].partition_broadcast(P)
                                         ).then_inc(S["spread_in"], 16)
                    if i == slab_at["mix", 1, 0]:
                        sp.wait_ge(S["pv_mm"], NH)
                        sp.wait_ge(S["gate_done"], 1)
                        sp.wait_ge(S["probsT_mm"], MLA_ITEMS)
                        sp.wait_ge(S["sweep_mm"], 2 * NT * len(LEVELS))
                        for m in range(MT):
                            sp.dma_start(mem_tok[:, m, :], A["mem"][0, m * P:(m + 1) * P, :]).then_inc(S["mem_in"], 16)
                    if i >= RAW:
                        sp.wait_ge(S["lo_split"], i - RAW + 1)
                    for dst, part in src(layer, raw[i % RAW]):
                        sp.dma_start(dst, part).then_inc(raw_in[i % RAW], 16)
                        total[i % RAW] += 16
                    arrivals.append(total[i % RAW])

            def recurrences(pool):
                pool.wait_ge(S["qkT_mm"], 4 * NT)
                for x in range(2):
                    pool.memset(Qx[x][0][:, :, :], 0.0).then_inc(S["zeroed"], 1)
                pool.wait_ge(S["diag_evac"], 1)
                for x, sc in enumerate((scores_g, scores_h)):
                    for n in range(NT):
                        c = DIAG + 8 * n + NH * x
                        pool.tensor_tensor(sc[:, n], ident[:, :].unsqueeze(1).to_broadcast([P, NH, P]),
                                           small[:, c:c + NH].unsqueeze(2).to_broadcast([P, NH, P]), ALU.mult
                                           ).then_inc(S["scores_base"], 1)
                pool.wait_ge(S["gate_done"], 1)
                for li, m in enumerate(LEVELS):
                    d = block_decay(m, slice(0, P), slice(0, 3)).rearrange("p f (b two) -> p f b two", two=2)
                    pool.tensor_tensor(block_decay(2 * m, slice(0, P), slice(0, 3)), d[:, :, :, 0], d[:, :, :, 1], ALU.mult
                                       ).then_inc(S["decays_done"], 1)
                    pool.wait_ge(S["decays_done"], li + 1)
                pool.wait_ge(S["pv_mm"], NH)
                for x in range(2):
                    pool.memset(Qx[x][1][:, :, :], 0.0).then_inc(S["zeroed"], 1)
                pool.memset(state[:, :, :], 0.0).then_inc(S["zeroed"], 1)
                for li, m in enumerate(LEVELS):
                    for x, f in enumerate((slice(0, 1), slice(1, 3))):
                        pool.wait_ge(S["sweep_mm"], 2 * NT * li + NT * (x + 1))
                        d = block_decay(m, slice(0, P), f).rearrange("p f (b two) -> p f b two", two=2)[:, :, :, 1:2]
                        k = K[:, f, :].rearrange("p f (b two m) -> p f b two m", two=2, m=m)[:, :, :, 0, :]
                        pool.tensor_tensor(k, k, d.to_broadcast([P, 1 + x, SEQ // (2 * m), m]), ALU.mult
                                           ).then_inc(S["k_level"], 1)

            @block.gpsimd
            def _(pool):
                for i, (nk, cols, _) in enumerate(slabs):
                    n = nk * cols
                    pool.wait_ge(S["hi_split"], i + 1)
                    pool.tensor_tensor(w_lo[i % SPLIT][:, 0:n], raw[i % RAW][:, 0:n],
                                       w_hi[i % SPLIT][:, 0:n].bitcast(f32), ALU.subtract).then_inc(S["lo_split"], 1)
                    if i == SPLIT - 1:
                        for half in range(2):
                            pool.memset(qT_r[:, 2 * half:2 * half + 2, :], 0.0).then_inc(S["zeroed"], 1)
                    if i == slab_at["feat", 0]:
                        pool.wait_ge(S["lat_sq_done"], 4)
                        for n in range(2):
                            pool.tensor_tensor(lat_sq[:, 2 * n, :], lat_sq[:, 2 * n, :], lat_sq[:, 2 * n + 1, :], ALU.add
                                               ).then_inc(S["lat_sq_sum"], 1)
                    if i == slab_at["cig", 3]:
                        pool.wait_ge(S["v_mm"], NT)
                        pool.wait_ge(S["q_scaled"], 1)
                        pool.tensor_tensor(qk[:, :, :], Q[:, :, :], K[:, :, :], ALU.mult).then_inc(S["qk_prod"], 1)
                    if i == slab_at["mix", 0, 1]:
                        recurrences(pool)

            released = {}

            @block.tensor
            def _(pe):
                freed, count = {}, {}

                def mark(ins, sem):
                    ins.then_inc(sem, 1)
                    count[id(sem)] = count.get(id(sem), 0) + 1
                    return sem, count[id(sem)]

                def claim(b):
                    if b in freed:
                        pe.wait_ge(*freed[b])

                def use(name):
                    i = slab_at[name]
                    nk, cols, _ = slabs[i]
                    pe.wait_ge(S["lo_split"], i + 1)
                    return [w[i % SPLIT][:, 0:nk * cols].rearrange("p (k c) -> p k c", k=nk) for w in (w_hi, w_lo)]

                def product(o, a, b, first, last):
                    (ah, al), (bh, bl) = a, b
                    pe.matmul(o, ah, bh, start=first, stop=False)
                    pe.matmul(o, ah, bl, start=False, stop=False)
                    return pe.matmul(o, al, bh, start=False, stop=last)

                def transpose_h(w, ks):
                    if w:
                        pe.wait_ge(S["h_added"], H_ADDS * w - (NT if ks[0] < KD // 2 else 0))
                    for k in ks:
                        b = H_BANKS[w][k]
                        claim(b)
                        for t in range(NT):
                            mm = pe.transpose(pb[b][:, t * P:(t + 1) * P], h[:, t, k * P:(k + 1) * P], ident[:, :])
                        mark(mm, S["hT_mm"])
                        freed[b] = (S["x_lo_done"], w * KD + k + 1)

                def spread_r(n):
                    claim(4)
                    pe.wait_ge(S["r_diag_done"], n + 1)
                    mark(pe.matmul(pb[4][:, :], ones[:, :], r_diag[:, :, :].rearrange("p t c -> p (t c)"),
                                   start=True, stop=True), S["r_mm"])
                    freed[4] = (S["r_bc_done"], n + 1)

                def feature_chunk(name, b, w, done, evac, cols=P):
                    claim(b)
                    wh, wl = use(name)
                    for k in range(KD):
                        pe.wait_ge(S["x_lo_done"], w * KD + k + 1)
                        mm = product(pb[b][0:cols, :], (wh[:, k, :], wl[:, k, :]), (x_hi[:, k, :], x_lo[:, k, :]),
                                     k == 0, k == KD - 1)
                    released[slab_at[name]] = mark(mm, done)
                    freed[b] = evac

                def token_group(names, b0, cols, x, k0, ready, done, evac, nt=NT, before={}):
                    xh, xl = x
                    nk_all = sum(slabs[slab_at[n]][0] for n in names)
                    k = 0
                    for i, n in enumerate(names):
                        if i in before:
                            before[i]()
                        wh, wl = use(n)
                        for kk in range(slabs[slab_at[n]][0]):
                            if ready is not None:
                                pe.wait_ge(*ready(k))
                            for t in range(nt):
                                if k == 0:
                                    claim(b0 + t)
                                mm = product(pb[b0 + t][:, 0:cols],
                                             (xh[:, k0 + k, t * P:(t + 1) * P], xl[:, k0 + k, t * P:(t + 1) * P]),
                                             (wh[:, kk, :], wl[:, kk, :]), k == 0, k == nk_all - 1)
                                if k == nk_all - 1:
                                    last = mark(mm, done)
                            k += 1
                        released[slab_at[n]] = last if k == nk_all else mark(mm, S["slab_used"])
                    for t in range(nt):
                        freed[b0 + t] = (evac[0], evac[1] + t + 1)

                def attend(base, groups, score, n_keys, q_from, values, pT, pr, steps=None):
                    n_groups = len(groups)
                    items = NH * n_groups
                    for i in steps or range(items + pv_after(base)):
                        if i < items:
                            hd, b = i // n_groups, SCORE_BANKS[i % FLIGHT]
                            claim(b)
                            c = 0
                            for t in groups[i % n_groups]:
                                n = n_keys(t)
                                mm = score(pb[b][:, c:c + n], hd, t, n)
                                c += n
                            mark(mm, S["score_mm"])
                            freed[b] = (S["score_exp"], base + i + 1)
                        j = i - FLIGHT
                        if 0 <= j < items:
                            b = TURN_BANKS[j % 2]
                            claim(b)
                            pe.wait_ge(S["probs_done"], base + j + 1)
                            for c in range(0, sum(n_keys(t) for t in groups[j % n_groups]), P):
                                mm = pe.transpose(pb[b][:, c:c + P], pr[j % FLIGHT][:, c:c + P], ident[:, :])
                            mark(mm, S["probsT_mm"])
                            freed[b] = (S["probsT_evac"], base + j + 1)
                        j = i - pv_after(base)
                        if 0 <= j < items and j % n_groups == n_groups - 1:
                            hd = j // n_groups
                            b = PV_BANKS[hd % 2]
                            claim(b)
                            pe.wait_ge(S["probsT_evac"], base + j + 1)
                            n_blocks = n_keys(NT - 1) // P
                            for n in range(n_blocks):
                                q0 = q_from(n)
                                mm = pe.matmul(pb[b][:, q0:SEQ], values(n, hd), pT[hd % len(pT)][:, n, q0:SEQ],
                                               start=(n == 0), stop=(n == n_blocks - 1))
                            mark(mm, S["pv_mm"])
                            freed[b] = (S["pv_lo"], base // MLA_ITEMS * NH + hd + 1)

                transpose_h(0, range(KD))
                feature_chunk("rope", 5, 0, S["rope_mm"], (S["rope_lr_done"], 1), ROPE_LR)
                for n in range(4):
                    feature_chunk(("lat", n), n, 0, S["lat_mm"], (S["lat_evac"], n + 1))
                    if n == 0:
                        spread_r(0)
                X = (x_hi, x_lo)
                feature_chunk(("feat", 0), 0, 0, S["feat_mm"], (S["feat_evac"], 1))
                claim(1)
                pe.wait_ge(S["lat_sq_sum"], 2)
                for n in range(2):
                    for t in range(NT):
                        mm = pe.matmul(pb[1][:, n * NT + t:n * NT + t + 1], lat_sq[:, 2 * n, t * P:(t + 1) * P],
                                       ones[:, 0:1], start=True, stop=True)
                mark(mm, S["lat_ss_mm"])
                freed[1] = (S["r_lat_done"], 1)
                claim(6)
                pe.wait_ge(S["rope_lr_done"], 1)
                for t in range(NT):
                    mm = pe.transpose(pb[6][:, t * ROPE:(t + 1) * ROPE], rope_lr[0:ROPE, t * P:(t + 1) * P], ident[0:ROPE, 0:ROPE])
                mark(mm, S["rope_t"])
                freed[6] = (S["rope_evac"], 1)
                L = (lat_hi, lat_lo)
                for n in range(2):
                    token_group([("q_up", n)], 4 * n, 2 * QK, L, 0, lambda k: (S["lat_lo_done"], k + 1),
                                S["q_mm"], (S["q_evac"], NT * n))
                token_group([("kv_up", 0)], 0, NH * P, L, 2, lambda k: (S["lat_lo_done"], k + 3), S["k_mm"], (S["k_evac"], 0))
                token_group([("kv_up", 1)], 4, NH * P, L, 2, None, S["v_mm"], (S["v_evac"], 0))
                for n in range(1, len(FEATS)):
                    feature_chunk(("feat", n), n % 4, 0, S["feat_mm"], (S["feat_evac"], n + 1))

                def transpose_qk(z, src):
                    for t in range(NT):
                        pe.wait_ge(S["qk_done"], z * NT + t + 1)
                        b = 2 * (t % 2)
                        claim(b)
                        for hd in range(NH):
                            mm = pe.transpose(pb[b][:, hd * P:(hd + 1) * P], src[:, t, PAIR * (hd // 2) + P * (hd % 2):][:, 0:P], ident[:, :])
                        mark(mm, S["qkT_mm"])
                        freed[b] = (S["qkT_evac"], 2 * (z * NT + t) + 1)
                        claim(b + 1)
                        for r in range(2):
                            mm = pe.transpose(pb[b + 1][:, r * P:(r + 1) * P], src[:, t, PAIR * r + 2 * NOPE:PAIR * (r + 1)], ident[:, :])
                        mark(mm, S["qkT_mm"])
                        freed[b + 1] = (S["qkT_evac"], 2 * (z * NT + t) + 2)

                token_group([("bv", n) for n in range(2)], 4, NH * GDV, X, 0, None, S["tok_mm"], (S["tok_evac"], 0))
                token_group([("br", n) for n in range(2)], 0, NH * GDV, X, 0, None, S["tok_mm"], (S["tok_evac"], NT))
                token_group([("cig", n) for n in range(4)], 4, 2 * NH * HDV, X, 0, None, S["tok_mm"], (S["tok_evac"], 2 * NT))
                transpose_qk(0, q_tok)
                transpose_qk(1, k_tok)
                claim(5)
                pe.wait_ge(S["spread_in"], 16 * (1 + len(spread_of)))
                mark(pe.matmul(pb[5][:, :], w_gate[ROPE:ROPE_LR, :], rope_lr[ROPE:ROPE_LR, :], start=True, stop=True), S["gate_mm"])
                freed[5] = (S["gate_min"], 1)
                claim(0)
                pe.wait_ge(S["qk_prod"], 1)
                for n in range(NT):
                    for f in range(3):
                        c, hs = (8 * n, slice(0, NH)) if f == 0 else (8 * n + NH + 2 * (f - 1), slice(NH, NH + 2))
                        mm = pe.matmul(pb[0][:, c:c + hs.stop - hs.start], qk[:, f, n * P:(n + 1) * P], head_of[:, hs],
                                       start=True, stop=True)
                mark(mm, S["diag_mm"])
                freed[0] = (S["diag_evac"], 1)
                pe.wait_ge(S["qkT_evac"], 4 * NT)
                pe.wait_ge(S["v_evac"], NT)

                pe.wait_ge(S["zeroed"], 2)

                def mla_score(o, hd, t, n):
                    pe.matmul(o, qT_n[:, hd, t * P:(t + 1) * P], kT_n[:, hd, 0:n], start=True, stop=False)
                    return pe.matmul(o, qT_r[:, hd, t * P:(t + 1) * P], kT_r[:, hd // 2, 0:n], start=False, stop=True)

                attend(0, MLA_GROUPS, mla_score, lambda t: (t + 1) * P, lambda n: n * P,
                       lambda n, hd: v_tok[:, n, hd * VD:(hd + 1) * VD], [probsT], probs)
                for li, m in enumerate(LEVELS):
                    for x in range(2):
                        pe.wait_ge(S["qx_done"], 2 * li + x + 1)
                        if li:
                            pe.wait_ge(S["k_level"], 2 * (li - 1) + x + 1)
                        for n in range(NT):
                            b = NT * x + n
                            claim(b)
                            bank = pb[b][:, 0:NH * P // 2].rearrange("p (h c m) -> p h c m", h=NH, m=m)
                            q = Qx[x][li % 2][:, :, n * P:(n + 1) * P].rearrange("p h (c two m) -> p h c two m", two=2, m=m)
                            parts = [(2 * m * c, m, slice(c, c + 1)) for c in range(P // (2 * m))] if m >= 32 else \
                                [(0, P, slice(0, P // (2 * m)))]
                            for j, nj, cs in parts:
                                for f in range(1 + x):
                                    hs = slice(0, NH) if x == 0 else slice(2 * f, 2 * f + 2)
                                    mm = pe.matmul(bank[j:j + nj, hs, cs, :], K[:, x + f, n * P + j:n * P + j + nj],
                                                   q[:, hs, cs, 1, :], start=True, stop=True)
                            mark(mm, S["sweep_mm"])
                            freed[b] = (S["swept"], 2 * NT * li + b + 1)
                pe.wait_ge(S["k_level"], 2 * len(LEVELS))
                for f in range(3):
                    claim(f)
                    for n in range(NT):
                        mm = pe.transpose(pb[f][:, n * P:(n + 1) * P], K[:, f, n * P:(n + 1) * P], ident[:, :])
                    mark(mm, S["khat_t"])
                    freed[f] = (S["khat_evac"], f + 1)
                pe.wait_ge(S["tok_evac"], 3 * NT)
                for n in range(NT - 1):
                    claim(3 + n)
                    pe.wait_ge(S["khat_evac"], 3)
                    pe.matmul(pb[3 + n][:, 0:256], k_hat[:, 0, n, :], bv_tok[:, n, 0:256], start=True, stop=True)
                    for f in range(2):
                        mm = pe.matmul(pb[3 + n][:, 256 + f * P:256 + (f + 1) * P], k_hat[:, 1 + f, n, :],
                                       ci_tok[:, n, f * P:(f + 1) * P], start=True, stop=True)
                    mark(mm, S["u_mm"])
                    freed[3 + n] = (S["state_done"], n + 1)
                for n in range(NT):
                    b = (6, 7, 4, 5)[n]
                    claim(b)
                    pe.wait_ge(S["swept"], 2 * NT * len(LEVELS))
                    pe.wait_ge(S["q_level"], 2 * len(LEVELS) + 2)
                    if n:
                        pe.wait_ge(S["state_done"], n)
                        for f in range(3):
                            c = slice(0, 256) if f == 0 else slice(P + f * P, 2 * P + f * P)
                            pe.matmul(pb[b][:, c], Q[:, f, n * P:(n + 1) * P], state[:, n - 1, c],
                                      start=(f == 0), stop=False, skip_group_check=True)
                    for hh in range(2 * NH):
                        sc, val = (scores_g, bv_tok) if hh < NH else (scores_h, ci_tok)
                        hd = hh % NH
                        mm = pe.matmul(pb[b][:, hh * 64:(hh + 1) * 64], sc[:, n, hd, :], val[:, n, hd * 64:(hd + 1) * 64],
                                       start=(n == 0 and hh == 0), stop=(hh == 2 * NH - 1), skip_group_check=True)
                    mark(mm, S["o_mm"])
                    freed[b] = (S["o_evac"], n + 1)
                def project(name, nk, ready, x, base, half, k0=0, before={}):
                    token_group([(name, half, n) for n in range((nk + 1) // 2)], PROJ_BANKS[base // H_ADDS][half], HALF, x, k0, ready,
                                S["proj_mm"], (S["h_added"], base + NT * half), before=before)

                def y_ready(k):
                    if k == NH:
                        for c in range(4):
                            claim(4 + c)
                            for n in range(NT):
                                pe.wait_ge(S["o_done"], n + 1)
                                mm = pe.transpose(pb[4 + c][:, n * P:(n + 1) * P], o_tok[:, n, c * P:(c + 1) * P], ident[:, :])
                            mark(mm, S["yT_mm"])
                            freed[4 + c] = (S["yT_lo"], c + 1)
                    return (S["pv_lo"], k + 1) if k < NH else (S["yT_lo"], k - NH + 1)

                project("mix", KD, y_ready, X, 0, 0)
                project("mix", KD, None, X, 0, 1, before={3: lambda: transpose_h(1, range(KD // 2))})
                pe.wait_ge(S["mem_in"], 16 * MT)
                for c in range(KD // 2):
                    claim(4 + c)
                    for k in range(2):
                        for m in range(MT):
                            mm = pe.transpose(pb[4 + c][:, k * NM + m * P:k * NM + (m + 1) * P],
                                              mem_tok[:, m, (2 * c + k) * P:(2 * c + k + 1) * P], ident[:, :])
                    mark(mm, S["memT_mm"])
                    freed[4 + c] = (S["m_lo_done"], 2 * c + 2)

                def memory_half(half, before={}):
                    token_group([("ckv", half, n) for n in range(KD // 2)], 4 - 4 * half, HALF, (m_hi, m_lo), 0,
                                lambda k: (S["m_lo_done"], k + 1), S["ckv_mm"], (S["ckv_evac"], MT * half), nt=MT, before=before)

                memory_half(0)
                transpose_h(1, range(KD // 2, KD))
                token_group([("caq", n) for n in range(KD // 2)], 0, NH * P, X, 0, lambda k: (S["x_lo_done"], KD + k + 1),
                            S["cq_mm"], (S["cq_evac"], 0))

                def queries_turned():
                    for t in range(NT):
                        claim(4 + t)
                        pe.wait_ge(S["cq_evac"], t + 1)
                        for hd in range(NH):
                            mm = pe.transpose(pb[4 + t][:, hd * P:(hd + 1) * P], cq_tok[:, t, hd * P:(hd + 1) * P], ident[:, :])
                        mark(mm, S["cqT_mm"])
                        freed[4 + t] = (S["cqT_evac"], t + 1)

                def keys_turned():
                    pe.wait_ge(S["ck_done"], 1)
                    for r in range(2):
                        claim(2 + r)
                        for hd in range(2):
                            for m in range(MT):
                                c = (2 * r + hd) * P
                                mm = pe.transpose(pb[2 + r][:, hd * NM + m * P:hd * NM + (m + 1) * P], ckv_tok[:, m, c:c + P], ident[:, :])
                        mark(mm, S["ckT_mm"])
                        freed[2 + r] = (S["ckT_evac"], r + 1)

                def operands_turned():
                    keys_turned()
                    queries_turned()

                def ca_score(o, hd, t, n):
                    return pe.matmul(o, cqT[:, hd, t * P:(t + 1) * P], ckT[:, hd, :], start=True, stop=True)

                def steps(*some):
                    if some[0] == 0:
                        pe.wait_ge(S["ckT_evac"], 2)
                        pe.wait_ge(S["cqT_evac"], NT)
                    attend(MLA_ITEMS, CA_GROUPS, ca_score, lambda t: NM, lambda n: 0,
                           lambda n, hd: ckv_tok[:, n, HALF + hd * P:HALF + (hd + 1) * P], cprobsT, cprobs, some)

                memory_half(1, before={1: operands_turned, 2: lambda: steps(0, 1), 3: lambda: steps(2)})
                steps(*range(3, NH * len(CA_GROUPS) + pv_after(MLA_ITEMS)))
                project("cao", NH, lambda k: (S["pv_lo"], NH + k + 1), X, H_ADDS, 0, k0=NH)
                project("cao", NH, None, X, H_ADDS, 1, k0=NH, before={1: lambda: transpose_h(2, range(KD // 2))})
                transpose_h(2, range(KD // 2, KD))
                for g in range(FG):
                    for c in range(FCG):
                        n = g * FCG + c
                        b = 4 * g + 2 * (n % 2)
                        feature_chunk(("gate", g, c), b, 2, S["ffn_mm"], (S["gate_ready"], n + 1))
                        feature_chunk(("up", g, c), b + 1, 2, S["ffn_mm"], (S["act_ready"], n + 1))
                        if n == 0:
                            spread_r(1)
                    for half in range(2):
                        project(("ffo", g), FCG, lambda k: (S["a_lo_done"], g * FCG + k + 1), (a_hi, a_lo),
                                (2 + g) * H_ADDS, half)

            @block.scalar
            def _(act_):
                link = chain(act_, S["chain_a"])
                nsplit = [0]

                def split_through(i):
                    while nsplit[0] <= min(i, NS - 1):
                        k = nsplit[0]
                        n = slabs[k][0] * slabs[k][1]
                        act_.wait_ge(raw_in[k % RAW], arrivals[k])
                        if k >= SPLIT:
                            act_.wait_ge(*released[k - SPLIT])
                        act_.activation(w_hi[k % SPLIT][:, 0:n], raw[k % RAW][:, 0:n], ACT.Copy).then_inc(S["hi_split"], 1)
                        nsplit[0] += 1

                def ahead(name):
                    split_through(slab_at[name] + SPLIT - 1)

                def inverse_rms(dst, tmp, ss, n, done):
                    link(act_.activation(tmp, ss, ACT.Ln, bias=eps_c[:, 0:1], scale=1.0 / n))
                    act_.activation(dst, tmp, ACT.Exp, scale=-0.5).then_inc(done, 1)

                LOG_EXP = "natural_log_exp_and_others"

                def norm(w, name, r_col, ks):
                    for k in ks:
                        act_.wait_ge(S["hT_mm"], w * KD + k + 1)
                        act_.activation(x_hi[:, k, :], pb[H_BANKS[w][k]][:, :], ACT.Copy, scale=gain(name, k)).then_inc(S["x_hi_done"], 1)
                    if ks[-1] == KD - 1:
                        for t in range(NT):
                            if w == 0 and t == 0:
                                split_through(1)
                            link(act_.activation(junk[:, :], h[:, t, :], ACT.Square, accum_out=small[:, r_col + t:r_col + t + 1]))
                        inverse_rms(small[:, r_col + 8:r_col + 12], small[:, r_col + 4:r_col + 8], small[:, r_col:r_col + 4], D, S["r_done"])

                def attend(base, groups, n_keys, scale, pT, pr, between):
                    n_groups = len(groups)
                    items = NH * n_groups
                    for i in range(items + pv_after(base)):
                        if i < items:
                            hd, c = i // n_groups, 0
                            act_.wait_ge(S["score_max"], base + i + 1)
                            if i >= FLIGHT:
                                act_.wait_ge(S["probsT_mm"], base + i - FLIGHT + 1)
                            for t in groups[i % n_groups]:
                                n, st = n_keys(t), ATT + base // MLA_ITEMS * NH * NT + hd * NT + t
                                ex = act_.activation(pr[i % FLIGHT][:, c:c + n], pb[SCORE_BANKS[i % FLIGHT]][:, c:c + n], ACT.Exp,
                                                     bias=small[:, st + 32:st + 33], scale=scale(hd, t),
                                                     accum_out=small[:, st + 64:st + 65])
                                c += n
                            ex.then_inc(S["score_exp"], 1)
                        j = i - FLIGHT
                        if 0 <= j < items:
                            hd, c = j // n_groups, 0
                            act_.wait_ge(S["probsT_mm"], base + j + 1)
                            if j % n_groups == 0 and hd >= len(pT):
                                act_.wait_ge(S["pv_mm"], base // MLA_ITEMS * NH + hd - len(pT) + 1)
                            for t in groups[j % n_groups]:
                                nb = n_keys(t) // P
                                ev = act_.activation(pT[hd % len(pT)][:, 0:nb, t * P:(t + 1) * P],
                                                     pb[TURN_BANKS[j % 2]][:, c:c + nb * P].rearrange("p (n q) -> p n q", n=nb), ACT.Copy)
                                c += nb * P
                            ev.then_inc(S["probsT_evac"], 1)
                        j = i - pv_after(base)
                        if 0 <= j < items and j % n_groups == n_groups - 1:
                            hd = j // n_groups
                            act_.wait_ge(S["pv_mm"], base // MLA_ITEMS * NH + hd + 1)
                            y = base // MLA_ITEMS * NH + hd
                            act_.activation(x_hi[:, y, :], pb[PV_BANKS[hd % 2]][:, :], ACT.Copy).then_inc(S["pv_hi"], 1)
                        between(i)

                def expand(li, x, hd):
                    f, r0, dk = (0, GDK * hd, GDK) if x == 0 else (1 + hd // 2, HDK * (hd % 2), HDK)
                    r = slice(r0, r0 + dk)
                    dst, src = (odd_blocks(a, LEVELS[li]) for a in (Qx[x][li % 2][r, hd:hd + 1, :], Q[r, f:f + 1, :]))
                    ex = act_.activation(dst, src, ACT.Copy)
                    if hd == NH - 1:
                        ex.then_inc(S["qx_done"], 1)

                act_.preload_act_table_set(LOG_EXP)
                act_.activation(gains[:, :], gains_all[:, bass.ds(layer, 1), :].rearrange("p l r -> p (l r)"), ACT.Copy
                                ).then_inc(S["gains_ready"], 1)
                act_.wait_ge(S["gains_ready"], 1)
                norm(0, "norm_mix", R_MIX, range(2))
                split_through(0)
                norm(0, "norm_mix", R_MIX, range(2, KD))
                for n in range(4):
                    ahead(("lat", n))
                    act_.wait_ge(S["lat_evac"], n + 1)
                    act_.activation(lat_sq[:, n, :], lat[:, n, :], ACT.Square).then_inc(S["lat_sq_done"], 1)
                    g_ = gain("mla_q_lat_norm", n) if n < 2 else gain("mla_kv_lat_norm", n - 2)
                    act_.activation(lat_hi[:, n, :], lat[:, n, :], ACT.Copy, scale=g_).then_inc(S["lat_hi_done"], 1)
                ahead(("feat", 0))
                act_.wait_ge(S["lat_ss_mm"], 1)
                inverse_rms(small[:, R_LAT + 8:R_LAT + 16], small[:, R_LAT:R_LAT + 8], pb[1][:, 0:8], QL, S["r_lat_done"])
                act_.wait_ge(S["rope_t"], 1)
                act_.activation(kr_tok[:, :, :], pb[6][:, 0:NT * ROPE].rearrange("p (t c) -> p t c", t=NT), ACT.Copy
                                ).then_inc(S["rope_evac"], 1)
                act_.wait_ge(S["r_lat_done"], 1)
                for n in range(2):
                    ahead(("q_up", n))
                    for t in range(NT):
                        act_.wait_ge(S["q_mm"], NT * n + t + 1)
                        act_.activation(q_tok[:, t, n * 2 * QK:(n + 1) * 2 * QK], pb[4 * n + t][:, 0:2 * QK], ACT.Copy,
                                        scale=small[:, R_LAT + 8 + t:R_LAT + 9 + t]).then_inc(S["q_evac"], 1)
                ahead(("kv_up", 0))
                for t in range(NT):
                    act_.wait_ge(S["k_mm"], t + 1)
                    act_.activation(nope_of(k_tok, t), pb[t][:, :].rearrange("p (r h x) -> p r h x", r=2, h=2), ACT.Copy,
                                    scale=small[:, R_LAT + 12 + t:R_LAT + 13 + t]).then_inc(S["k_evac"], 1)
                ahead(("kv_up", 1))
                for t in range(NT):
                    act_.wait_ge(S["v_mm"], t + 1)
                    act_.activation(v_tok[:, t, :], pb[4 + t][:, :], ACT.Copy,
                                    scale=small[:, R_LAT + 12 + t:R_LAT + 13 + t]).then_inc(S["v_evac"], 1)
                def r_mix(t):
                    return small[:, R_MIX + 8 + t:R_MIX + 9 + t]

                for n in range(2 * NT):
                    ahead(("feat", n + 1) if n + 1 < len(FEATS) else ("bv", n - 5) if n < 7 else ("br", 0))
                    if n == 2 * NT - 1:
                        for t in range(NT):
                            act_.wait_ge(S["tok_mm"], t + 1)
                            act_.activation(bv_tok[:, t, :], pb[4 + t][:, 0:NH * GDV], ACT.Copy, scale=r_mix(t)).then_inc(S["tok_evac"], 1)
                    c = R_QK + 4 * n
                    act_.wait_ge(S["qk_ss"], n + 1)
                    inverse_rms(small[:, c + 128:c + 132], small[:, c + 96:c + 100], small[:, c + 64:c + 68], QK, S["qk_r"])

                def qkT(z, dn, dr):
                    for t in range(NT):
                        b = 2 * (t % 2)
                        act_.wait_ge(S["qkT_mm"], 2 * (z * NT + t) + 1)
                        act_.activation(dn[:, :, t * P:(t + 1) * P], pb[b][:, :].rearrange("p (h q) -> p h q", h=NH),
                                        ACT.Copy).then_inc(S["qkT_evac"], 1)
                        act_.wait_ge(S["qkT_mm"], 2 * (z * NT + t) + 2)
                        two = pb[b + 1][:, 0:2 * P].rearrange("p (r q) -> p r q", r=2)
                        if z:
                            ev = act_.activation(dr[:, :, t * P:(t + 1) * P], two, ACT.Copy)
                        else:
                            for r in range(2):
                                half = slice(ROPE * r, ROPE * (r + 1))
                                ev = act_.activation(dr[half, r::2, t * P:(t + 1) * P], two[half], ACT.Copy)
                        ev.then_inc(S["qkT_evac"], 1)

                ahead(("cig", 0))
                act_.wait_ge(S["feat_evac"], 2)
                link(act_.activation(K[:, 1:3, :], decay[:, 1:3, :], ACT.Sigmoid, scale=-1.0))
                act_.activation(decay[:, 1:3, :], decay[:, 1:3, :], ACT.Sigmoid).then_inc(S["f_sig"], 1)
                act_.wait_ge(S["feat_evac"], 4)
                act_.activation(Q[:, 1:3, :], Q[:, 1:3, :], ACT.Silu).then_inc(S["q_silu"], 1)

                ahead(("br", 1))
                for t in range(NT):
                    act_.wait_ge(S["tok_mm"], NT + t + 1)
                    act_.activation(sg_tok[:, t, 0:256], pb[t][:, 0:256], ACT.Silu, scale=r_mix(t)).then_inc(S["tok_evac"], 1)
                ahead(("cig", 3))
                for t in range(NT):
                    act_.wait_ge(S["tok_mm"], 2 * NT + t + 1)
                    act_.activation(ci_tok[:, t, :], pb[4 + t][:, 0:256], ACT.Copy, scale=r_mix(t))
                    act_.activation(sg_tok[:, t, 256:512], pb[4 + t][:, 256:512], ACT.Silu, scale=r_mix(t)).then_inc(S["tok_evac"], 1)
                qkT(0, qT_n, qT_r)
                qkT(1, kT_n, kT_r)
                act_.wait_ge(S["gate_mm"], 1)
                act_.preload_act_table_set(LOG_EXP)
                link(act_.activation(gate_tmp[:, :], pb[5][:, :], ACT.Abs, bias=gain("gla_b_gate", 0)))
                link(act_.activation(gate_tmp[:, :], gate_tmp[:, :], ACT.Exp, scale=-1.0))
                act_.activation(gate_tmp[:, :], gate_tmp[:, :], ACT.Ln, bias=ones[:, 0:1]).then_inc(S["gate_exp"], 1)
                act_.wait_ge(S["gate_min"], 1)
                act_.activation(decay[:, 0, :], decay[:, 0, :], ACT.Exp, scale=1.0 / TAU).then_inc(S["gate_done"], 1)
                act_.wait_ge(S["diag_mm"], 1)
                act_.activation(small[:, DIAG:DIAG + 8 * NT], pb[0][:, 0:8 * NT], ACT.Copy).then_inc(S["diag_evac"], 1)

                def first_queries(i):
                    if i == 4:
                        act_.wait_ge(S["zeroed"], 4)
                        act_.wait_ge(S["q_level"], 2)
                    if 4 <= i < 4 + 2 * NH:
                        expand(0, (i - 4) // NH, (i - 4) % NH)

                attend(0, MLA_GROUPS, lambda t: (t + 1) * P, lambda hd, t: QK ** -0.5, [probsT], probs, first_queries)
                for li, m in enumerate(LEVELS):
                    for x in range(2):
                        if li + 1 < len(LEVELS):
                            act_.wait_ge(S["q_level"], 2 * (li + 1) + x + 1)
                            if li == 0:
                                act_.wait_ge(S["zeroed"], 6)
                            else:
                                act_.wait_ge(S["sweep_mm"], 2 * NT * (li - 1) + NT * (x + 1))
                            for hd in range(NH):
                                expand(li + 1, x, hd)
                for f in range(3):
                    act_.wait_ge(S["khat_t"], f + 1)
                    act_.activation(k_hat[:, f], pb[f][:, :].rearrange("p (n q) -> p n q", n=NT), ACT.Copy).then_inc(S["khat_evac"], 1)
                for n in range(NT):
                    act_.wait_ge(S["o_mm"], n + 1)
                    act_.activation(o_tok[:, n, :], pb[(6, 7, 4, 5)[n]][:, :], ACT.Copy).then_inc(S["o_evac"], 1)
                    c = R_O + 8 * n
                    act_.wait_ge(S["o_ss"], n + 1)
                    inverse_rms(small[:, c + 64:c + 72], small[:, c + 32:c + 40], small[:, c:c + 8], GDV, S["o_r"])
                ahead(("mix", 0, 1))
                for c in range(4):
                    act_.wait_ge(S["yT_mm"], c + 1)
                    act_.activation(y_hi[:, NH + c, :], pb[4 + c][:, :], ACT.Copy).then_inc(S["yT_hi"], 1)
                act_.wait_ge(S["mem_in"], 16 * MT)
                ahead(("mix", 1, 1))
                for m in range(MT):
                    link(act_.activation(junk[:, :], mem_tok[:, m, :], ACT.Square, accum_out=small[:, R_MEM + m:R_MEM + m + 1]))
                inverse_rms(small[:, R_MEM + 4:R_MEM + 6], small[:, R_MEM + 2:R_MEM + 4], small[:, R_MEM:R_MEM + 2], D, S["mem_r"])
                ahead(("mix", 1, 2))
                norm(1, "norm_ca", R_CA, range(KD // 2))
                ahead(("mix", 1, 3))
                for k in range(KD):
                    act_.wait_ge(S["memT_mm"], k // 2 + 1)
                    act_.activation(m_hi[:, k, :], pb[4 + k // 2][:, (k % 2) * NM:(k % 2 + 1) * NM], ACT.Copy,
                                    scale=gain("norm_mem", k)).then_inc(S["m_hi_done"], 1)
                act_.wait_ge(S["mem_r"], 1)
                ahead(("ckv", 0, 3))
                norm(1, "norm_ca", R_CA, range(KD // 2, KD))

                def memory_half(half):
                    for m in range(MT):
                        act_.wait_ge(S["ckv_mm"], MT * half + m + 1)
                        act_.activation(ckv_tok[:, m, half * HALF:(half + 1) * HALF], pb[4 - 4 * half + m][:, :], ACT.Copy,
                                        scale=small[:, R_MEM + 4 + m:R_MEM + 5 + m]).then_inc(S["ckv_evac"], 1)

                ahead(("caq", 0))
                memory_half(0)
                ahead(("caq", 1))
                act_.wait_ge(S["ck_ss"], 1)
                inverse_rms(small[:, R_CK + 16:R_CK + 24], small[:, R_CK + 8:R_CK + 16], small[:, R_CK:R_CK + 8], P, S["ck_r"])
                ahead(("caq", 3))
                act_.wait_ge(S["r_done"], 2)
                for t in range(NT):
                    act_.wait_ge(S["cq_mm"], t + 1)
                    act_.activation(cq_tok[:, t, :], pb[t][:, :], ACT.Copy,
                                    scale=small[:, R_CA + 8 + t:R_CA + 9 + t]).then_inc(S["cq_evac"], 1)
                ahead(("ckv", 1, 0))
                for r in range(2):
                    act_.wait_ge(S["ckT_mm"], r + 1)
                    act_.activation(ckT[:, 2 * r:2 * r + 2, :], pb[2 + r][:, :].rearrange("p (h q) -> p h q", h=2), ACT.Copy,
                                    scale=gain("ca_k_norm", 0)).then_inc(S["ckT_evac"], 1)
                ahead(("ckv", 1, 1))
                for t in range(NT):
                    act_.wait_ge(S["cqT_mm"], t + 1)
                    act_.activation(cqT[:, :, t * P:(t + 1) * P], pb[4 + t][:, :].rearrange("p (h q) -> p h q", h=NH),
                                    ACT.Copy, scale=gain("ca_q_norm", 0)).then_inc(S["cqT_evac"], 1)
                for t in range(NT):
                    c = R_CQ + 4 * t
                    act_.wait_ge(S["cq_ss"], t + 1)
                    link(act_.activation(small[:, c + 16:c + 20], small[:, c:c + 4], ACT.Ln, bias=eps_c[:, 1:2]))
                    act_.activation(small[:, c + 32:c + 36], small[:, c + 16:c + 20], ACT.Exp, scale=-0.5).then_inc(S["cq_r"], 1)
                ahead(("ckv", 1, 2))

                def values_of_memory(i):
                    if i == 1:
                        ahead(("ckv", 1, 3))
                    if i == 2:
                        memory_half(1)

                attend(MLA_ITEMS, CA_GROUPS, lambda t: NM, lambda hd, t: small[:, R_CQ + 32 + 4 * t + hd:R_CQ + 33 + 4 * t + hd],
                       cprobsT, cprobs, values_of_memory)
                ahead(("cao", 1, 0))
                norm(2, "norm_ffn", R_FFN, range(KD // 2))
                ahead(("cao", 1, 1))
                norm(2, "norm_ffn", R_FFN, range(KD // 2, KD))
                for g in range(FG):
                    for c in range(FCG):
                        n = g * FCG + c
                        ahead(("gate", g, c))
                        ahead(("up", g, c))
                        act_.wait_ge(S["silu_done"], 2 * n + 1)
                        act_.activation(conv_silu[n % 2][:, :], conv[n % 2][:, :], ACT.Silu).then_inc(S["silu_done"], 1)
                        act_.wait_ge(S["act_ready"], n + 1)
                        act_.activation(a_hi[:, c, :], act[n % 2][:, :], ACT.Copy).then_inc(S["a_hi_done"], 1)
                    ahead((("ffo", g), 1, FCG // 2))

            @block.vector
            def _(dve):
                link = chain(dve, S["chain_v"])

                def norm(w, name, ks):
                    for k in ks:
                        dve.wait_ge(S["x_hi_done"], w * KD + k + 1)
                        dve.scalar_tensor_tensor(x_lo[:, k, :], pb[H_BANKS[w][k]][:, :], gain(name, k), x_hi[:, k, :].bitcast(f32),
                                                 ALU.mult, ALU.subtract).then_inc(S["x_lo_done"], 1)

                def spread_r(w, r_col, n_spread):
                    dve.wait_ge(S["r_done"], w + 1)
                    dve.tensor_tensor(r_diag[:, :, :], ident[:, :].unsqueeze(1).to_broadcast([P, NT, P]),
                                      small[:, r_col + 8:r_col + 12].unsqueeze(2).to_broadcast([P, NT, P]),
                                      ALU.mult).then_inc(S["r_diag_done"], 1)
                    dve.wait_ge(S["r_mm"], n_spread + 1)
                    dve.tensor_copy(r_bc[:, :], pb[4][:, :]).then_inc(S["r_bc_done"], 1)
                    dve.wait_ge(S["r_bc_done"], n_spread + 1)

                def attend(base, groups, n_keys, scale, causal, pr, between):
                    n_groups = len(groups)
                    items = NH * n_groups
                    for i in range(items + pv_after(base)):
                        if i < items:
                            g_ = groups[i % n_groups]
                            bank, c = pb[SCORE_BANKS[i % FLIGHT]], 0
                            st = ATT + base // MLA_ITEMS * NH * NT + i // n_groups * NT + g_[0]
                            dve.wait_ge(S["score_mm"], base + i + 1)
                            if causal:
                                for t in g_:
                                    c += n_keys(t)
                                    last = dve.memset(bank[0:BLOCK, c - BLOCK:c], MASKED)
                                link(last)
                            c = 0
                            if causal or len(g_) == 1:
                                for k, t in enumerate(g_):
                                    last = dve.reduce_max(small[:, st + k:st + k + 1], bank[:, c:c + n_keys(t)], AX.X)
                                    c += n_keys(t)
                            else:
                                last = dve.reduce_max(small[:, st:st + len(g_)], bank[:, :].rearrange("p (t k) -> p t k", t=len(g_)), AX.X)
                            link(last)
                            if causal:
                                ng = dve.tensor_scalar(small[:, st + 32:st + 32 + len(g_)], small[:, st:st + len(g_)], -scale, None, ALU.mult)
                            else:
                                c = R_CQ + 32 + 4 * g_[0] + i // n_groups
                                ng = dve.scalar_tensor_tensor(small[:, st + 32:st + 32 + len(g_)], small[:, st:st + len(g_)], -1.0,
                                                              small[:, c:c + 4 * len(g_) - 3:4], ALU.mult, ALU.mult)
                            ng.then_inc(S["score_max"], 1)
                        j = i - 1
                        if 0 <= j < items:
                            g_, c = groups[j % n_groups], 0
                            st = ATT + base // MLA_ITEMS * NH * NT + j // n_groups * NT + g_[0]
                            dve.wait_ge(S["score_exp"], base + j + 1)
                            link(dve.reciprocal(small[:, st + 96:st + 96 + len(g_)], small[:, st + 64:st + 64 + len(g_)]))
                            for k, t in enumerate(g_):
                                n = n_keys(t)
                                last = dve.tensor_scalar(pr[j % FLIGHT][:, c:c + n], pr[j % FLIGHT][:, c:c + n],
                                                         small[:, st + 96 + k:st + 97 + k], None, ALU.mult)
                                c += n
                            last.then_inc(S["probs_done"], 1)
                        j = i - pv_after(base)
                        if 0 <= j < items and j % n_groups == n_groups - 1:
                            hd = j // n_groups
                            y = base // MLA_ITEMS * NH + hd
                            dve.wait_ge(S["pv_hi"], y + 1)
                            dve.tensor_tensor(x_lo[:, y, :], pb[PV_BANKS[hd % 2]][:, :], x_hi[:, y, :].bitcast(f32), ALU.subtract
                                              ).then_inc(S["pv_lo"], 1)
                        between(i)

                def add_to_h(base, halves=range(2)):
                    for half in halves:
                        for t in range(NT):
                            dve.wait_ge(S["proj_mm"], base + half * NT + t + 1)
                            c = slice(half * HALF, (half + 1) * HALF)
                            dve.tensor_tensor(h[:, t, c], h[:, t, c], pb[PROJ_BANKS[base // H_ADDS][half] + t][:, :], ALU.add).then_inc(S["h_added"], 1)

                link(dve.tensor_scalar(lb_floor[:, :], lb_all[:, :, bass.ds(layer, 1)].squeeze(2), 1.0, None, ALU.mult))
                link(dve.tensor_scalar(lb_rest[:, :], lb_floor[:, :], -1.0, 1.0, ALU.mult, ALU.add))
                link(dve.tensor_scalar(lb_floor[:, :], lb_floor[:, :], LB_FLOOR, None, ALU.max))
                dve.wait_ge(S["gains_ready"], 1)
                norm(0, "norm_mix", range(KD))
                spread_r(0, R_MIX, 0)

                def lat_lo_part(n):
                    g_ = gain("mla_q_lat_norm", n) if n < 2 else gain("mla_kv_lat_norm", n - 2)
                    dve.wait_ge(S["lat_hi_done"], n + 1)
                    dve.scalar_tensor_tensor(lat_lo[:, n, :], lat[:, n, :], g_, lat_hi[:, n, :].bitcast(f32),
                                             ALU.mult, ALU.subtract).then_inc(S["lat_lo_done"], 1)

                for n in range(4):
                    dve.wait_ge(S["lat_mm"], n + 1)
                    dve.tensor_tensor(lat[:, n, :], pb[n][:, :], r_bc[:, :], ALU.mult).then_inc(S["lat_evac"], 1)
                    if n == 1:
                        dve.wait_ge(S["rope_mm"], 1)
                        dve.tensor_tensor(rope_lr[:, :], pb[5][0:ROPE_LR, :], r_bc[0:ROPE_LR, :], ALU.mult
                                          ).then_inc(S["rope_lr_done"], 1)
                    if n:
                        lat_lo_part(n - 1)
                lat_lo_part(3)
                dve.wait_ge(S["spread_in"], 16 * (1 + len(spread_of)))

                def prepare(z, t):
                    tok, name = (q_tok, "mla_q_norm") if z == 0 else (k_tok, "mla_k_norm")
                    nope, rope = nope_of(tok, t), rope_of(tok, t)
                    c = R_QK + 4 * (z * NT + t)
                    if z:
                        dve.wait_ge(S["k_evac"], t + 1)
                        dve.wait_ge(S["rope_evac"], 1)
                        link(dve.tensor_copy(rope, kr_tok[:, t, :].unsqueeze(1).unsqueeze(1).to_broadcast([P, 2, 2, ROPE])))
                    else:
                        dve.wait_ge(S["q_evac"], NT + t + 1)
                    for hd in range(NH):
                        for part, x, n in ((nope, 0, NOPE), (rope, NOPE, ROPE)):
                            head = part[:, hd // 2, hd % 2, :]
                            col = c + hd + (32 if x else 0)
                            last = dve.tensor_tensor_reduce(out=junk_v[:, hd, x:x + n], in0=head, in1=head, scale=1.0, scalar=0.0,
                                                            op0=ALU.mult, op1=ALU.add, accum_out=small[:, col:col + 1])
                    link(last)
                    dve.tensor_tensor(small[:, c + 64:c + 68], small[:, c:c + 4], small[:, c + 32:c + 36], ALU.add
                                      ).then_inc(S["qk_ss"], 1)
                    dve.wait_ge(S["qk_r"], z * NT + t + 1)
                    factor = small[:, c + 128:c + 132].rearrange("p (r h) -> p r h", r=2).unsqueeze(3)
                    dve.tensor_tensor(nope, nope, factor.to_broadcast([P, 2, 2, NOPE]), ALU.mult)
                    link(dve.tensor_tensor(rope, rope, factor.to_broadcast([P, 2, 2, ROPE]), ALU.mult))
                    g_ = spread_col(name).unsqueeze(1).unsqueeze(1)
                    dve.tensor_tensor(nope, nope, g_[:, :, :, 0:NOPE].to_broadcast([P, 2, 2, NOPE]), ALU.mult)
                    link(dve.tensor_tensor(rope, rope, g_[:, :, :, NOPE:QK].to_broadcast([P, 2, 2, ROPE]), ALU.mult))
                    R2_ = ROPE // 2
                    x1, x2 = rope[:, :, :, 0:R2_], rope[:, :, :, R2_:ROPE]
                    cs, sn = (a[:, t, :].unsqueeze(1).unsqueeze(1).to_broadcast([P, 2, 2, R2_]) for a in (cos, sin))
                    rot = r_diag[:, :, :].rearrange("p a (r h x) -> p a r h x", r=2, h=2)
                    dve.tensor_tensor(rot[:, 0], x1, cs, ALU.mult)
                    dve.tensor_tensor(rot[:, 1], x2, sn, ALU.mult)
                    dve.tensor_tensor(rot[:, 2], x2, cs, ALU.mult)
                    link(dve.tensor_tensor(rot[:, 3], x1, sn, ALU.mult))
                    dve.tensor_tensor(x1, rot[:, 0], rot[:, 1], ALU.subtract)
                    dve.tensor_tensor(x2, rot[:, 2], rot[:, 3], ALU.add).then_inc(S["qk_done"], 1)
                    dve.wait_ge(S["qk_done"], z * NT + t + 1)

                dests = [decay[:, 1, :], decay[:, 2, :], Q[:, 1, :], Q[:, 2, :], Q[:, 0, :], K[:, 0, :]]

                def feature(n):
                    dve.wait_ge(S["feat_mm"], n + 1)
                    dve.scalar_tensor_tensor(dests[n], pb[n % 4][:, :], GDK ** -0.5 if n == 4 else 1.0, r_bc[:, :],
                                             ALU.mult, ALU.mult).then_inc(S["feat_evac"], 1)

                feature(0)
                for n in range(2 * NT):
                    prepare(n // NT, n % NT)
                    if n + 1 < len(FEATS):
                        feature(n + 1)
                dve.wait_ge(S["f_sig"], 1)
                for n in range(2):
                    r, fl = lb_rest[:, n:n + 1], lb_floor[:, n:n + 1]
                    dve.tensor_scalar(K[:, 1 + n, :], K[:, 1 + n, :], r, None, ALU.mult)
                    link(dve.tensor_scalar(decay[:, 1 + n, :], decay[:, 1 + n, :], r, fl, ALU.mult, ALU.add))
                    dve.tensor_scalar(decay[:, 1 + n, :], decay[:, 1 + n, :], 1.0, None, ALU.min)
                dve.wait_ge(S["feat_evac"], 6)
                dve.wait_ge(S["q_silu"], 1)
                dve.tensor_scalar(Q[:, 1:3, :], Q[:, 1:3, :], HDK ** -0.5, None, ALU.mult).then_inc(S["q_scaled"], 1)
                dve.wait_ge(S["gate_exp"], 1)
                link(dve.tensor_scalar(decay[:, 0, :], pb[5][:, :], gain("gla_b_gate", 0), 0.0, ALU.add, ALU.min))
                dve.tensor_tensor(decay[:, 0, :], decay[:, 0, :], gate_tmp[:, :], ALU.subtract).then_inc(S["gate_min"], 1)

                def next_queries(x, m):
                    f = slice(1, 3) if x else slice(0, 1)
                    if m == 0:
                        ins = dve.tensor_tensor(Q[:, f, :], Q[:, f, :], decay[:, f, :], ALU.mult)
                    else:
                        q = odd_blocks(Q[:, f, :], m)
                        d = block_decay(m, slice(0, P), f).rearrange("p f (b two) -> p f b two", two=2)[:, :, :, 0:1]
                        ins = dve.tensor_tensor(q, q, d.to_broadcast([P, 1 + x, SEQ // (2 * m), m]), ALU.mult)
                    ins.then_inc(S["q_level"], 1)

                def first_queries(i):
                    if i == 1:
                        dve.wait_ge(S["qk_prod"], 1)
                        dve.wait_ge(S["gate_done"], 1)
                        for x in range(2):
                            next_queries(x, 0)

                attend(0, MLA_GROUPS, lambda t: (t + 1) * P, QK ** -0.5, True, probs, first_queries)
                dve.wait_ge(S["scores_base"], 2 * NT)
                for li, m in enumerate(LEVELS):
                    dve.wait_ge(S["decays_done"], li + 1)
                    for x in range(2):
                        dve.wait_ge(S["qx_done"], 2 * li + x + 1)
                        next_queries(x, m)
                    mask = pair_mask[:, li, :].rearrange("p (c m) -> p c m", m=m).unsqueeze(1).to_broadcast([P, NH, P // (2 * m), m])
                    for x, sc in enumerate((scores_g, scores_h)):
                        for n in range(NT):
                            dve.wait_ge(S["sweep_mm"], 2 * NT * li + NT * x + n + 1)
                            bank = pb[x * NT + n][:, 0:NH * P // 2].rearrange("p (h c m) -> p h c m", h=NH, m=m)
                            dve.copy_predicated(odd_blocks(sc[:, n], m), mask, bank).then_inc(S["swept"], 1)
                dve.wait_ge(S["zeroed"], 7)
                for n in range(NT - 1):
                    dve.wait_ge(S["u_mm"], n + 1)
                    for hh in range(2 * NH):
                        f, r0, dk = (0, GDK * hh, GDK) if hh < NH else (1 + (hh - NH) // 2, HDK * (hh % 2), HDK)
                        r, c = slice(r0, r0 + dk), slice(64 * hh, 64 * hh + 64)
                        u = pb[3 + n][r, c]
                        if n == 0:
                            st = dve.tensor_copy(state[r, n, c], u)
                        else:
                            st = dve.scalar_tensor_tensor(state[r, n, c], state[r, n - 1, c], block_decay(P, r, f)[:, n:n + 1],
                                                          u, ALU.mult, ALU.add)
                    st.then_inc(S["state_done"], 1)
                    dve.wait_ge(S["state_done"], n + 1)
                for n in range(NT):
                    c = R_O + 8 * n
                    o = o_tok[:, n, :].rearrange("p (h x) -> p h x", x=64)
                    sq = o_sq[:, :].rearrange("p (h x) -> p h x", x=64)
                    dve.wait_ge(S["o_evac"], n + 1)
                    link(dve.tensor_tensor(sq, o, o, ALU.mult))
                    dve.reduce_sum(small[:, c:c + 8], sq, AX.X).then_inc(S["o_ss"], 1)
                    dve.wait_ge(S["o_r"], n + 1)
                    link(dve.tensor_tensor(o, o, small[:, c + 64:c + 72].unsqueeze(2).to_broadcast([P, 8, 64]), ALU.mult))
                    g0 = spread_of["gla_out_norm"][0]
                    link(dve.tensor_tensor(o_tok[:, n, :].rearrange("p (m h x) -> p m h x", m=2, x=64),
                                           o_tok[:, n, :].rearrange("p (m h x) -> p m h x", m=2, x=64),
                                           spread[:, g0:g0 + 128].rearrange("p (m x) -> p m x", m=2).unsqueeze(2)
                                           .to_broadcast([P, 2, NH, 64]), ALU.mult))
                    dve.tensor_tensor(o_tok[:, n, :], o_tok[:, n, :], sg_tok[:, n, :], ALU.mult).then_inc(S["o_done"], 1)
                for c in range(4):
                    dve.wait_ge(S["yT_hi"], c + 1)
                    dve.tensor_tensor(y_lo[:, NH + c, :], pb[4 + c][:, :], y_hi[:, NH + c, :].bitcast(f32), ALU.subtract
                                      ).then_inc(S["yT_lo"], 1)
                add_to_h(0, (0,))
                norm(1, "norm_ca", range(KD // 2))
                add_to_h(0, (1,))
                for k in range(KD):
                    dve.wait_ge(S["m_hi_done"], k // 2 * 2 + 2)
                    dve.scalar_tensor_tensor(m_lo[:, k, :], pb[4 + k // 2][:, (k % 2) * NM:(k % 2 + 1) * NM], gain("norm_mem", k),
                                             m_hi[:, k, :].bitcast(f32), ALU.mult, ALU.subtract).then_inc(S["m_lo_done"], 1)
                norm(1, "norm_ca", range(KD // 2, KD))

                keys = ckv_tok[:, :, 0:HALF].rearrange("p m (h x) -> p m h x", h=NH)
                key_r = small[:, R_CK + 16:R_CK + 24].rearrange("p (m h) -> p m h", m=MT).unsqueeze(3)
                dve.wait_ge(S["ckv_evac"], MT)
                link(dve.tensor_tensor(ckv_sq[:, :, :, :], keys, keys, ALU.mult))
                dve.tensor_reduce(small[:, R_CK:R_CK + 8].rearrange("p (m h) -> p m h", m=MT), ckv_sq[:, :, :, :], AX.X, ALU.add
                                  ).then_inc(S["ck_ss"], 1)
                dve.wait_ge(S["ck_r"], 1)
                dve.tensor_tensor(keys, keys, key_r.to_broadcast([P, MT, NH, P]), ALU.mult).then_inc(S["ck_done"], 1)
                for t in range(NT):
                    c = R_CQ + 4 * t
                    q = cq_tok[:, t, :].rearrange("p (h x) -> p h x", h=NH)
                    sq = cq_sq[:, t, :].rearrange("p (h x) -> p h x", h=NH)
                    dve.wait_ge(S["cq_evac"], t + 1)
                    link(dve.tensor_tensor(sq, q, q, ALU.mult))
                    dve.reduce_sum(small[:, c:c + 4], sq, AX.X).then_inc(S["cq_ss"], 1)
                dve.wait_ge(S["cq_r"], NT)
                attend(MLA_ITEMS, CA_GROUPS, lambda t: NM, P ** -0.5, False, cprobs, lambda i: None)
                add_to_h(H_ADDS, (0,))
                for i in range(2):
                    dve.memset(gate_in[i][:, 0:CONV - 1], 0.0)
                norm(2, "norm_ffn", range(KD // 2))
                add_to_h(H_ADDS, (1,))
                norm(2, "norm_ffn", range(KD // 2, KD))
                spread_r(2, R_FFN, 1)
                for g in range(FG):
                    for c in range(FCG):
                        n = g * FCG + c
                        gi, cv = gate_in[n % 2], conv[n % 2]

                        def w_(t):
                            return gain("ffn_conv_w", t * FC + n)

                        dve.wait_ge(S["ffn_mm"], 2 * n + 1)
                        dve.tensor_tensor(gi[:, CONV - 1:], pb[4 * g + 2 * (n % 2)][:, :], r_bc[:, :], ALU.mult).then_inc(S["gate_ready"], 1)
                        dve.wait_ge(S["gate_ready"], n + 1)
                        link(dve.tensor_scalar(cv[:, :], gi[:, 0:SEQ], w_(0), gain("ffn_conv_b", n), ALU.mult, ALU.add))
                        for t in range(1, CONV - 1):
                            link(dve.scalar_tensor_tensor(cv[:, :], gi[:, t:t + SEQ], w_(t), cv[:, :], ALU.mult, ALU.add))
                        dve.scalar_tensor_tensor(cv[:, :], gi[:, CONV - 1:], w_(CONV - 1), cv[:, :], ALU.mult, ALU.add
                                                 ).then_inc(S["silu_done"], 1)
                        dve.wait_ge(S["ffn_mm"], 2 * n + 2)
                        link(dve.tensor_tensor(up_s[n % 2][:, :], pb[4 * g + 2 * (n % 2) + 1][:, :], r_bc[:, :], ALU.mult))
                        dve.wait_ge(S["silu_done"], 2 * n + 2)
                        dve.tensor_tensor(act[n % 2][:, :], conv_silu[n % 2][:, :], up_s[n % 2][:, :], ALU.mult).then_inc(S["act_ready"], 1)
                        dve.wait_ge(S["a_hi_done"], n + 1)
                        dve.tensor_tensor(a_lo[:, c, :], act[n % 2][:, :], a_hi[:, c, :].bitcast(f32), ALU.subtract
                                          ).then_inc(S["a_lo_done"], 1)
                    add_to_h((2 + g) * H_ADDS)

        clear_semaphores()
        layers.close()

        with nc.Block() as block:
            @block.sync
            def _(sp):
                for t in range(NT):
                    sp.dma_start(out[0, t * P:(t + 1) * P, :], h[:, t, :]).then_inc(stored, 16)
                sp.wait_ge(stored, 16 * NT)


_INS = ['x', 'mem', 'positions', 'norm_mix', 'w_in', 'mla_q_lat_norm', 'w_q_up', 'mla_kv_lat_norm', 'w_kv_up',
        'mla_q_norm', 'mla_k_norm', 'gla_w_gate', 'gla_b_gate', 'gla_out_norm', 'hgrn_lb_logits', 'hgrn_out_norm',
        'w_mix_out', 'norm_ca', 'norm_mem', 'w_ca_q', 'w_ca_kv', 'ca_q_norm', 'ca_k_norm', 'w_ca_out',
        'norm_ffn', 'w_ffn_in', 'ffn_conv_w', 'ffn_conv_b', 'w_ffn_out']


def kernel(**inputs):
    import numpy as np
    import concourse.bacc as bacc
    from concourse import mybir
    from concourse.bass_utils import run_bass_kernel_spmd

    nc = bacc.Bacc("TRN2", target_bir_lowering=False, num_devices=1)
    arrays, aps = {}, {}
    for name in _INS:
        a = np.ascontiguousarray(inputs[name])
        arrays[f"in_{name}"] = a
        aps[name] = nc.dram_tensor(f"in_{name}", a.shape, mybir.dt.from_np(a.dtype), kind="ExternalInput").ap()
    out = nc.dram_tensor("out_h", inputs['x'].shape, mybir.dt.float32, kind="ExternalOutput").ap()
    build_trunk(nc, aps, out)
    r = run_bass_kernel_spmd(nc, [arrays], core_ids=[0])
    return r.results[0]["out_h"]
```
